# Optimizing a Trainium2 kernel written in Bass

```python
import jax, jax.numpy as jnp
from jax import lax
import numpy as np

D_MODEL = 1024
BATCH = 1
SEQ = 512
DEPTH = 1
DEC_BATCH = 8
DEC_SEQ = 1
PAST_LEN = 4096
PAGE_SIZE = 128

MIX = D_MODEL
RET_WIDTH = MIX // 2
RET_HEADS = 4
RET_DK = RET_WIDTH // RET_HEADS
RET_DV = RET_WIDTH // RET_HEADS
RET_CHUNK = 128
CONV_WIDTH = MIX - RET_WIDTH
CONV_K = 3
IN_COLS = 4 * RET_WIDTH + 3 * CONV_WIDTH
ROPE_BASE = 10000.0
PEER_HEADS = 8
PEER_NKEYS = 128
PEER_NEXPERTS = PEER_NKEYS * PEER_NKEYS
PEER_DKEY = 256
PEER_HALF = PEER_DKEY // 2
PEER_TOPK = 16
PEER_BLOCK = 128
N_MOD = 6
EPS = 1e-6

kernel_name = "hybrid_retention_shortconv_peer_step"

def rms_norm(x, g):
    xf = x.astype(jnp.float32)
    y = xf * lax.rsqrt(jnp.mean(xf * xf, axis=-1, keepdims=True) + EPS)
    return (y * g.astype(jnp.float32)).astype(x.dtype)

def modulate(x, shift, scale):
    return x * (1 + scale[:, None, :]) + shift[:, None, :]

def rotary(x, pos):
    half = x.shape[-1] // 2
    freqs = ROPE_BASE ** (-jnp.arange(half, dtype=jnp.float32) / half)
    ang = pos.astype(jnp.float32)[:, None] * freqs[None, :]
    cos = jnp.cos(ang)[None, :, None, :]
    sin = jnp.sin(ang)[None, :, None, :]
    x1, x2 = x[..., :half], x[..., half:]
    return jnp.concatenate([x1 * cos - x2 * sin, x1 * sin + x2 * cos], axis=-1)

def retention_log_decay():
    return jnp.log(1.0 - 2.0 ** (-5.0 - jnp.arange(RET_HEADS, dtype=jnp.float32)))

def retention_chunk(q, k, v, S0):
    L = q.shape[1]
    lg = retention_log_decay()
    idx = jnp.arange(L, dtype=jnp.float32)
    rel = idx[:, None] - idx[None, :]
    decay = jnp.where(rel[None] >= 0, jnp.exp(lg[:, None, None] * jnp.maximum(rel, 0.0)[None]), 0.0)
    scores = jnp.einsum('blhd,bmhd->bhlm', q, k) * decay[None]
    inner = jnp.einsum('bhlm,bmhe->blhe', scores, v)
    cross_decay = jnp.exp(lg[None, :] * (idx[:, None] + 1.0))
    cross = jnp.einsum('blhd,bhde->blhe', q, S0) * cross_decay[None, :, :, None]
    k_decay = jnp.exp(lg[None, :] * (L - 1.0 - idx[:, None]))
    S_new = jnp.exp(lg * L)[None, :, None, None] * S0 + jnp.einsum(
        'blhd,blhe->bhde', k * k_decay[None, :, :, None], v)
    return inner + cross, S_new

def retention_scan(q, k, v, S0):
    B, S, H, _ = q.shape
    C = RET_CHUNK if S % RET_CHUNK == 0 else S
    n = S // C

    def to_chunks(a):
        return a.reshape(B, n, C, H, a.shape[-1]).transpose(1, 0, 2, 3, 4)

    def step(Sc, blk):
        qc, kc, vc = blk
        o, Sn = retention_chunk(qc, kc, vc, Sc)
        return Sn, o

    S_fin, o = lax.scan(step, S0, (to_chunks(q), to_chunks(k), to_chunks(v)))
    o = o.transpose(1, 0, 2, 3, 4).reshape(B, S, H, v.shape[-1])
    return o, S_fin

def retention_group(q, k, v, g, S0, pos):
    B, S, _ = q.shape
    qf = rotary(q.astype(jnp.float32).reshape(B, S, RET_HEADS, RET_DK), pos)
    kf = rotary(k.astype(jnp.float32).reshape(B, S, RET_HEADS, RET_DK), pos) * (RET_DK ** -0.5)
    vf = v.astype(jnp.float32).reshape(B, S, RET_HEADS, RET_DV)
    o, S_new = retention_scan(qf, kf, vf, S0.astype(jnp.float32))
    mu = jnp.mean(o, axis=-1, keepdims=True)
    var = jnp.mean(jnp.square(o - mu), axis=-1, keepdims=True)
    o = ((o - mu) * lax.rsqrt(var + EPS)).reshape(B, S, RET_WIDTH)
    out = (jax.nn.silu(g.astype(jnp.float32)) * o).astype(q.dtype)
    return out, S_new

def short_conv_group(bg, cg, xv, conv_w, conv_b, buf):
    S = xv.shape[1]
    u = cg * xv
    ext = jnp.concatenate([buf.astype(u.dtype), u], axis=1)
    y = conv_b[None, None, :]
    for j in range(CONV_K):
        y = y + ext[:, j:j + S, :] * conv_w[j][None, None, :]
    return bg * y, ext[:, -(CONV_K - 1):, :]

def peer_ffn(h, w_q, sub_keys, u_tab, v_tab):
    B, S, D = h.shape
    t = h.reshape(B * S, D)
    T = t.shape[0]
    n_blocks = -(-T // PEER_BLOCK)
    pad = n_blocks * PEER_BLOCK - T
    t = jnp.pad(t, ((0, pad), (0, 0))).reshape(n_blocks, PEER_BLOCK, D)
    keys_f = sub_keys.astype(jnp.float32)

    def block(xb):
        P = xb.shape[0]
        q = jnp.einsum('pd,dk->pk', xb, w_q).astype(jnp.float32).reshape(P, PEER_HEADS, 2, PEER_HALF)
        s = jnp.einsum('phcd,hcnd->phcn', q, keys_f)
        s1, i1 = lax.top_k(s[:, :, 0], PEER_TOPK)
        s2, i2 = lax.top_k(s[:, :, 1], PEER_TOPK)
        cand = (s1[..., :, None] + s2[..., None, :]).reshape(P, PEER_HEADS, PEER_TOPK * PEER_TOPK)
        cidx = (i1[..., :, None] * PEER_NKEYS + i2[..., None, :]).reshape(P, PEER_HEADS, PEER_TOPK * PEER_TOPK)
        top_s, top_pos = lax.top_k(cand, PEER_TOPK)
        eidx = jnp.take_along_axis(cidx, top_pos, axis=-1).reshape(P, PEER_HEADS * PEER_TOPK)
        gate = jax.nn.softmax(top_s, axis=-1).reshape(P, PEER_HEADS * PEER_TOPK)
        u = u_tab[eidx]
        a = jax.nn.gelu(jnp.einsum('pd,ped->pe', xb, u))
        coef = gate.astype(xb.dtype) * a
        return jnp.einsum('pe,ped->pd', coef, v_tab[eidx])

    out = lax.map(block, t)
    return out.reshape(n_blocks * PEER_BLOCK, D)[:T].reshape(B, S, D)

def layer(x, c, pos, S0, buf, w_ada, b_ada, g_pre1, g_post1, g_pre2, g_post2,
          w_in, w_out, conv_w, conv_b, w_q, sub_keys, u_tab, v_tab):
    mod = jnp.einsum('bd,de->be', jax.nn.silu(c), w_ada) + b_ada[None, :]
    sh1, sc1, gt1, sh2, sc2, gt2 = jnp.split(mod, N_MOD, axis=-1)
    h = modulate(rms_norm(x, g_pre1), sh1, sc1)
    proj = jnp.einsum('bsd,dc->bsc', h, w_in)
    cuts = [RET_WIDTH, 2 * RET_WIDTH, 3 * RET_WIDTH, 4 * RET_WIDTH,
            4 * RET_WIDTH + CONV_WIDTH, 4 * RET_WIDTH + 2 * CONV_WIDTH]
    q, k, v, g, bg, cg, xv = jnp.split(proj, cuts, axis=-1)
    r_out, S_new = retention_group(q, k, v, g, S0, pos)
    c_out, buf_new = short_conv_group(bg, cg, xv, conv_w, conv_b, buf)
    m = jnp.einsum('bsc,cd->bsd', jnp.concatenate([r_out, c_out], axis=-1), w_out)
    x = x + gt1[:, None, :] * rms_norm(m, g_post1)
    h = modulate(rms_norm(x, g_pre2), sh2, sc2)
    f = peer_ffn(h, w_q, sub_keys, u_tab, v_tab)
    x = x + gt2[:, None, :] * rms_norm(f, g_post2)
    return x, S_new, buf_new

def setup_inputs(seed: int = 0) -> dict:
    key = jax.random.key(seed)
    ks = jax.random.split(key, 24)
    f32 = jnp.float32
    nrm = lambda k, shape, s: jax.random.normal(k, shape, f32) * s
    D = D_MODEL
    return {
        "x_prompt": nrm(ks[0], (BATCH, SEQ, D), 1.0),
        "x_sample": nrm(ks[1], (DEC_BATCH, DEC_SEQ, D), 1.0),
        "c_prompt": nrm(ks[2], (BATCH, D), 1.0),
        "c_sample": nrm(ks[3], (DEC_BATCH, D), 1.0),
        "state_ret": nrm(ks[4], (DEPTH, DEC_BATCH, RET_HEADS, RET_DK, RET_DV), 0.5),
        "cache_conv": nrm(ks[5], (DEPTH, DEC_BATCH, CONV_K - 1, CONV_WIDTH), 1.0),
        "w_ada": nrm(ks[6], (DEPTH, D, N_MOD * D), 0.5 * D ** -0.5),
        "b_ada": nrm(ks[7], (DEPTH, N_MOD * D), 0.01),
        "g_pre1": 1.0 + nrm(ks[8], (DEPTH, D), 0.05),
        "g_post1": 1.0 + nrm(ks[9], (DEPTH, D), 0.05),
        "g_pre2": 1.0 + nrm(ks[10], (DEPTH, D), 0.05),
        "g_post2": 1.0 + nrm(ks[11], (DEPTH, D), 0.05),
        "w_in": nrm(ks[12], (DEPTH, D, IN_COLS), D ** -0.5),
        "w_out": nrm(ks[13], (DEPTH, MIX, D), MIX ** -0.5),
        "conv_w": nrm(ks[14], (DEPTH, CONV_K, CONV_WIDTH), CONV_K ** -0.5),
        "conv_b": nrm(ks[15], (DEPTH, CONV_WIDTH), 0.01),
        "w_q": nrm(ks[16], (DEPTH, D, PEER_HEADS * PEER_DKEY), D ** -0.5),
        "sub_keys": nrm(ks[17], (DEPTH, PEER_HEADS, 2, PEER_NKEYS, PEER_HALF), PEER_HALF ** -0.5),
        "u_tab": nrm(ks[18], (DEPTH, PEER_NEXPERTS, D), D ** -0.5),
        "v_tab": nrm(ks[19], (DEPTH, PEER_NEXPERTS, D), PEER_HEADS ** -0.5),
    }

def reference(x_prompt, x_sample, c_prompt, c_sample, state_ret, cache_conv,
              w_ada, b_ada, g_pre1, g_post1, g_pre2, g_post2,
              w_in, w_out, conv_w, conv_b, w_q, sub_keys, u_tab, v_tab):
    pos_p = jnp.arange(SEQ, dtype=jnp.int32)
    pos_s = PAST_LEN + jnp.arange(DEC_SEQ, dtype=jnp.int32)
    xp, xs = x_prompt, x_sample
    rp_list, cp_list, rs_list, cs_list = [], [], [], []
    for l in range(DEPTH):
        params = (w_ada[l], b_ada[l], g_pre1[l], g_post1[l], g_pre2[l], g_post2[l],
                  w_in[l], w_out[l], conv_w[l], conv_b[l], w_q[l], sub_keys[l], u_tab[l], v_tab[l])
        S0_p = jnp.zeros((BATCH, RET_HEADS, RET_DK, RET_DV), jnp.float32)
        buf_p = jnp.zeros((BATCH, CONV_K - 1, CONV_WIDTH), xp.dtype)
        xp, Sp, bp = layer(xp, c_prompt, pos_p, S0_p, buf_p, *params)
        xs, Ss, bs = layer(xs, c_sample, pos_s, state_ret[l], cache_conv[l], *params)
        rp_list.append(Sp)
        cp_list.append(bp)
        rs_list.append(Ss)
        cs_list.append(bs)
    ret_state_prompt = jnp.stack(rp_list, axis=0)
    conv_cache_prompt = jnp.stack(cp_list, axis=0)
    ret_state_sample = jnp.stack(rs_list, axis=0)
    conv_cache_sample = jnp.stack(cs_list, axis=0)
    return (xp, xs, ret_state_prompt, conv_cache_prompt, ret_state_sample, conv_cache_sample)


_drawn_inputs = setup_inputs


def setup_inputs(seed=0):
    import zlib

    import numpy as np

    out = dict(_drawn_inputs(seed))
    spreads = {}
    factors = {'g_post2': 3.875, 'conv_b': 3.468}
    for name, (base, spread) in spreads.items():
        noise = np.random.default_rng([zlib.crc32(name.encode()), seed]).standard_normal(out[name].shape)
        drawn = base * np.exp(spread * noise) if base else spread * noise
        out[name] = __import__('jax').numpy.asarray(drawn.astype(out[name].dtype))
    for name, factor in factors.items():
        out[name] = (out[name] * factor).astype(out[name].dtype)
    return out
```

```python
from contextlib import ExitStack

import numpy as np
import concourse.bass as bass
from concourse import mybir

F32 = mybir.dt.float32
F32R = mybir.dt.float32r
U32 = mybir.dt.uint32
ALU = mybir.AluOpType
ACT = mybir.ActivationFunctionType
AX = mybir.AxisListType

P = 128
D = 1024
KD = D // P
SEQ = 512
NS = 8
T = SEQ + NS
TH = T // 2
RH = 4
CHUNKS = SEQ // P
CK = 3
PAST = 4096
EPS = 1e-6
WC = 256
WB = WC // P
NSLOT = 4
PH = 8
NK = 128
TOPK = 16
HK = PH * TOPK
TT = 104
TILES = T // TT
CH = 52
TCH = TT // CH
NCH = T // CH
OH = 4
GB = 4
NGRP = NK // GB
LOWEST = -3.0e38

ADA, WIN, WOUT, WQ = "ada", "in", "out", "q"


def weight_loads():
    order = [(ADA, n) for n in range(2 * KD // WB)]
    for group in (0, 1, 2, 3, 5, 6, 4):
        order += [(WIN, group * 2 + n) for n in range(2)]
    order += [(WOUT, n) for n in range(D // WC)]
    order += [(ADA, n) for n in range(2 * KD // WB, 6 * KD // WB)]
    order += [(WQ, n) for n in range(2 * PH * P // WC)]
    return order


def build(nc, xT, cT, w_ada, b_ada, gains, w_in, w_out, w_q, keysT, utab, vtab, s0, conv_s, conv_w,
          trig, decay, kdecay, consts, starts,
          yT, ret_p, conv_p, ret_s, conv_so, gates_dram):
    outer = ExitStack()
    with outer:
        def sb(stack, name, shape, dt=F32):
            return stack.enter_context(nc.sbuf_tensor(name, shape, dt))

        def sem(name):
            return outer.enter_context(nc.semaphore(name))

        x = sb(outer, "x", [P, KD, T])
        h = sb(outer, "h", [P, KD, T])
        mod = sb(outer, "mod", [P, 6 * KD, 1 + NS])
        cst = sb(outer, "cst", [P, 3, P])
        gain = sb(outer, "gain", [P, 4, KD])
        co = sb(outer, "co", [P, 4, KD, 1 + NS])
        tsm = sb(outer, "tsm", [P, KD, NS])
        rs = sb(outer, "rs", [P, T])
        ones, ident, iota = cst[:, 0, :], cst[:, 1, :], cst[:, 2, :]
        ps = outer.enter_context(nc.psum_tensor("ps", [P, 8, 512], F32))

        def pair(n):
            return ps[:, 2 * n:2 * n + 2, 0:TH]

        def halves(ap):
            return ap.rearrange("p (a b) -> p a b", a=2)

        def residual(dve, link, m, slot):
            link(nc.vector.tensor_tensor(m[:], m[:], rs[:].unsqueeze(1).to_broadcast([P, KD, T]), ALU.mult))
            for k in range(KD):
                nc.vector.scalar_tensor_tensor(x[:, k, 0:SEQ], m[:, k, 0:SEQ], co[:, slot, k, 0:1], x[:, k, 0:SEQ],
                                               ALU.mult, ALU.add)
            link(nc.vector.tensor_tensor(tsm[:], m[:, :, SEQ:T], co[:, slot, :, 1:1 + NS], ALU.mult))
            return nc.vector.tensor_tensor(x[:, :, SEQ:T], x[:, :, SEQ:T], tsm[:], ALU.add)

        upto_gates = ExitStack()
        qp = sb(upto_gates, "qp", [P, 2 * PH, T])
        io = dict(xT=xT, cT=cT, b_ada=b_ada, gains=gains, keysT=keysT, utab=utab, vtab=vtab, s0=s0,
                  conv_s=conv_s, conv_w=conv_w, trig=trig, decay=decay, kdecay=kdecay, consts=consts,
                  starts=starts, yT=yT, ret_p=ret_p, conv_p=conv_p, ret_s=ret_s, conv_so=conv_so,
                  gates=gates_dram)
        on_chip = (x, h, mod, cst, gain, co, tsm, rs, ps)
        mixer_stage(nc, sem, sb, pair, halves, residual, on_chip, qp, io,
                    {ADA: w_ada, WIN: w_in, WOUT: w_out, WQ: w_q})
        gate_stage(nc, sem, sb, on_chip, qp, io)
        upto_gates.close()
        expert_stage(nc, sem, sb, pair, halves, residual, on_chip, io)


def mixer_stage(nc, sem, sb, pair, halves, residual, on_chip, qp, io, w_dram):
    x, h, mod, cst, gain, co, tsm, rs, ps = on_chip
    ones, ident = cst[:, 0, :], cst[:, 1, :]
    stack = ExitStack()
    with stack:
        wr = sb(stack, "wr", [P, NSLOT, KD, WC])
        scr = sb(stack, "scr", [P, KD, T])
        qk = sb(stack, "qk", [P, 2, RH, T])
        vt = sb(stack, "vt", [P, CHUNKS, RH * P])
        vs = sb(stack, "vs", [NS, RH * P])
        mix = sb(stack, "mix", [P, KD, T])
        ext = sb(stack, "ext", [P, RH, CK - 1 + SEQ])
        exs = sb(stack, "exs", [P, RH, CK, NS])
        tg = sb(stack, "tg", [P, 4, T])
        dec = sb(stack, "dec", [P, 2, SEQ])
        kde = sb(stack, "kde", [P, RH, CHUNKS])
        pr = sb(stack, "pr", [P, CHUNKS, SEQ])
        kd = sb(stack, "kd", [P, CHUNKS, P])
        so = sb(stack, "so", [P, RH, P])
        t1 = sb(stack, "t1", [P, T])
        t2 = sb(stack, "t2", [P, T])
        cs = sb(stack, "cs", [P, KD, 1 + NS])
        bad = sb(stack, "bad", [P, 6 * KD])
        cw = sb(stack, "cw", [P, RH, CK + 1])
        sel = sb(stack, "sel", [NS, NS, P])
        state = scr[:, :, :].rearrange("p a b -> p (a b)")[:, 0:NS * RH * P]\
            .rearrange("p (b h e) -> p b h e", b=NS, h=RH)

        w_slot = [sem(f"w_slot{n}") for n in range(NSLOT)]
        in_x, in_c, in_cst, in_trig, in_state, in_misc = (
            sem(n) for n in ("in_x", "in_c", "in_cst", "in_trig", "in_state", "in_misc"))
        in_dec = [sem(f"in_dec{hd}") for hd in range(RH)]
        stored = sem("mixer_stored")
        silu_c = sem("silu_c")
        mod_mm = sem("mod_mm")
        mod_ok = sem("mod_ok")
        sq_ok = sem("sq_ok")
        ss_mm = sem("ss_mm")
        ms_ok = sem("ms_ok")
        rt_ok = sem("rt_ok")
        h_ok = sem("h_ok")
        proj_mm = sem("proj_mm")
        rot_mul = sem("rot_mul")
        rot_ok = sem("rot_ok")
        v_mm = sem("v_mm")
        v_ok = sem("v_ok")
        g_ok = sem("g_ok")
        cg_ok = sem("cg_ok")
        zero_ok = sem("zero_ok")
        u_ok = sem("u_ok")
        conv_ok = sem("conv_ok")
        sc_mm = sem("sc_mm")
        pr_ok = sem("pr_ok")
        kt_mm = sem("kt_mm")
        kd_ok = sem("kd_ok")
        st_mm = sem("st_mm")
        st_ok = sem("st_ok")
        s0_ok = sem("s0_ok")
        vb_mm = sem("vb_mm")
        sn_ok = sem("sn_ok")
        o_mm = sem("o_mm")
        o_ok = sem("o_ok")
        mu_mm = sem("mu_mm")
        oc_ok = sem("oc_ok")
        oq_ok = sem("oq_ok")
        va_mm = sem("va_mm")
        ve_ok = sem("ve_ok")
        sd_ok = sem("sd_ok")
        ret_ok = sem("ret_ok")
        m_ok = sem("m_ok")
        x1_ok = sem("x1_ok")
        qp_ok = sem("qp_ok")
        steps = sem("mixer_dve")

        Q0, K0, G0, C0, X0, B0, M0 = (RH * n for n in range(7))
        Q2 = M0 + KD
        RING = 3

        def read_of(m):
            for start, s in ((Q2, qp_ok), (M0, m_ok), (B0, conv_ok), (X0, u_ok), (C0, cg_ok), (G0, g_ok),
                             (Q0, rot_mul)):
                if m >= start:
                    return s, m - start + 1

        order = weight_loads()
        used_of, n_ada, n_v, n_blocks = [], 0, 0, 0
        for kind, at in order:
            if kind == ADA:
                n_ada += 1
                used_of.append((mod_mm, n_ada))
            elif kind == WIN and at // 2 == 2:
                n_v += 1
                used_of.append((v_mm, n_v))
            else:
                n_blocks += WB
                used_of.append((proj_mm, n_blocks))

        ADA1 = 2 * KD // WB
        ADA2 = 4 * KD // WB

        with nc.Block() as block:

            @block.sync
            def _(sp):
                sp.dma_start(cs[:], io["cT"]).then_inc(in_c, 16)

                def load(n):
                    kind, at = order[n]
                    if n >= NSLOT:
                        s, value = used_of[n - NSLOT]
                        sp.wait_ge(s, value)
                    sp.dma_start(wr[:, n % NSLOT], w_dram[kind][at]).then_inc(w_slot[n % NSLOT], 16)

                load(0)
                sp.dma_start(x[:], io["xT"]).then_inc(in_x, 16)
                sp.dma_start(cst[:], io["consts"]).then_inc(in_cst, 16)
                for n in range(1, NSLOT):
                    load(n)
                for dst, name in ((bad[:], "b_ada"), (gain[:], "gains"), (cw[:], "conv_w"),
                                  (exs[:, :, 0:CK - 1, :], "conv_s"), (kde[:], "kdecay"), (sel[:], "starts")):
                    sp.dma_start(dst, io[name]).then_inc(in_misc, 16)
                sp.dma_start(tg[:], io["trig"]).then_inc(in_trig, 16)
                for hd in range(2):
                    sp.dma_start(dec[:, hd, :], io["decay"][hd]).then_inc(in_dec[hd], 16)
                for n in range(NSLOT, len(order)):
                    load(n)
                    if n == 3 * NSLOT:
                        sp.wait_ge(ss_mm, 1)
                        sp.dma_start(state, io["s0"]).then_inc(in_state, 16)

            @block.tensor
            def _(pe):
                loaded = [0]
                made = [0]

                def weights():
                    n = loaded[0]
                    loaded[0] += 1
                    pe.wait_ge(w_slot[n % NSLOT], 16 * (n // NSLOT + 1))
                    return n % NSLOT

                def adaln(n_loads):
                    for n in range(n_loads):
                        s = weights()
                        for b in range(WB):
                            at = (n * WB + b) * (1 + NS)
                            for k in range(KD):
                                last = nc.tensor.matmul(ps[:, 7, at:at + 1 + NS], wr[:, s, k, b * P:(b + 1) * P],
                                                        cs[:, k, :], start=(k == 0), stop=(k == KD - 1))
                        last.then_inc(mod_mm, 1)

                def norm_sum(n, squares):
                    pe.wait_ge(sq_ok, n)
                    for k in range(KD):
                        for a in range(2):
                            last = nc.tensor.matmul(ps[:, a, 0:TH], ones, squares[:, k, a * TH:(a + 1) * TH],
                                                    start=(k == 0), stop=(k == KD - 1))
                    last.then_inc(ss_mm, 1)

                def blocks(n_loads, rhs):
                    for n in range(n_loads):
                        s = weights()
                        for b in range(WB):
                            m = made[0]
                            if m >= RING:
                                pe.wait_ge(*read_of(m - RING))
                            for k in range(KD):
                                for a in range(2):
                                    last = nc.tensor.matmul(ps[:, 2 * (m % RING) + a, 0:TH],
                                                            wr[:, s, k, b * P:(b + 1) * P],
                                                            rhs[:, k, a * TH:(a + 1) * TH],
                                                            start=(k == 0), stop=(k == KD - 1))
                            last.then_inc(proj_mm, 1)
                            made[0] += 1

                def all_read():
                    for m in range(max(0, made[0] - RING), made[0]):
                        pe.wait_ge(*read_of(m))

                pe.wait_ge(silu_c, 1)
                adaln(ADA1)
                pe.wait_ge(in_cst, 16)
                norm_sum(1, scr)
                pe.wait_ge(h_ok, 1)
                blocks(4, h)
                all_read()
                for half in range(2):
                    s = weights()
                    for c in range(CHUNKS + 1):
                        cols = slice(c * P, min(T, (c + 1) * P))
                        rows = cols.stop - cols.start
                        for k in range(KD):
                            last = nc.tensor.matmul(ps[0:rows, c, half * WC:(half + 1) * WC],
                                                    h[:, k, cols], wr[:, s, k, :],
                                                    start=(k == 0), stop=(k == KD - 1))
                    last.then_inc(v_mm, 1)
                pe.wait_ge(v_ok, 2)
                blocks(8, h)

                pe.wait_ge(rot_ok, 2 * RH)
                all_read()
                for hd in range(RH):
                    q, k = qk[:, 0, hd, :], qk[:, 1, hd, :]
                    for c in range(CHUNKS):
                        if hd:
                            pe.wait_ge(pr_ok, CHUNKS * (hd - 1) + c + 1)
                        nc.tensor.matmul(ps[:, c, 0:SEQ - c * P], k[:, c * P:(c + 1) * P], q[:, c * P:SEQ],
                                         start=True, stop=True).then_inc(sc_mm, 1)
                    if hd:
                        pe.wait_ge(kd_ok, CHUNKS * hd)
                    for c in range(CHUNKS):
                        last = nc.tensor.transpose(ps[:, 4, c * P:(c + 1) * P], k[:, c * P:(c + 1) * P], ident)
                    last.then_inc(kt_mm, 1)
                    if hd:
                        pe.wait_ge(o_ok, hd)
                    for c in range(CHUNKS):
                        pe.wait_ge(pr_ok, CHUNKS * hd + c + 1)
                        last = nc.tensor.matmul(ps[:, 5, c * P:SEQ], vt[:, c, hd * P:(hd + 1) * P],
                                                pr[:, c, 0:SEQ - c * P], start=(c == 0), stop=(c == CHUNKS - 1))
                    last.then_inc(o_mm, 1)
                    pe.wait_ge(kd_ok, CHUNKS * (hd + 1))
                    if hd:
                        pe.wait_ge(st_ok, hd)
                    for c in range(CHUNKS):
                        last = nc.tensor.matmul(ps[:, 6, 0:P], kd[:, c, :], vt[:, c, hd * P:(hd + 1) * P],
                                                start=(c == 0), stop=(c == CHUNKS - 1))
                    last.then_inc(st_mm, 1)
                pe.wait_ge(in_misc, 16 * 6)
                for b in range(NS):
                    if b >= 2:
                        pe.wait_ge(sn_ok, b - 1)
                    nc.tensor.matmul(ps[:, b % 2, :], sel[:, b, :], vs[:], start=True, stop=True)\
                        .then_inc(vb_mm, 1)
                pe.wait_ge(sn_ok, NS)
                for hd in range(RH):
                    for b in range(NS):
                        last = nc.tensor.matmul(ps[:, 2, hd * NS + b:hd * NS + b + 1], state[:, b, hd, :],
                                                qk[:, 0, hd, SEQ + b:SEQ + b + 1], start=True, stop=True)
                last.then_inc(o_mm, 1)
                pe.wait_ge(o_ok, RH + 1)
                for hd in range(RH):
                    o = qk[:, 1, hd, :]
                    if hd:
                        pe.wait_ge(oc_ok, hd)
                    for a in range(2):
                        last = nc.tensor.matmul(ps[:, a, 0:TH], ones, o[:, a * TH:(a + 1) * TH],
                                                start=True, stop=True)
                    last.then_inc(mu_mm, 1)
                    pe.wait_ge(oq_ok, hd + 1)
                    if hd:
                        pe.wait_ge(ve_ok, hd)
                    for a in range(2):
                        last = nc.tensor.matmul(ps[:, 2 + a, 0:TH], ones, t1[:, a * TH:(a + 1) * TH],
                                                start=True, stop=True)
                    last.then_inc(va_mm, 1)
                pe.wait_ge(ret_ok, RH)
                pe.wait_ge(conv_ok, RH)
                pe.wait_ge(st_ok, RH)
                blocks(D // WC, mix)
                pe.wait_ge(mod_ok, 1)
                adaln(ADA2)
                all_read()
                norm_sum(2, mix)
                norm_sum(3, mix)
                pe.wait_ge(h_ok, 2)
                blocks(2 * PH * P // WC, h)

            @block.scalar
            def _(act):
                act.wait_ge(in_c, 16)
                nc.scalar.activation(cs[:], cs[:], ACT.Silu).then_inc(silu_c, 1)
                act.wait_ge(in_x, 16)
                nc.scalar.activation(scr[:], x[:], ACT.Square).then_inc(sq_ok, 1)

                def root(n):
                    act.wait_ge(ms_ok, n)
                    nc.scalar.activation(rs[:], rs[:], ACT.Sqrt).then_inc(rt_ok, 1)

                root(1)
                act.wait_ge(v_mm, 2)
                nc.scalar.activation(vt[:], ps[:, 0:CHUNKS, :], ACT.Copy).then_inc(v_ok, 1)
                nc.scalar.activation(vs[:], ps[0:NS, CHUNKS, :], ACT.Copy).then_inc(v_ok, 1)
                act.wait_ge(rot_ok, 2 * RH)
                for b in range(RH):
                    act.wait_ge(proj_mm, G0 + b + 1)
                    nc.scalar.activation(halves(mix[:, b, :]), pair((G0 + b) % RING), ACT.Silu).then_inc(g_ok, 1)
                for b in range(RH):
                    act.wait_ge(proj_mm, C0 + b + 1)
                    nc.scalar.activation(halves(mix[:, RH + b, :]), pair((C0 + b) % RING), ACT.Copy)\
                        .then_inc(cg_ok, 1)
                act.wait_ge(in_misc, 16 * 6)
                for hd in range(RH):
                    act.wait_ge(kt_mm, hd + 1)
                    if hd:
                        act.wait_ge(st_mm, hd)
                    for c in range(CHUNKS):
                        nc.scalar.activation(kd[:, c, :], ps[:, 4, c * P:(c + 1) * P], ACT.Copy,
                                             scale=kde[:, hd, c:c + 1]).then_inc(kd_ok, 1)
                    act.wait_ge(o_mm, hd + 1)
                    nc.scalar.activation(qk[:, 1, hd, 0:SEQ], ps[:, 5, :], ACT.Copy).then_inc(o_ok, 1)
                    act.wait_ge(st_mm, hd + 1)
                    nc.scalar.activation(so[:, hd, :], ps[:, 6, 0:P], ACT.Copy).then_inc(st_ok, 1)
                act.wait_ge(o_mm, RH + 1)
                nc.scalar.activation(qk[:, 1, :, SEQ:T], ps[:, 2, 0:RH * NS].rearrange("p (h b) -> p h b", h=RH),
                                     ACT.Copy).then_inc(o_ok, 1)
                for hd in range(RH):
                    act.wait_ge(oc_ok, hd + 1)
                    if hd:
                        act.wait_ge(va_mm, hd)
                    nc.scalar.activation(t1[:], qk[:, 1, hd, :], ACT.Square).then_inc(oq_ok, 1)
                    act.wait_ge(ve_ok, hd + 1)
                    nc.scalar.activation(t2[:], t2[:], ACT.Sqrt).then_inc(sd_ok, 1)
                act.wait_ge(stored, 16 * 4)
                for b in range(KD):
                    act.wait_ge(proj_mm, M0 + b + 1)
                    nc.scalar.activation(halves(scr[:, b, :]), pair((M0 + b) % RING), ACT.Copy).then_inc(m_ok, 1)
                act.wait_ge(m_ok, KD)
                nc.scalar.activation(mix[:], scr[:], ACT.Square).then_inc(sq_ok, 1)
                root(2)
                act.wait_ge(x1_ok, 1)
                nc.scalar.activation(mix[:], x[:], ACT.Square).then_inc(sq_ok, 1)
                root(3)
                for b in range(2 * PH):
                    act.wait_ge(proj_mm, Q2 + b + 1)
                    nc.scalar.activation(halves(qp[:, b, :]), pair((Q2 + b) % RING), ACT.Copy).then_inc(qp_ok, 1)
                act.wait_ge(qp_ok, 2 * PH)

            @block.gpsimd
            def _(pool):
                nc.gpsimd.memset(ext[:, :, 0:CK - 1], 0.0).then_inc(zero_ok, 1)
                for n in range(2 * RH):
                    pool.wait_ge(rot_mul, n + 1)
                    nc.gpsimd.tensor_tensor(qk[:, n // RH, n % RH, :], mix[:, n % 2, :], mix[:, 2 + n % 2, :],
                                            ALU.add).then_inc(rot_ok, 1)
                pool.wait_ge(in_state, 16)
                for hd in range(RH):
                    nc.gpsimd.tensor_scalar(state[:, :, hd, :], state[:, :, hd, :], 1.0 - 2.0 ** (-5 - hd),
                                            None, ALU.mult).then_inc(s0_ok, 1)
                pool.wait_ge(u_ok, RH)
                pool.wait_ge(in_misc, 16 * 6)
                pool.dma_start(io["conv_p"], ext[:, :, SEQ:SEQ + CK - 1]).then_inc(stored, 16)
                pool.dma_start(io["conv_so"], exs[:, :, 1:CK, :]).then_inc(stored, 16)
                for hd in range(2, RH):
                    pool.wait_ge(pr_ok, CHUNKS * (hd - 1))
                    pool.dma_start(dec[:, hd % 2, :], io["decay"][hd]).then_inc(in_dec[hd], 16)
                pool.wait_ge(st_ok, RH)
                pool.dma_start(io["ret_p"], so[:]).then_inc(stored, 16)
                pool.wait_ge(sn_ok, NS)
                pool.dma_start(io["ret_s"], state).then_inc(stored, 16)
                pool.wait_ge(stored, 16 * 4)

            @block.vector
            def _(dve):
                done = [0]

                def link(ins):
                    done[0] += 1
                    ins.then_inc(steps, 1)
                    dve.wait_ge(steps, done[0])

                def coefficients(slot, part, g):
                    m = mod[:, part * KD:(part + 1) * KD, :]
                    gb = gain[:, g, :].unsqueeze(2).to_broadcast([P, KD, 1 + NS])
                    if part % 3 == 1:
                        link(nc.vector.scalar_tensor_tensor(co[:, slot], m, 1.0, gb, ALU.add, ALU.mult))
                    else:
                        link(nc.vector.tensor_tensor(co[:, slot], m, gb, ALU.mult))

                def mod_part(n_loads, lo, hi):
                    dve.wait_ge(mod_mm, n_loads)
                    sums = ps[:, 7, 0:(hi - lo) * 9].rearrange("p (b s) -> p b s", s=9)
                    nc.vector.tensor_tensor(mod[:, lo:hi, :], sums,
                                            bad[:, lo:hi].unsqueeze(2).to_broadcast([P, hi - lo, 9]), ALU.add)\
                        .then_inc(mod_ok, 1)

                def inverse_rms(n):
                    dve.wait_ge(ss_mm, n)
                    nc.vector.tensor_scalar(halves(rs[:]), pair(0), 1.0 / D, EPS, ALU.mult, ALU.add)\
                        .then_inc(ms_ok, 1)
                    dve.wait_ge(rt_ok, n)
                    link(nc.vector.reciprocal(rs[:], rs[:]))

                def modulated(slot, shift):
                    link(nc.vector.tensor_tensor(h[:], x[:], rs[:].unsqueeze(1).to_broadcast([P, KD, T]), ALU.mult))
                    for k in range(KD):
                        nc.vector.tensor_scalar(h[:, k, 0:SEQ], h[:, k, 0:SEQ], co[:, slot, k, 0:1],
                                                mod[:, shift * KD + k, 0:1], ALU.mult, ALU.add)
                    link(nc.vector.tensor_tensor(tsm[:], h[:, :, SEQ:T], co[:, slot, :, 1:1 + NS], ALU.mult))
                    nc.vector.tensor_tensor(h[:, :, SEQ:T], tsm[:], mod[:, shift * KD:(shift + 1) * KD, 1:1 + NS],
                                            ALU.add).then_inc(h_ok, 1)

                dve.wait_ge(in_misc, 16 * 6)
                mod_part(ADA1, 0, 2 * KD)
                dve.wait_ge(mod_ok, 1)
                coefficients(0, 1, 0)
                inverse_rms(1)
                modulated(0, 0)

                dve.wait_ge(in_trig, 16)
                for n in range(2 * RH):
                    pq = pair(n % RING)
                    which = 2 * (n // RH)
                    dve.wait_ge(proj_mm, n + 1)
                    if n >= 2:
                        dve.wait_ge(rot_ok, n - 1)
                    nc.vector.tensor_tensor(halves(mix[:, n % 2, :]), pq, halves(tg[:, which, :]), ALU.mult)
                    for lo in (0, P // 2):
                        hi = P // 2 - lo
                        last = nc.vector.tensor_tensor(halves(mix[lo:lo + P // 2, 2 + n % 2, :]),
                                                       pq[hi:hi + P // 2],
                                                       halves(tg[hi:hi + P // 2, which + 1, :]), ALU.mult)
                    last.then_inc(rot_mul, 1)
                dve.wait_ge(zero_ok, 1)
                for b in range(RH):
                    n = X0 + b
                    dve.wait_ge(proj_mm, n + 1)
                    dve.wait_ge(cg_ok, b + 1)
                    c, xv = mix[:, RH + b, :], pair(n % RING)
                    nc.vector.tensor_tensor(ext[:, b, CK - 1:CK - 1 + TH], xv[:, 0, :], c[:, 0:TH], ALU.mult)
                    nc.vector.tensor_tensor(ext[:, b, CK - 1 + TH:CK - 1 + SEQ], xv[:, 1, 0:SEQ - TH],
                                            c[:, TH:SEQ], ALU.mult)
                    nc.vector.tensor_tensor(exs[:, b, CK - 1, :], xv[:, 1, SEQ - TH:TH],
                                            c[:, SEQ:T], ALU.mult).then_inc(u_ok, 1)
                dve.wait_ge(u_ok, RH)
                for j in range(CK):
                    for b in range(RH):
                        y = mix[:, RH + b, :]
                        for tap, out in ((ext[:, b, j:j + SEQ], y[:, 0:SEQ]), (exs[:, b, j, :], y[:, SEQ:T])):
                            if j == 0:
                                last = nc.vector.tensor_scalar(out, tap, cw[:, b, 0:1], cw[:, b, CK:CK + 1],
                                                               ALU.mult, ALU.add)
                            else:
                                last = nc.vector.scalar_tensor_tensor(out, tap, cw[:, b, j:j + 1], out,
                                                                      ALU.mult, ALU.add)
                    link(last)
                for b in range(RH):
                    y = halves(mix[:, RH + b, :])
                    dve.wait_ge(proj_mm, B0 + b + 1)
                    nc.vector.tensor_tensor(y, pair((B0 + b) % RING), y, ALU.mult).then_inc(conv_ok, 1)
                for hd in range(RH):
                    dve.wait_ge(in_dec[hd], 16)
                    if hd:
                        dve.wait_ge(o_mm, hd)
                    for c in range(CHUNKS):
                        dve.wait_ge(sc_mm, CHUNKS * hd + c + 1)
                        nc.vector.tensor_tensor(pr[:, c, 0:SEQ - c * P], ps[:, c, 0:SEQ - c * P],
                                                dec[:, hd % 2, 0:SEQ - c * P], ALU.mult).then_inc(pr_ok, 1)
                dve.wait_ge(s0_ok, RH)
                for b in range(NS):
                    dve.wait_ge(vb_mm, b + 1)
                    for hd in range(RH):
                        last = nc.vector.scalar_tensor_tensor(
                            state[:, b, hd, :], ps[:, b % 2, hd * P:(hd + 1) * P],
                            qk[:, 1, hd, SEQ + b:SEQ + b + 1], state[:, b, hd, :], ALU.mult, ALU.add)
                    last.then_inc(sn_ok, 1)
                for hd in range(RH):
                    o = qk[:, 1, hd, :]
                    dve.wait_ge(mu_mm, hd + 1)
                    nc.vector.scalar_tensor_tensor(halves(o), pair(0), -1.0 / P, halves(o), ALU.mult, ALU.add)\
                        .then_inc(oc_ok, 1)
                    dve.wait_ge(va_mm, hd + 1)
                    nc.vector.tensor_scalar(halves(t2[:]), pair(1), 1.0 / P, EPS, ALU.mult, ALU.add)\
                        .then_inc(ve_ok, 1)
                    dve.wait_ge(sd_ok, hd + 1)
                    link(nc.vector.reciprocal(t2[:], t2[:]))
                    link(nc.vector.tensor_tensor(t2[:], t2[:], o, ALU.mult))
                    nc.vector.tensor_tensor(mix[:, hd, :], t2[:], mix[:, hd, :], ALU.mult).then_inc(ret_ok, 1)
                mod_part(ADA1 + ADA2, 2 * KD, 6 * KD)
                dve.wait_ge(mod_ok, 2)
                for slot, part in ((1, 2), (2, 4), (3, 5)):
                    coefficients(slot, part, slot)
                inverse_rms(2)
                residual(dve, link, scr, 1).then_inc(x1_ok, 1)
                inverse_rms(3)
                modulated(2, 3)
                dve.wait_ge(h_ok, 2)


def gate_stage(nc, sem, sb, on_chip, qp, io):
    x, h, mod, cst, gain, co, tsm, rs, ps = on_chip
    ident, iota = cst[:, 1, :], cst[:, 2, :]
    NB = CH // OH
    stack = ExitStack()
    with stack:
        keys = sb(stack, "keys", [P, 2 * PH, NK])
        qt = sb(stack, "qt", [P, 2 * PH, TT])
        s = sb(stack, "s", [TT, 2 * PH, NK])
        s2 = sb(stack, "s2", [TT, 2 * PH, NK])
        cand = sb(stack, "cand", [TT, PH, TOPK * TOPK])
        cand2 = sb(stack, "cand2", [TT, PH, TOPK * TOPK])
        top = sb(stack, "top", [TT, 2 * PH, TOPK])
        topi = sb(stack, "topi", [TT, 2 * PH, TOPK], U32)
        topf = sb(stack, "topf", [TT, 2 * PH, TOPK])
        best = sb(stack, "best", [TT, PH, TOPK])
        pos = sb(stack, "pos", [TT, PH, TOPK], U32)
        nib = sb(stack, "nib", [TT, 2, PH, TOPK], U32)
        nibf = sb(stack, "nibf", [TT, 2, HK])
        ex = sb(stack, "ex", [TT, PH, TOPK])
        den = sb(stack, "den", [TT, PH])
        pick = sb(stack, "pick", [TT, 3, HK])
        pt = sb(stack, "pt", [P, 3, TT])
        eq1 = sb(stack, "eq1", [P, 2, OH, P])
        ga = sb(stack, "ga", [P, 2, OH, P])
        eq2 = sb(stack, "eq2", [P, 2, OH, P])
        stage = sb(stack, "stage", [P, TCH, NK, CH])

        in_keys = sem("in_keys")
        qt_ok = sem("qt_ok")
        s_mm = sem("s_mm")
        s_ok = sem("s_ok")
        steps = sem("gate_dve")
        best_ok = sem("best_ok")
        ex_ok = sem("ex_ok")
        pick_ok = sem("pick_ok")
        pt_mm = sem("pt_mm")
        pt_ok = sem("pt_ok")
        eq_ok = sem("eq_ok")
        ga_ok = sem("ga_ok")
        g_mm = sem("gate_mm")
        g_ok = sem("gate_ok")
        kept = [sem(f"kept{c}") for c in range(TCH)]
        settled = sem("settled")
        BT = TCH * NB
        CREDIT = 2
        STEPS = 15


        with nc.Block() as block:

            @block.sync
            def _(sp):
                for c in range(TCH):
                    sp.sem_inc(kept[c], 16)
                sp.dma_start(keys[:], io["keysT"]).then_inc(in_keys, 16)
                out = io["gates"].rearrange("g p (i c) a t -> i c p g (a t)", c=TCH)
                with sp.Fori(0, TILES) as i:
                    for c in range(TCH):
                        sp.wait_ge(g_ok, i * BT + (c + 1) * NB + CREDIT)
                        sp.dma_start(out[bass.ds(i, 1), c].rearrange("i p g a -> (i p) g a"),
                                     stage[:, c].rearrange("p (g a) t -> p g (a t)", a=GB)).then_inc(kept[c], 16)
                for c in range(TCH):
                    sp.wait_ge(kept[c], 16 * TILES + 16)

            @block.tensor
            def _(pe):
                def scores(i):
                    for m in range(4):
                        pe.wait_ge(qt_ok, i * 4 + (m + 1))
                        if not (isinstance(i, int) and i == 0):
                            pe.wait_ge(s_ok, i * 4 + (m - 3))
                        for j in range(4 * m, 4 * m + 4):
                            last = nc.tensor.matmul(ps[0:TT, m, (j % 4) * NK:(j % 4 + 1) * NK], qt[:, j, :],
                                                    keys[:, j, :], start=True, stop=True)
                        last.then_inc(s_mm, 1)

                def gate_matrix(i):
                    for b in range(BT):
                        pe.wait_ge(ga_ok, i * BT + (b + 1 - BT))
                        pe.wait_ge(g_ok, i * BT + (b + 1 - BT))
                        for t in range(OH):
                            last = nc.tensor.matmul(ps[:, 5 + b % 2, t * P:(t + 1) * P], ga[:, b % 2, t, :],
                                                    eq2[:, b % 2, t, :], start=True, stop=True)
                        last.then_inc(g_mm, 1)

                def turn(i):
                    pe.wait_ge(pick_ok, i + 1)
                    if not (isinstance(i, int) and i == 0):
                        pe.wait_ge(pt_ok, i)
                    for j in range(3):
                        last = nc.tensor.transpose(ps[:, 4, j * TT:(j + 1) * TT], pick[:, j, :],
                                                   ident[0:TT, 0:TT])
                    last.then_inc(pt_mm, 1)

                pe.sem_inc(g_mm, CREDIT)
                pe.wait_ge(in_keys, 16)
                scores(0)
                turn(0)
                with pe.Fori(1, TILES) as i:
                    scores(i)
                    gate_matrix(i)
                    turn(i)
                gate_matrix(TILES)

            @block.scalar
            def _(act):
                tiles_of_qp = qp[:].rearrange("p j (i t) -> p i j t", t=TT)

                def inputs(i):
                    for m in range(4):
                        if isinstance(i, int):
                            src = tiles_of_qp[:, i]
                        else:
                            act.wait_ge(s_mm, i * 4 + (m - 3))
                            src = tiles_of_qp[:, bass.ds(i, 1)].rearrange("p i j t -> p (i j) t")
                        nc.scalar.activation(qt[:, 4 * m:4 * m + 4, :], src[:, 4 * m:4 * m + 4, :], ACT.Copy)\
                            .then_inc(qt_ok, 1)
                    for m in range(4):
                        act.wait_ge(s_mm, i * 4 + (m + 1))
                        nc.scalar.activation(s[:, 4 * m:4 * m + 4, :].rearrange("p j n -> p (j n)"), ps[0:TT, m, :],
                                             ACT.Copy).then_inc(s_ok, 1)

                def copied(i, b):
                    c, at = b // NB, (b % NB) * OH
                    act.wait_ge(g_mm, i * BT + (b + 1 - BT + CREDIT))
                    if b % NB == 0:
                        act.wait_ge(kept[c], i * 16)
                    nc.scalar.activation(stage[:, c, :, at:at + OH].rearrange("p n t -> p t n"),
                                         ps[:, 5 + b % 2, :].rearrange("p (t n) -> p t n", t=OH), ACT.Copy)\
                        .then_inc(g_ok, 1)

                def gated(i):
                    for b in range(BT):
                        act.wait_ge(eq_ok, i * BT + (b + 1 - BT))
                        for t in range(OH):
                            last = nc.scalar.activation(ga[:, b % 2, t, :], eq1[:, b % 2, t, :], ACT.Copy,
                                                        scale=pt[:, 2, b * OH + t:b * OH + t + 1])
                        last.then_inc(ga_ok, 1)
                        if b:
                            copied(i, b - 1)
                    copied(i, BT - 1)

                def softmax(i):
                    act.wait_ge(best_ok, i + 1)
                    nc.scalar.activation(ex[:], ex[:], ACT.Exp).then_inc(ex_ok, 1)
                    act.wait_ge(pt_mm, i + 1)
                    nc.scalar.activation(pt[:], ps[:, 4, 0:3 * TT].rearrange("p (j t) -> p j t", j=3), ACT.Copy)\
                        .then_inc(pt_ok, 1)

                act.sem_inc(g_ok, CREDIT)
                inputs(0)
                softmax(0)
                with act.Fori(1, TILES) as i:
                    inputs(i)
                    gated(i)
                    softmax(i)
                gated(TILES)
                act.wait_ge(g_ok, TILES * BT + CREDIT)

            @block.vector
            def _(dve):
                rows = lambda a: a.rearrange("p h k -> p (h k)")

                def choose(i, matrix):
                    done = [0]
                    calls = [0]
                    batch = [0]

                    def step(ins):
                        done[0] += 1
                        ins.then_inc(steps, 1)

                    def settle():
                        dve.wait_ge(steps, i * STEPS + done[0])
                        dve.sem_inc(settled, 1)

                    def one_hot():
                        b = batch[0]
                        batch[0] += 1
                        if b == 0:
                            dve.wait_ge(pt_ok, i)
                        dve.wait_ge(g_mm, i * BT + (b + 1 - BT))
                        for j, eq in ((0, eq1), (1, eq2)):
                            last = nc.vector.tensor_tensor(
                                eq[:, b % 2], iota.unsqueeze(1).to_broadcast([P, OH, P]),
                                pt[:, j, b * OH:(b + 1) * OH].unsqueeze(2).to_broadcast([P, OH, P]), ALU.is_equal)
                        last.then_inc(eq_ok, 1)

                    def between():
                        calls[0] += 1
                        if matrix and calls[0] % 4 == 0 and batch[0] < BT:
                            one_hot()

                    sets = range(2 * PH)
                    for j in sets:
                        if j % 4 == 0:
                            dve.wait_ge(s_ok, i * 4 + (j // 4 + 1))
                            dve.sem_inc(settled, 1)
                        last = nc.vector.max(top[:, j, 0:8], s[:, j, :])
                        if j == 2 * PH - 1:
                            step(last)
                        between()
                    settle()
                    for j in sets:
                        last = nc.vector.match_replace(s2[:, j, :], top[:, j, 0:8], s[:, j, :], LOWEST)
                        if j == 2 * PH - 1:
                            step(last)
                        between()
                    for j in sets:
                        nc.vector.max_index(topi[:, j, 0:8], top[:, j, 0:8], s[:, j, :])
                        between()
                    settle()
                    for j in sets:
                        last = nc.vector.max(top[:, j, 8:16], s2[:, j, :])
                        if j == 2 * PH - 1:
                            step(last)
                        between()
                    settle()
                    for j in sets:
                        last = nc.vector.max_index(topi[:, j, 8:16], top[:, j, 8:16], s2[:, j, :])
                        between()
                    step(last)
                    both = top[:].rearrange("p (h c) k -> p c h k", c=2)
                    shape = [TT, PH, TOPK, TOPK]
                    step(nc.vector.tensor_tensor(cand[:].rearrange("p h (a b) -> p h a b", a=TOPK),
                                                 both[:, 0].unsqueeze(3).to_broadcast(shape),
                                                 both[:, 1].unsqueeze(2).to_broadcast(shape), ALU.add))
                    settle()
                    for j in range(PH):
                        last = nc.vector.max(best[:, j, 0:8], cand[:, j, :])
                        between()
                    step(last)
                    nc.vector.tensor_copy(topf[:], topi[:])
                    settle()
                    for j in range(PH):
                        last = nc.vector.match_replace(cand2[:, j, :], best[:, j, 0:8], cand[:, j, :], LOWEST)
                        between()
                    step(last)
                    for j in range(PH):
                        nc.vector.max_index(pos[:, j, 0:8], best[:, j, 0:8], cand[:, j, :])
                        between()
                    settle()
                    for j in range(PH):
                        last = nc.vector.max(best[:, j, 8:16], cand2[:, j, :])
                        between()
                    step(last)
                    settle()
                    for j in range(PH):
                        last = nc.vector.max_index(pos[:, j, 8:16], best[:, j, 8:16], cand2[:, j, :])
                        between()
                    step(last)
                    while matrix and batch[0] < BT:
                        one_hot()
                    nc.vector.tensor_tensor(ex[:], best[:], best[:, :, 0:1].to_broadcast([TT, PH, TOPK]),
                                            ALU.subtract).then_inc(best_ok, 1)
                    settle()
                    nc.vector.tensor_scalar(nib[:, 0], pos[:], 4, None, ALU.logical_shift_right)
                    step(nc.vector.tensor_scalar(nib[:, 1], pos[:], 15, None, ALU.bitwise_and))
                    settle()
                    step(nc.vector.tensor_copy(nibf[:], nib[:].rearrange("p c h k -> p c (h k)")))
                    settle()
                    work = (s2[:].rearrange("p j n -> p (j n)").rearrange("p (k a) -> p k a", a=TOPK),
                            cand2[:].rearrange("p h n -> p (h n)").rearrange("p (k a) -> p k a", a=TOPK))
                    keys_at = topf[:].rearrange("p (h c) a -> p c h a", c=2)
                    for c in range(2):
                        last = nc.vector.tensor_tensor(work[c], nibf[:, c, :].unsqueeze(2).to_broadcast([TT, HK, TOPK]),
                                                       iota[0:TT, 0:TOPK].unsqueeze(1).to_broadcast([TT, HK, TOPK]),
                                                       ALU.is_equal)
                    step(last)
                    settle()
                    for c in range(2):
                        w = work[c].rearrange("p (h k) a -> p h k a", h=PH)
                        last = nc.vector.tensor_tensor(w, w, keys_at[:, c].unsqueeze(2).to_broadcast(shape), ALU.mult)
                    step(last)
                    settle()
                    for c in range(2):
                        nc.vector.tensor_reduce(pick[:, c, :], work[c], AX.X, ALU.add)
                    dve.wait_ge(ex_ok, i + 1)
                    step(nc.vector.tensor_reduce(den[:], ex[:], AX.X, ALU.add))
                    settle()
                    step(nc.vector.reciprocal(den[:], den[:]))
                    settle()
                    nc.vector.tensor_tensor(pick[:, 2, :].rearrange("p (h k) -> p h k", h=PH), ex[:],
                                            den[:].unsqueeze(2).to_broadcast([TT, PH, TOPK]), ALU.mult)\
                        .then_inc(pick_ok, 1)
                    assert done[0] == STEPS, done[0]

                def one_hots_of_last():
                    for b in range(BT):
                        if b == 0:
                            dve.wait_ge(pt_ok, TILES)
                        dve.wait_ge(g_mm, TILES * BT + (b + 1 - BT))
                        for j, eq in ((0, eq1), (1, eq2)):
                            last = nc.vector.tensor_tensor(
                                eq[:, b % 2], iota.unsqueeze(1).to_broadcast([P, OH, P]),
                                pt[:, j, b * OH:(b + 1) * OH].unsqueeze(2).to_broadcast([P, OH, P]), ALU.is_equal)
                        last.then_inc(eq_ok, 1)

                choose(0, False)
                with dve.Fori(1, TILES) as i:
                    choose(i, True)
                one_hots_of_last()


def expert_stage(nc, sem, sb, pair, halves, residual, on_chip, io):
    x, h, mod, cst, gain, co, tsm, rs, ps = on_chip
    ones = cst[:, 0, :]
    NU, NV = 4, 2
    stack = ExitStack()
    with stack:
        hh = sb(stack, "hh", [P, KD, T], F32R)
        hl = sb(stack, "hl", [P, KD, T], F32R)
        us = sb(stack, "us", [P, NU, KD, P])
        uh = sb(stack, "uh", [P, 2, KD, P], F32R)
        ul = sb(stack, "ul", [P, 2, KD, P], F32R)
        vs = sb(stack, "vblk", [P, NV, D])
        vh = sb(stack, "vh", [P, GB, D], F32R)
        vl = sb(stack, "vl", [P, GB, D], F32R)
        gt = sb(stack, "gt", [P, 2, NCH, GB, CH])
        a = sb(stack, "a", [P, 2, T])
        cf = sb(stack, "cf", [P, 2, T])
        ch = sb(stack, "ch", [P, 2, GB, T], F32R)
        cl = sb(stack, "cl", [P, 2, GB, T], F32R)
        acc = h
        squares = gt[:].rearrange("p a c g t -> p (a c g t)").rearrange("p (k t) -> p k t", k=KD)

        hh_ok = sem("hh_ok")
        hl_ok = sem("hl_ok")
        u_in = [sem(f"u_in{n}") for n in range(NU)]
        v_in = [sem(f"v_in{n}") for n in range(NV)]
        g_in = [sem(f"g_in{n}") for n in range(2)]
        uh_ok = sem("uh_ok")
        ul_ok = sem("ul_ok")
        u_mm = sem("u_mm")
        a_ok = sem("a_ok")
        c_ok = sem("c_ok")
        ch_ok = sem("ch_ok")
        cl_ok = sem("cl_ok")
        vh_ok = sem("vh_ok")
        vl_ok = sem("vl_ok")
        f_mm = sem("f_mm")
        f_ok = sem("f_ok")
        acc_ok = sem("acc_ok")
        fsq_ok, fss_mm, fms_ok, frt_ok = (sem(n) for n in ("fsq_ok", "fss_mm", "fms_ok", "frt_ok"))
        y_ok = sem("y_ok")
        y_out = sem("y_out")
        steps = sem("expert_dve")

        def positive(value):
            return not isinstance(value, int) or value > 0

        def groups(eng, step):
            step(0, 0, True, False)
            with eng.Fori(0, NGRP // 2 - 1) as i:
                step(i * 2 + 1, 1, True, True)
                step(i * 2 + 2, 0, True, True)
            step(NGRP - 1, 1, True, True)
            step(NGRP, 0, False, True)

        with nc.Block() as block:

            @block.sync
            def _(sp):
                u_pairs = io["utab"].rearrange("(i j) p k e -> i j p k e", j=2 * GB)
                v_pairs = io["vtab"].rearrange("p (i j) d -> i j p d", j=2 * GB)
                g_pairs = io["gates"].rearrange("(i j) p c a t -> i j p c a t", j=2)

                def load_u(i, j, wait):
                    if wait is not None:
                        sp.wait_ge(ul_ok, wait)
                    sp.dma_start(us[:, j % NU], u_pairs[bass.ds(i, 1), j].rearrange("i p k e -> (i p) k e"))\
                        .then_inc(u_in[j % NU], 16)

                def load_v(i, j, wait):
                    if wait is not None:
                        sp.wait_ge(vl_ok, wait)
                    sp.dma_start(vs[:, j % NV], v_pairs[bass.ds(i, 1), j].rearrange("i p d -> (i p) d"))\
                        .then_inc(v_in[j % NV], 16)

                def load_g(i, j, wait):
                    if wait is not None:
                        sp.wait_ge(c_ok, wait)
                    sp.dma_start(gt[:, j], g_pairs[bass.ds(i, 1), j].rearrange("i p c a t -> (i p) c a t"))\
                        .then_inc(g_in[j], 16)

                for j in range(GB):
                    load_u(0, j, None)
                for j in range(2):
                    load_g(0, j, None)
                for j in range(NV):
                    load_v(0, j, None)
                for j in range(GB):
                    load_u(0, GB + j, j + 1)
                with sp.Fori(0, NGRP // 2 - 1) as i:
                    for j in range(GB):
                        load_u(i + 1, j, i * (2 * GB) + (GB + j + 1))
                        if j == 0:
                            load_g(i + 1, 0, i * (2 * GB) + GB)
                        load_v(i, j + 2, i * (2 * GB) + (j + 1))
                    for j in range(GB):
                        load_u(i + 1, GB + j, i * (2 * GB) + (2 * GB + j + 1))
                        if j == 0:
                            load_g(i + 1, 1, i * (2 * GB) + 2 * GB)
                        at = GB + j + 2
                        if at < 2 * GB:
                            load_v(i, at, i * (2 * GB) + (GB + j + 1))
                        else:
                            load_v(i + 1, at - 2 * GB, i * (2 * GB) + (GB + j + 1))
                last = NGRP // 2 - 1
                for j in range(2 * GB - NV):
                    load_v(last, j + NV, last * 2 * GB + j + 1)
                sp.wait_ge(y_ok, 1)
                sp.dma_start(io["yT"], x[:]).then_inc(y_out, 16)
                sp.wait_ge(y_out, 16)

            @block.tensor
            def _(pe):
                def product(out, terms, first, final):
                    for n, (wp, xp) in enumerate(terms):
                        for half in range(2):
                            last = nc.tensor.matmul(out[:, half, :], wp, xp[:, half * TH:(half + 1) * TH],
                                                    start=(first and n == 0), stop=(final and n == 2))
                    return last

                def step(g, parity, make, add):
                    if make:
                        for j in range(GB):
                            n = g * GB + j
                            pe.wait_ge(ul_ok, n + 1)
                            if positive(n - 1):
                                pe.wait_ge(a_ok, n - 1)
                            for k in range(KD):
                                last = product(pair(j % 2),
                                               ((uh[:, j % 2, k, :], hl[:, k, :]), (uh[:, j % 2, k, :], hh[:, k, :]),
                                                (ul[:, j % 2, k, :], hh[:, k, :])), k == 0, k == KD - 1)
                            last.then_inc(u_mm, 1)
                    if add:
                        pe.wait_ge(cl_ok, g * GB)
                        pe.wait_ge(vl_ok, g * GB)
                        for k in range(KD):
                            pe.wait_ge(f_ok, g * KD + (k + 1 - KD))
                            for j in range(GB):
                                hi, lo = vh[:, j, k * P:(k + 1) * P], vl[:, j, k * P:(k + 1) * P]
                                c_hi, c_lo = ch[:, 1 - parity, j, :], cl[:, 1 - parity, j, :]
                                last = product(pair(2 + k % 2), ((hi, c_lo), (hi, c_hi), (lo, c_hi)),
                                               j == 0, j == GB - 1)
                            last.then_inc(f_mm, 1)

                pe.sem_inc(f_mm, KD)
                pe.wait_ge(hl_ok, 1)
                groups(pe, step)
                pe.wait_ge(fsq_ok, 1)
                for k in range(KD):
                    for half in range(2):
                        last = nc.tensor.matmul(ps[:, half, 0:TH], ones, squares[:, k, half * TH:(half + 1) * TH],
                                                start=(k == 0), stop=(k == KD - 1))
                last.then_inc(fss_mm, 1)

            @block.scalar
            def _(act):
                def high_u(slot, buf, loads, free):
                    act.wait_ge(u_in[slot], loads)
                    if free is not None:
                        act.wait_ge(u_mm, free)
                    nc.scalar.activation(uh[:, buf], us[:, slot], ACT.Copy).then_inc(uh_ok, 1)

                def step(g, parity, make, add):
                    for j in range(GB):
                        n = g * GB + j
                        if make:
                            if not (isinstance(g, int) and g == NGRP - 1 and j == GB - 1):
                                nxt = (j + 1) % GB
                                group = g if j < GB - 1 else g + 1
                                high_u(nxt, (j + 1) % 2, group * 16 + 16, n if positive(n) else None)
                            act.wait_ge(u_mm, n + 1)
                            if positive(n - 1):
                                act.wait_ge(c_ok, n - 1)
                            nc.scalar.activation(halves(a[:, j % 2]), pair(j % 2), ACT.Gelu_apprx_tanh).then_inc(a_ok, 1)
                        if add:
                            act.wait_ge(f_mm, g * KD)
                            act.wait_ge(v_in[j % NV], g * (16 * GB // NV) + 16 * (j // NV + 1 - GB // NV))
                            nc.scalar.activation(vh[:, j], vs[:, j % NV], ACT.Copy).then_inc(vh_ok, 1)
                        if make:
                            act.wait_ge(c_ok, n + 1)
                            nc.scalar.activation(ch[:, parity, j], cf[:, j % 2], ACT.Copy).then_inc(ch_ok, 1)

                nc.scalar.activation(hh[:], h[:], ACT.Copy).then_inc(hh_ok, 1)
                high_u(0, 0, 16, None)
                groups(act, step)
                act.wait_ge(acc_ok, 2)
                nc.scalar.activation(squares, acc[:], ACT.Square).then_inc(fsq_ok, 1)
                act.wait_ge(fms_ok, 1)
                nc.scalar.activation(rs[:], rs[:], ACT.Sqrt).then_inc(frt_ok, 1)
                act.wait_ge(frt_ok, 1)

            @block.vector
            def _(dve):
                done = [0]

                def link(ins):
                    done[0] += 1
                    ins.then_inc(steps, 1)
                    dve.wait_ge(steps, done[0])

                def low(out, full, high):
                    return nc.vector.tensor_tensor(out, full, high.bitcast(F32), ALU.subtract)

                def step(g, parity, make, add):
                    for j in range(GB):
                        n = g * GB + j
                        if make:
                            if not (isinstance(g, int) and g == NGRP - 1 and j == GB - 1):
                                dve.wait_ge(uh_ok, n + 2)
                                low(ul[:, (j + 1) % 2], us[:, (j + 1) % NU], uh[:, (j + 1) % 2]).then_inc(ul_ok, 1)
                            dve.wait_ge(a_ok, n + 1)
                            if j == 0:
                                dve.wait_ge(g_in[parity], g * 8 + (16 - 8 * parity))
                            by_chunk = lambda ap: ap.rearrange("p (c t) -> p c t", t=CH)
                            nc.vector.tensor_tensor(by_chunk(cf[:, j % 2]), by_chunk(a[:, j % 2]),
                                                    gt[:, parity, :, j, :], ALU.mult).then_inc(c_ok, 1)
                        if add:
                            dve.wait_ge(vh_ok, g * GB + (j + 1 - GB))
                            low(vl[:, j], vs[:, j % NV], vh[:, j]).then_inc(vl_ok, 1)
                        if make:
                            dve.wait_ge(ch_ok, n + 1)
                            low(cl[:, parity, j], cf[:, j % 2], ch[:, parity, j]).then_inc(cl_ok, 1)
                    if add:
                        for k in range(KD):
                            dve.wait_ge(f_mm, g * KD + (k + 1))
                            nc.vector.tensor_tensor(halves(acc[:, k]), pair(2 + k % 2), halves(acc[:, k]), ALU.add)\
                                .then_inc(f_ok, 1)

                dve.sem_inc(f_ok, 2)
                dve.wait_ge(hh_ok, 1)
                low(hl[:], h[:], hh[:]).then_inc(hl_ok, 1)
                dve.wait_ge(uh_ok, 1)
                low(ul[:, 0], us[:, 0], uh[:, 0]).then_inc(ul_ok, 1)
                dve.wait_ge(hl_ok, 1)
                nc.vector.memset(acc[:], 0.0).then_inc(acc_ok, 1)
                groups(dve, step)
                dve.wait_ge(f_ok, NGRP * KD + 2)
                dve.sem_inc(acc_ok, 1)
                dve.wait_ge(fss_mm, 1)
                nc.vector.tensor_scalar(halves(rs[:]), pair(0), 1.0 / D, EPS, ALU.mult, ALU.add).then_inc(fms_ok, 1)
                dve.wait_ge(frt_ok, 1)
                link(nc.vector.reciprocal(rs[:], rs[:]))
                residual(dve, link, acc, 3).then_inc(y_ok, 1)


def kernel(**inputs):
    from concourse import bacc
    from concourse.bass_utils import run_bass_kernel_spmd

    f32 = np.float32
    a = {k: np.asarray(v) for k, v in inputs.items()}
    laid = {}

    def rows_to_partitions(m):
        return np.ascontiguousarray(m.reshape(-1, P, m.shape[-1]).transpose(1, 0, 2))

    def columns(w):
        return np.ascontiguousarray(w.reshape(KD, P, -1, WC).transpose(2, 1, 0, 3))

    tokens = np.concatenate([a["x_prompt"][0], a["x_sample"][:, 0]])
    laid["xT"] = rows_to_partitions(tokens.T)
    laid["cT"] = rows_to_partitions(np.concatenate([a["c_prompt"], a["c_sample"]]).T)
    laid["w_ada"] = columns(a["w_ada"][0])
    laid["b_ada"] = np.ascontiguousarray(a["b_ada"][0].reshape(-1, P).T)
    laid["gains"] = np.ascontiguousarray(
        np.stack([a[n][0].reshape(KD, P) for n in ("g_pre1", "g_post1", "g_pre2", "g_post2")]).transpose(2, 0, 1))
    laid["w_in"] = columns(a["w_in"][0])
    laid["w_out"] = columns(a["w_out"][0])
    laid["w_q"] = columns(a["w_q"][0])
    laid["keysT"] = np.ascontiguousarray(a["sub_keys"][0].reshape(2 * PH, NK, P).transpose(2, 0, 1))
    laid["utab"] = np.ascontiguousarray(a["u_tab"][0].reshape(NK, NK, KD, P).transpose(1, 3, 2, 0))
    laid["vtab"] = np.ascontiguousarray(a["v_tab"][0].reshape(NK, NK, D))
    laid["s0"] = np.ascontiguousarray(a["state_ret"][0].transpose(2, 0, 1, 3))
    laid["conv_s"] = np.ascontiguousarray(a["cache_conv"][0].reshape(NS, CK - 1, RH, P).transpose(3, 2, 1, 0))
    laid["conv_w"] = np.ascontiguousarray(
        np.concatenate([a["conv_w"][0], a["conv_b"]]).reshape(CK + 1, RH, P).transpose(2, 1, 0))

    half = P // 2
    freqs = (f32(10000.0) ** (-np.arange(half, dtype=f32) / half)).astype(f32)
    where = np.concatenate([np.arange(SEQ), np.full(NS, PAST)]).astype(f32)
    angle = (freqs[:, None] * where[None, :]).astype(f32).astype(np.float64)
    cos = np.concatenate([np.cos(angle)] * 2)
    sin = np.concatenate([np.sin(angle), -np.sin(angle)])
    laid["trig"] = np.ascontiguousarray(
        np.stack([cos, sin, cos * P ** -0.5, sin * P ** -0.5]).transpose(1, 0, 2).astype(f32))
    gamma = 1.0 - 2.0 ** (-5.0 - np.arange(RH))
    rel = np.arange(SEQ)[None, :] - np.arange(P)[:, None]
    laid["decay"] = np.where(rel >= 0, gamma[:, None, None] ** np.maximum(rel, 0), 0.0).astype(f32)
    age = SEQ - 1 - np.arange(SEQ).reshape(CHUNKS, P)
    laid["kdecay"] = np.ascontiguousarray((gamma[:, None, None] ** age).transpose(2, 0, 1).astype(f32))
    laid["consts"] = np.ascontiguousarray(np.stack(
        [np.ones((P, P)), np.eye(P), np.tile(np.arange(P), (P, 1))]).transpose(1, 0, 2).astype(f32))
    laid["starts"] = np.repeat(np.eye(NS, dtype=f32)[:, :, None], P, 2)

    nc = bacc.Bacc("TRN2", target_bir_lowering=False, num_devices=1)
    args = {k: nc.dram_tensor(k, v.shape, F32, kind="ExternalInput").ap() for k, v in laid.items()}
    outs = {"yT": (P, KD, T), "ret_p": (P, RH, P), "conv_p": (P, RH, CK - 1), "ret_s": (P, NS, RH, P),
            "conv_so": (P, RH, CK - 1, NS)}
    args |= {k: nc.dram_tensor(k, v, F32, kind="ExternalOutput").ap() for k, v in outs.items()}
    args["gates_dram"] = nc.dram_tensor("gates_dram", (NGRP, P, NCH, GB, CH), F32, kind="Internal").ap()
    build(nc, **args)
    r = run_bass_kernel_spmd(nc, [laid], core_ids=[0]).results[0]

    y = r["yT"].transpose(2, 1, 0).reshape(T, D)
    return (y[None, :SEQ], y[SEQ:, None, :],
            r["ret_p"].transpose(1, 0, 2)[None, None],
            r["conv_p"].transpose(2, 1, 0).reshape(1, 1, CK - 1, RH * P),
            r["ret_s"].transpose(1, 2, 0, 3)[None],
            r["conv_so"].transpose(3, 2, 1, 0).reshape(1, NS, CK - 1, RH * P))
```

```python
from contextlib import ExitStack

import numpy as np
import concourse.bass as bass
from concourse import mybir

F32 = mybir.dt.float32
F32R = mybir.dt.float32r
U32 = mybir.dt.uint32
ALU = mybir.AluOpType
ACT = mybir.ActivationFunctionType
AX = mybir.AxisListType

P = 128
D = 1024
KD = D // P
SEQ = 512
NS = 8
T = SEQ + NS
TH = T // 2
RH = 4
CHUNKS = SEQ // P
CK = 3
PAST = 4096
EPS = 1e-6
WC = 256
WB = WC // P
NSLOT = 4
PH = 8
NK = 128
TOPK = 16
HK = PH * TOPK
TT = 104
TILES = T // TT
CH = 26
TCH = TT // CH
NCH = T // CH
OH = 4
GB = 4
NGRP = NK // GB
AB = 12
AHEAD = AB * (TILES + 1)
AGRP = AHEAD // GB
NU = 2
LOWEST = -3.0e38

ADA, WIN, WOUT, WQ = "ada", "in", "out", "q"


def weight_loads():
    order = [(ADA, n) for n in range(2 * KD // WB)]
    for group in (0, 1, 2, 3, 5, 6, 4):
        order += [(WIN, group * 2 + n) for n in range(2)]
    order += [(WOUT, n) for n in range(D // WC)]
    order += [(ADA, n) for n in range(2 * KD // WB, 6 * KD // WB)]
    order += [(WQ, n) for n in range(2 * PH * P // WC)]
    return order


def build(nc, xT, cT, w_ada, b_ada, gains, w_in, w_out, w_q, keysT, utab, vtab, s0, conv_s, conv_w,
          trig, decay, kdecay, consts, starts,
          yT, ret_p, conv_p, ret_s, conv_so, gates_dram, ahead_dram):
    outer = ExitStack()
    with outer:
        def sb(stack, name, shape, dt=F32, side="left"):
            return stack.enter_context(nc.sbuf_tensor(name, shape, dt, side=side))

        def sem(name):
            return outer.enter_context(nc.semaphore(name))

        x = sb(outer, "x", [P, KD, T])
        h = sb(outer, "h", [P, KD, T])
        mod = sb(outer, "mod", [P, 6 * KD, 1 + NS])
        cst = sb(outer, "cst", [P, 4, P])
        gain = sb(outer, "gain", [P, 4, KD])
        co = sb(outer, "co", [P, 4, KD, 1 + NS])
        tsm = sb(outer, "tsm", [P, KD, NS])
        rs = sb(outer, "rs", [P, T])
        ones, ident, iota = cst[:, 0, :], cst[:, 1, :], cst[:, 2, :]
        ps = outer.enter_context(nc.psum_tensor("ps", [P, 8, 512], F32))

        def pair(n):
            return ps[:, 2 * n:2 * n + 2, 0:TH]

        def halves(ap):
            return ap.rearrange("p (a b) -> p a b", a=2)

        def residual(dve, link, m, slot):
            link(nc.vector.tensor_tensor(m[:], m[:], rs[:].unsqueeze(1).to_broadcast([P, KD, T]), ALU.mult))
            for k in range(KD):
                nc.vector.scalar_tensor_tensor(x[:, k, 0:SEQ], m[:, k, 0:SEQ], co[:, slot, k, 0:1], x[:, k, 0:SEQ],
                                               ALU.mult, ALU.add)
            link(nc.vector.tensor_tensor(tsm[:], m[:, :, SEQ:T], co[:, slot, :, 1:1 + NS], ALU.mult))
            return nc.vector.tensor_tensor(x[:, :, SEQ:T], x[:, :, SEQ:T], tsm[:], ALU.add)

        upto_gates = ExitStack()
        qp = sb(upto_gates, "qp", [P, 2 * PH, T])
        io = dict(xT=xT, cT=cT, b_ada=b_ada, gains=gains, keysT=keysT, utab=utab, vtab=vtab, s0=s0,
                  conv_s=conv_s, conv_w=conv_w, trig=trig, decay=decay, kdecay=kdecay, consts=consts,
                  starts=starts, yT=yT, ret_p=ret_p, conv_p=conv_p, ret_s=ret_s, conv_so=conv_so,
                  gates=gates_dram)
        on_chip = (x, h, mod, cst, gain, co, tsm, rs, ps)
        mixer_stage(nc, sem, sb, pair, halves, residual, on_chip, qp, io,
                    {ADA: w_ada, WIN: w_in, WOUT: w_out, WQ: w_q})
        io["ahead"] = ahead_dram
        u_side = dict(
            hh=sb(outer, "hh", [P, KD, T], F32R, "right"), hl=sb(outer, "hl", [P, KD, T], F32R, "right"),
            us=sb(outer, "us", [P, NU, KD, P], F32, "right"),
            uh=sb(outer, "uh", [P, 2, KD, P], F32R, "right"), ul=sb(outer, "ul", [P, 2, KD, P], F32R, "right"),
            a=sb(outer, "a", [P, 2, T], F32, "right"),
            u_in=[sem(f"u_in{n}") for n in range(NU)],
            uh_ok=sem("uh_ok"),
            ul_ok=sem("ul_ok"),
            u_mm=sem("u_mm"),
            a_ok=sem("a_ok"))
        gate_stage(nc, sem, sb, pair, halves, on_chip, qp, u_side, io)
        upto_gates.close()
        expert_stage(nc, sem, sb, pair, halves, residual, on_chip, u_side, io)


def u_pairs(i):
    return 1 + i % 2


def u_product(nc, out, uh, ul, hh, hl, k):
    for n, (w, m) in enumerate(((uh, hl), (uh, hh), (ul, hh))):
        for half in range(2):
            last = nc.tensor.matmul(out[:, half, :], w[:, k, :], m[:, k, half * TH:(half + 1) * TH],
                                    start=(k == 0 and n == 0), stop=(k == KD - 1 and n == 2))
    return last


def positive(value):
    return not isinstance(value, int) or value > 0


def mixer_stage(nc, sem, sb, pair, halves, residual, on_chip, qp, io, w_dram):
    x, h, mod, cst, gain, co, tsm, rs, ps = on_chip
    ones, ident = cst[:, 0, :], cst[:, 1, :]
    stack = ExitStack()
    with stack:
        wr = sb(stack, "wr", [P, NSLOT, KD, WC])
        scr = sb(stack, "scr", [P, KD, T])
        qk = sb(stack, "qk", [P, 2, RH, T])
        vt = sb(stack, "vt", [P, CHUNKS, RH * P])
        vs = sb(stack, "vs", [NS, RH * P])
        mix = sb(stack, "mix", [P, KD, T])
        ext = sb(stack, "ext", [P, RH, CK - 1 + SEQ])
        exs = sb(stack, "exs", [P, RH, CK, NS])
        tg = sb(stack, "tg", [P, 4, T])
        dec = sb(stack, "dec", [P, 2, SEQ])
        kde = sb(stack, "kde", [P, RH, CHUNKS])
        pr = sb(stack, "pr", [P, CHUNKS, SEQ])
        kd = sb(stack, "kd", [P, CHUNKS, P])
        so = sb(stack, "so", [P, RH, P])
        t1 = sb(stack, "t1", [P, T])
        t2 = sb(stack, "t2", [P, T])
        cs = sb(stack, "cs", [P, KD, 1 + NS])
        bad = sb(stack, "bad", [P, 6 * KD])
        cw = sb(stack, "cw", [P, RH, CK + 1])
        sel = sb(stack, "sel", [NS, NS, P])
        state = scr[:, :, :].rearrange("p a b -> p (a b)")[:, 0:NS * RH * P]\
            .rearrange("p (b h e) -> p b h e", b=NS, h=RH)

        w_slot = [sem(f"w_slot{n}") for n in range(NSLOT)]
        in_x, in_c, in_cst, in_trig, in_state, in_misc = (
            sem(n) for n in ("in_x", "in_c", "in_cst", "in_trig", "in_state", "in_misc"))
        in_dec = [sem(f"in_dec{hd}") for hd in range(RH)]
        stored = sem("mixer_stored")
        silu_c = sem("silu_c")
        mod_mm = sem("mod_mm")
        mod_ok = sem("mod_ok")
        sq_ok = sem("sq_ok")
        ss_mm = sem("ss_mm")
        ms_ok = sem("ms_ok")
        rt_ok = sem("rt_ok")
        h_ok = sem("h_ok")
        proj_mm = sem("proj_mm")
        rot_mul = sem("rot_mul")
        rot_ok = sem("rot_ok")
        v_mm = sem("v_mm")
        v_ok = sem("v_ok")
        g_ok = sem("g_ok")
        cg_ok = sem("cg_ok")
        zero_ok = sem("zero_ok")
        u_ok = sem("u_ok")
        conv_ok = sem("conv_ok")
        sc_mm = sem("sc_mm")
        pr_ok = sem("pr_ok")
        kt_mm = sem("kt_mm")
        kd_ok = sem("kd_ok")
        st_mm = sem("st_mm")
        st_ok = sem("st_ok")
        s0_ok = sem("s0_ok")
        vb_mm = sem("vb_mm")
        sn_ok = sem("sn_ok")
        o_mm = sem("o_mm")
        o_ok = sem("o_ok")
        mu_mm = sem("mu_mm")
        oc_ok = sem("oc_ok")
        oq_ok = sem("oq_ok")
        va_mm = sem("va_mm")
        ve_ok = sem("ve_ok")
        sd_ok = sem("sd_ok")
        ret_ok = sem("ret_ok")
        m_ok = sem("m_ok")
        x1_ok = sem("x1_ok")
        qp_ok = sem("qp_ok")
        steps = sem("mixer_dve")

        Q0, K0, G0, C0, X0, B0, M0 = (RH * n for n in range(7))
        Q2 = M0 + KD
        RING = 3

        def read_of(m):
            for start, s in ((Q2, qp_ok), (M0, m_ok), (B0, conv_ok), (X0, u_ok), (C0, cg_ok), (G0, g_ok),
                             (Q0, rot_mul)):
                if m >= start:
                    return s, m - start + 1

        order = weight_loads()
        used_of, n_ada, n_v, n_blocks = [], 0, 0, 0
        for kind, at in order:
            if kind == ADA:
                n_ada += 1
                used_of.append((mod_mm, n_ada))
            elif kind == WIN and at // 2 == 2:
                n_v += 1
                used_of.append((v_mm, n_v))
            else:
                n_blocks += WB
                used_of.append((proj_mm, n_blocks))

        ADA1 = 2 * KD // WB
        ADA2 = 4 * KD // WB

        with nc.Block() as block:

            @block.sync
            def _(sp):
                sp.dma_start(cs[:], io["cT"]).then_inc(in_c, 16)

                def load(n):
                    kind, at = order[n]
                    if n >= NSLOT:
                        s, value = used_of[n - NSLOT]
                        sp.wait_ge(s, value)
                    sp.dma_start(wr[:, n % NSLOT], w_dram[kind][at]).then_inc(w_slot[n % NSLOT], 16)

                load(0)
                sp.dma_start(x[:], io["xT"]).then_inc(in_x, 16)
                sp.dma_start(cst[:], io["consts"]).then_inc(in_cst, 16)
                for n in range(1, NSLOT):
                    load(n)
                for dst, name in ((bad[:], "b_ada"), (gain[:], "gains"), (cw[:], "conv_w"),
                                  (exs[:, :, 0:CK - 1, :], "conv_s"), (kde[:], "kdecay"), (sel[:], "starts")):
                    sp.dma_start(dst, io[name]).then_inc(in_misc, 16)
                sp.dma_start(tg[:], io["trig"]).then_inc(in_trig, 16)
                for hd in range(2):
                    sp.dma_start(dec[:, hd, :], io["decay"][hd]).then_inc(in_dec[hd], 16)
                for n in range(NSLOT, len(order)):
                    load(n)
                    if n == 3 * NSLOT:
                        sp.wait_ge(ss_mm, 1)
                        sp.dma_start(state, io["s0"]).then_inc(in_state, 16)

            @block.tensor
            def _(pe):
                loaded = [0]
                made = [0]

                def weights():
                    n = loaded[0]
                    loaded[0] += 1
                    pe.wait_ge(w_slot[n % NSLOT], 16 * (n // NSLOT + 1))
                    return n % NSLOT

                def adaln(n_loads):
                    for n in range(n_loads):
                        s = weights()
                        for b in range(WB):
                            at = (n * WB + b) * (1 + NS)
                            for k in range(KD):
                                last = nc.tensor.matmul(ps[:, 7, at:at + 1 + NS], wr[:, s, k, b * P:(b + 1) * P],
                                                        cs[:, k, :], start=(k == 0), stop=(k == KD - 1))
                        last.then_inc(mod_mm, 1)

                def norm_sum(n, squares):
                    pe.wait_ge(sq_ok, n)
                    for k in range(KD):
                        for a in range(2):
                            last = nc.tensor.matmul(ps[:, a, 0:TH], ones, squares[:, k, a * TH:(a + 1) * TH],
                                                    start=(k == 0), stop=(k == KD - 1))
                    last.then_inc(ss_mm, 1)

                def blocks(n_loads, rhs):
                    for n in range(n_loads):
                        s = weights()
                        for b in range(WB):
                            m = made[0]
                            if m >= RING:
                                pe.wait_ge(*read_of(m - RING))
                            for k in range(KD):
                                for a in range(2):
                                    last = nc.tensor.matmul(ps[:, 2 * (m % RING) + a, 0:TH],
                                                            wr[:, s, k, b * P:(b + 1) * P],
                                                            rhs[:, k, a * TH:(a + 1) * TH],
                                                            start=(k == 0), stop=(k == KD - 1))
                            last.then_inc(proj_mm, 1)
                            made[0] += 1

                def all_read():
                    for m in range(max(0, made[0] - RING), made[0]):
                        pe.wait_ge(*read_of(m))

                pe.wait_ge(silu_c, 1)
                adaln(ADA1)
                pe.wait_ge(in_cst, 16)
                norm_sum(1, scr)
                pe.wait_ge(h_ok, 1)
                blocks(4, h)
                all_read()
                for half in range(2):
                    s = weights()
                    for c in range(CHUNKS + 1):
                        cols = slice(c * P, min(T, (c + 1) * P))
                        rows = cols.stop - cols.start
                        for k in range(KD):
                            last = nc.tensor.matmul(ps[0:rows, c, half * WC:(half + 1) * WC],
                                                    h[:, k, cols], wr[:, s, k, :],
                                                    start=(k == 0), stop=(k == KD - 1))
                    last.then_inc(v_mm, 1)
                pe.wait_ge(v_ok, 2)
                blocks(8, h)

                pe.wait_ge(rot_ok, 2 * RH)
                all_read()
                for hd in range(RH):
                    q, k = qk[:, 0, hd, :], qk[:, 1, hd, :]
                    for c in range(CHUNKS):
                        if hd:
                            pe.wait_ge(pr_ok, CHUNKS * (hd - 1) + c + 1)
                        nc.tensor.matmul(ps[:, c, 0:SEQ - c * P], k[:, c * P:(c + 1) * P], q[:, c * P:SEQ],
                                         start=True, stop=True).then_inc(sc_mm, 1)
                    if hd:
                        pe.wait_ge(kd_ok, CHUNKS * hd)
                    for c in range(CHUNKS):
                        last = nc.tensor.transpose(ps[:, 4, c * P:(c + 1) * P], k[:, c * P:(c + 1) * P], ident)
                    last.then_inc(kt_mm, 1)
                    if hd:
                        pe.wait_ge(o_ok, hd)
                    for c in range(CHUNKS):
                        pe.wait_ge(pr_ok, CHUNKS * hd + c + 1)
                        last = nc.tensor.matmul(ps[:, 5, c * P:SEQ], vt[:, c, hd * P:(hd + 1) * P],
                                                pr[:, c, 0:SEQ - c * P], start=(c == 0), stop=(c == CHUNKS - 1))
                    last.then_inc(o_mm, 1)
                    pe.wait_ge(kd_ok, CHUNKS * (hd + 1))
                    if hd:
                        pe.wait_ge(st_ok, hd)
                    for c in range(CHUNKS):
                        last = nc.tensor.matmul(ps[:, 6, 0:P], kd[:, c, :], vt[:, c, hd * P:(hd + 1) * P],
                                                start=(c == 0), stop=(c == CHUNKS - 1))
                    last.then_inc(st_mm, 1)
                pe.wait_ge(in_misc, 16 * 6)
                for b in range(NS):
                    if b >= 2:
                        pe.wait_ge(sn_ok, b - 1)
                    nc.tensor.matmul(ps[:, b % 2, :], sel[:, b, :], vs[:], start=True, stop=True)\
                        .then_inc(vb_mm, 1)
                pe.wait_ge(sn_ok, NS)
                for hd in range(RH):
                    for b in range(NS):
                        last = nc.tensor.matmul(ps[:, 2, hd * NS + b:hd * NS + b + 1], state[:, b, hd, :],
                                                qk[:, 0, hd, SEQ + b:SEQ + b + 1], start=True, stop=True)
                last.then_inc(o_mm, 1)
                pe.wait_ge(o_ok, RH + 1)
                for hd in range(RH):
                    o = qk[:, 1, hd, :]
                    if hd:
                        pe.wait_ge(oc_ok, hd)
                    for a in range(2):
                        last = nc.tensor.matmul(ps[:, a, 0:TH], ones, o[:, a * TH:(a + 1) * TH],
                                                start=True, stop=True)
                    last.then_inc(mu_mm, 1)
                    pe.wait_ge(oq_ok, hd + 1)
                    if hd:
                        pe.wait_ge(ve_ok, hd)
                    for a in range(2):
                        last = nc.tensor.matmul(ps[:, 2 + a, 0:TH], ones, t1[:, a * TH:(a + 1) * TH],
                                                start=True, stop=True)
                    last.then_inc(va_mm, 1)
                pe.wait_ge(ret_ok, RH)
                pe.wait_ge(conv_ok, RH)
                pe.wait_ge(st_ok, RH)
                blocks(D // WC, mix)
                pe.wait_ge(mod_ok, 1)
                adaln(ADA2)
                all_read()
                norm_sum(2, mix)
                norm_sum(3, mix)
                pe.wait_ge(h_ok, 2)
                blocks(2 * PH * P // WC, h)

            @block.scalar
            def _(act):
                act.wait_ge(in_c, 16)
                nc.scalar.activation(cs[:], cs[:], ACT.Silu).then_inc(silu_c, 1)
                act.wait_ge(in_x, 16)
                nc.scalar.activation(scr[:], x[:], ACT.Square).then_inc(sq_ok, 1)

                def root(n):
                    act.wait_ge(ms_ok, n)
                    nc.scalar.activation(rs[:], rs[:], ACT.Sqrt).then_inc(rt_ok, 1)

                root(1)
                act.wait_ge(v_mm, 2)
                nc.scalar.activation(vt[:], ps[:, 0:CHUNKS, :], ACT.Copy).then_inc(v_ok, 1)
                nc.scalar.activation(vs[:], ps[0:NS, CHUNKS, :], ACT.Copy).then_inc(v_ok, 1)
                act.wait_ge(rot_ok, 2 * RH)
                for b in range(RH):
                    act.wait_ge(proj_mm, G0 + b + 1)
                    nc.scalar.activation(halves(mix[:, b, :]), pair((G0 + b) % RING), ACT.Silu).then_inc(g_ok, 1)
                for b in range(RH):
                    act.wait_ge(proj_mm, C0 + b + 1)
                    nc.scalar.activation(halves(mix[:, RH + b, :]), pair((C0 + b) % RING), ACT.Copy)\
                        .then_inc(cg_ok, 1)
                act.wait_ge(in_misc, 16 * 6)
                for hd in range(RH):
                    act.wait_ge(kt_mm, hd + 1)
                    if hd:
                        act.wait_ge(st_mm, hd)
                    for c in range(CHUNKS):
                        nc.scalar.activation(kd[:, c, :], ps[:, 4, c * P:(c + 1) * P], ACT.Copy,
                                             scale=kde[:, hd, c:c + 1]).then_inc(kd_ok, 1)
                    act.wait_ge(o_mm, hd + 1)
                    nc.scalar.activation(qk[:, 1, hd, 0:SEQ], ps[:, 5, :], ACT.Copy).then_inc(o_ok, 1)
                    act.wait_ge(st_mm, hd + 1)
                    nc.scalar.activation(so[:, hd, :], ps[:, 6, 0:P], ACT.Copy).then_inc(st_ok, 1)
                act.wait_ge(o_mm, RH + 1)
                nc.scalar.activation(qk[:, 1, :, SEQ:T], ps[:, 2, 0:RH * NS].rearrange("p (h b) -> p h b", h=RH),
                                     ACT.Copy).then_inc(o_ok, 1)
                for hd in range(RH):
                    act.wait_ge(oc_ok, hd + 1)
                    if hd:
                        act.wait_ge(va_mm, hd)
                    nc.scalar.activation(t1[:], qk[:, 1, hd, :], ACT.Square).then_inc(oq_ok, 1)
                    act.wait_ge(ve_ok, hd + 1)
                    nc.scalar.activation(t2[:], t2[:], ACT.Sqrt).then_inc(sd_ok, 1)
                act.wait_ge(stored, 16 * 4)
                for b in range(KD):
                    act.wait_ge(proj_mm, M0 + b + 1)
                    nc.scalar.activation(halves(scr[:, b, :]), pair((M0 + b) % RING), ACT.Copy).then_inc(m_ok, 1)
                act.wait_ge(m_ok, KD)
                nc.scalar.activation(mix[:], scr[:], ACT.Square).then_inc(sq_ok, 1)
                root(2)
                act.wait_ge(x1_ok, 1)
                nc.scalar.activation(mix[:], x[:], ACT.Square).then_inc(sq_ok, 1)
                root(3)
                for b in range(2 * PH):
                    act.wait_ge(proj_mm, Q2 + b + 1)
                    nc.scalar.activation(halves(qp[:, b, :]), pair((Q2 + b) % RING), ACT.Copy).then_inc(qp_ok, 1)
                act.wait_ge(qp_ok, 2 * PH)

            @block.gpsimd
            def _(pool):
                nc.gpsimd.memset(ext[:, :, 0:CK - 1], 0.0).then_inc(zero_ok, 1)
                for n in range(2 * RH):
                    pool.wait_ge(rot_mul, n + 1)
                    nc.gpsimd.tensor_tensor(qk[:, n // RH, n % RH, :], mix[:, n % 2, :], mix[:, 2 + n % 2, :],
                                            ALU.add).then_inc(rot_ok, 1)
                pool.wait_ge(in_state, 16)
                for hd in range(RH):
                    nc.gpsimd.tensor_scalar(state[:, :, hd, :], state[:, :, hd, :], 1.0 - 2.0 ** (-5 - hd),
                                            None, ALU.mult).then_inc(s0_ok, 1)
                pool.wait_ge(u_ok, RH)
                pool.wait_ge(in_misc, 16 * 6)
                pool.dma_start(io["conv_p"], ext[:, :, SEQ:SEQ + CK - 1]).then_inc(stored, 16)
                pool.dma_start(io["conv_so"], exs[:, :, 1:CK, :]).then_inc(stored, 16)
                for hd in range(2, RH):
                    pool.wait_ge(pr_ok, CHUNKS * (hd - 1))
                    pool.dma_start(dec[:, hd % 2, :], io["decay"][hd]).then_inc(in_dec[hd], 16)
                pool.wait_ge(st_ok, RH)
                pool.dma_start(io["ret_p"], so[:]).then_inc(stored, 16)
                pool.wait_ge(sn_ok, NS)
                pool.dma_start(io["ret_s"], state).then_inc(stored, 16)
                pool.wait_ge(stored, 16 * 4)

            @block.vector
            def _(dve):
                done = [0]

                def link(ins):
                    done[0] += 1
                    ins.then_inc(steps, 1)
                    dve.wait_ge(steps, done[0])

                def coefficients(slot, part, g):
                    m = mod[:, part * KD:(part + 1) * KD, :]
                    gb = gain[:, g, :].unsqueeze(2).to_broadcast([P, KD, 1 + NS])
                    if part % 3 == 1:
                        link(nc.vector.scalar_tensor_tensor(co[:, slot], m, 1.0, gb, ALU.add, ALU.mult))
                    else:
                        link(nc.vector.tensor_tensor(co[:, slot], m, gb, ALU.mult))

                def mod_part(n_loads, lo, hi):
                    dve.wait_ge(mod_mm, n_loads)
                    sums = ps[:, 7, 0:(hi - lo) * 9].rearrange("p (b s) -> p b s", s=9)
                    nc.vector.tensor_tensor(mod[:, lo:hi, :], sums,
                                            bad[:, lo:hi].unsqueeze(2).to_broadcast([P, hi - lo, 9]), ALU.add)\
                        .then_inc(mod_ok, 1)

                def inverse_rms(n):
                    dve.wait_ge(ss_mm, n)
                    nc.vector.tensor_scalar(halves(rs[:]), pair(0), 1.0 / D, EPS, ALU.mult, ALU.add)\
                        .then_inc(ms_ok, 1)
                    dve.wait_ge(rt_ok, n)
                    link(nc.vector.reciprocal(rs[:], rs[:]))

                def modulated(slot, shift):
                    link(nc.vector.tensor_tensor(h[:], x[:], rs[:].unsqueeze(1).to_broadcast([P, KD, T]), ALU.mult))
                    for k in range(KD):
                        nc.vector.tensor_scalar(h[:, k, 0:SEQ], h[:, k, 0:SEQ], co[:, slot, k, 0:1],
                                                mod[:, shift * KD + k, 0:1], ALU.mult, ALU.add)
                    link(nc.vector.tensor_tensor(tsm[:], h[:, :, SEQ:T], co[:, slot, :, 1:1 + NS], ALU.mult))
                    nc.vector.tensor_tensor(h[:, :, SEQ:T], tsm[:], mod[:, shift * KD:(shift + 1) * KD, 1:1 + NS],
                                            ALU.add).then_inc(h_ok, 1)

                dve.wait_ge(in_misc, 16 * 6)
                mod_part(ADA1, 0, 2 * KD)
                dve.wait_ge(mod_ok, 1)
                coefficients(0, 1, 0)
                inverse_rms(1)
                modulated(0, 0)

                dve.wait_ge(in_trig, 16)
                for n in range(2 * RH):
                    pq = pair(n % RING)
                    which = 2 * (n // RH)
                    dve.wait_ge(proj_mm, n + 1)
                    if n >= 2:
                        dve.wait_ge(rot_ok, n - 1)
                    nc.vector.tensor_tensor(halves(mix[:, n % 2, :]), pq, halves(tg[:, which, :]), ALU.mult)
                    for lo in (0, P // 2):
                        hi = P // 2 - lo
                        last = nc.vector.tensor_tensor(halves(mix[lo:lo + P // 2, 2 + n % 2, :]),
                                                       pq[hi:hi + P // 2],
                                                       halves(tg[hi:hi + P // 2, which + 1, :]), ALU.mult)
                    last.then_inc(rot_mul, 1)
                dve.wait_ge(zero_ok, 1)
                for b in range(RH):
                    n = X0 + b
                    dve.wait_ge(proj_mm, n + 1)
                    dve.wait_ge(cg_ok, b + 1)
                    c, xv = mix[:, RH + b, :], pair(n % RING)
                    nc.vector.tensor_tensor(ext[:, b, CK - 1:CK - 1 + TH], xv[:, 0, :], c[:, 0:TH], ALU.mult)
                    nc.vector.tensor_tensor(ext[:, b, CK - 1 + TH:CK - 1 + SEQ], xv[:, 1, 0:SEQ - TH],
                                            c[:, TH:SEQ], ALU.mult)
                    nc.vector.tensor_tensor(exs[:, b, CK - 1, :], xv[:, 1, SEQ - TH:TH],
                                            c[:, SEQ:T], ALU.mult).then_inc(u_ok, 1)
                dve.wait_ge(u_ok, RH)
                for j in range(CK):
                    for b in range(RH):
                        y = mix[:, RH + b, :]
                        for tap, out in ((ext[:, b, j:j + SEQ], y[:, 0:SEQ]), (exs[:, b, j, :], y[:, SEQ:T])):
                            if j == 0:
                                last = nc.vector.tensor_scalar(out, tap, cw[:, b, 0:1], cw[:, b, CK:CK + 1],
                                                               ALU.mult, ALU.add)
                            else:
                                last = nc.vector.scalar_tensor_tensor(out, tap, cw[:, b, j:j + 1], out,
                                                                      ALU.mult, ALU.add)
                    link(last)
                for b in range(RH):
                    y = halves(mix[:, RH + b, :])
                    dve.wait_ge(proj_mm, B0 + b + 1)
                    nc.vector.tensor_tensor(y, pair((B0 + b) % RING), y, ALU.mult).then_inc(conv_ok, 1)
                for hd in range(RH):
                    dve.wait_ge(in_dec[hd], 16)
                    if hd:
                        dve.wait_ge(o_mm, hd)
                    for c in range(CHUNKS):
                        dve.wait_ge(sc_mm, CHUNKS * hd + c + 1)
                        nc.vector.tensor_tensor(pr[:, c, 0:SEQ - c * P], ps[:, c, 0:SEQ - c * P],
                                                dec[:, hd % 2, 0:SEQ - c * P], ALU.mult).then_inc(pr_ok, 1)
                dve.wait_ge(s0_ok, RH)
                for b in range(NS):
                    dve.wait_ge(vb_mm, b + 1)
                    for hd in range(RH):
                        last = nc.vector.scalar_tensor_tensor(
                            state[:, b, hd, :], ps[:, b % 2, hd * P:(hd + 1) * P],
                            qk[:, 1, hd, SEQ + b:SEQ + b + 1], state[:, b, hd, :], ALU.mult, ALU.add)
                    last.then_inc(sn_ok, 1)
                for hd in range(RH):
                    o = qk[:, 1, hd, :]
                    dve.wait_ge(mu_mm, hd + 1)
                    nc.vector.scalar_tensor_tensor(halves(o), pair(0), -1.0 / P, halves(o), ALU.mult, ALU.add)\
                        .then_inc(oc_ok, 1)
                    dve.wait_ge(va_mm, hd + 1)
                    nc.vector.tensor_scalar(halves(t2[:]), pair(1), 1.0 / P, EPS, ALU.mult, ALU.add)\
                        .then_inc(ve_ok, 1)
                    dve.wait_ge(sd_ok, hd + 1)
                    link(nc.vector.reciprocal(t2[:], t2[:]))
                    link(nc.vector.tensor_tensor(t2[:], t2[:], o, ALU.mult))
                    nc.vector.tensor_tensor(mix[:, hd, :], t2[:], mix[:, hd, :], ALU.mult).then_inc(ret_ok, 1)
                mod_part(ADA1 + ADA2, 2 * KD, 6 * KD)
                dve.wait_ge(mod_ok, 2)
                for slot, part in ((1, 2), (2, 4), (3, 5)):
                    coefficients(slot, part, slot)
                inverse_rms(2)
                residual(dve, link, scr, 1).then_inc(x1_ok, 1)
                inverse_rms(3)
                modulated(2, 3)
                dve.wait_ge(h_ok, 2)


def gate_stage(nc, sem, sb, pair, halves, on_chip, qp, u_side, io):
    x, h, mod, cst, gain, co, tsm, rs, ps = on_chip
    hh, hl, us, uh, ul, a, u_in, uh_ok, ul_ok, u_mm, a_ok = (
        u_side[n] for n in ("hh", "hl", "us", "uh", "ul", "a", "u_in", "uh_ok", "ul_ok", "u_mm", "a_ok"))
    ident, iota = cst[:, 1, :], cst[:, 2, :]
    starts, widths = cst[0:TT, 3, 0:TOPK], cst[0:TT, 3, TOPK:TOPK + 8]
    BT = TT // OH
    BC = 2 * CH // OH
    CREDIT = 2
    STEPS = 22
    BANK_T, BANK_G = 1, 6
    ROW = [TOPK // (r + 1) for r in range(TOPK)]
    AT = [sum(ROW[:r]) for r in range(TOPK)]
    NC = sum(ROW)
    HEAD, TAIL = 1, 4
    STEP = [HEAD * KD + b * (AB - HEAD - TAIL) * KD // BT for b in range(BT + 1)]
    BEHIND = [-1 if r < HEAD else BT if r >= AB - TAIL else
              min(b for b in range(BT) if STEP[b + 1] >= (r + 1) * KD) for r in range(AB)]
    stack = ExitStack()
    with stack:
        keys = sb(stack, "keys", [P, 2 * PH, NK])
        qt = sb(stack, "qt", [P, 2 * PH, TT])
        on_h = h[:].rearrange("p k t -> p (k t)")
        s = on_h[0:TT, 0:2 * PH * NK].rearrange("p (j n) -> p j n", n=NK)
        s2 = on_h[0:TT, 2 * PH * NK:4 * PH * NK].rearrange("p (j n) -> p j n", n=NK)
        cand = sb(stack, "cand", [TT, PH, NC])
        cand2 = sb(stack, "cand2", [TT, PH, NC])
        top = sb(stack, "top", [TT, 2 * PH, TOPK])
        topi = sb(stack, "topi", [TT, 2 * PH, TOPK], U32)
        topf = sb(stack, "topf", [TT, 2 * PH, TOPK])
        diff = sb(stack, "diff", [TT, PH, TOPK])
        best = sb(stack, "best", [TT, PH, TOPK])
        pos = sb(stack, "pos", [TT, PH, TOPK], U32)
        posf = sb(stack, "posf", [TT, HK])
        start = sb(stack, "start", [TT, HK])
        over = sb(stack, "over", [TT, HK])
        ex = sb(stack, "ex", [TT, PH, TOPK])
        den = sb(stack, "den", [TT, PH])
        pick = sb(stack, "pick", [TT, 3, HK])
        pt = sb(stack, "pt", [P, 3, TT])
        eq1 = sb(stack, "eq1", [P, 2, OH, P])
        ga = sb(stack, "ga", [P, 2, OH, P])
        eq2 = sb(stack, "eq2", [P, 2, OH, P])
        stage = sb(stack, "stage", [P, 2, NK, CH])

        in_keys = sem("in_keys")
        hh_ok = sem("hh_ok")
        hl_ok = sem("hl_ok")
        qt_ok = sem("qt_ok")
        s_mm = sem("s_mm")
        s_ok = sem("s_ok")
        steps = sem("gate_dve")
        best_ok = sem("best_ok")
        ex_ok = sem("ex_ok")
        pick_ok = sem("pick_ok")
        pt_mm = sem("pt_mm")
        pt_ok = sem("pt_ok")
        eq1_ok = sem("eq1_ok")
        df2_ok = sem("df2_ok")
        eq2_ok = sem("eq2_ok")
        ga_ok = sem("ga_ok")
        g_mm = sem("gate_mm")
        g_ok = sem("gate_ok")
        kept = [sem(f"kept{c}") for c in range(2)]
        a_kept = [sem(f"a_kept{c}") for c in range(2)]
        settled = sem("settled")
        p_settled = sem("p_settled")

        with nc.Block() as block:

            @block.sync
            def _(sp):
                for c in range(2):
                    sp.sem_inc(a_kept[c], 16)
                sp.dma_start(keys[:], io["keysT"]).then_inc(in_keys, 16)
                u_of = io["utab"][0:AB * (TILES + 2)].rearrange("(i r) p k e -> i r p k e", r=AB)
                out = io["ahead"].rearrange("(i r) p t -> i r p t", r=AB)
                for r in range(NU):
                    sp.dma_start(us[:, r], io["utab"][r]).then_inc(u_in[r], 16)

                with sp.Fori(0, TILES + 1) as i:
                    for r in range(AB):
                        sp.wait_ge(ul_ok, i * AB + (r + 1))
                        nxt = u_of[bass.ds(i, 1), r + NU] if r + NU < AB else u_of[bass.ds(i + 1, 1), r + NU - AB]
                        sp.dma_start(us[:, r % NU], nxt.rearrange("i p k e -> (i p) k e")).then_inc(u_in[r % NU], 16)
                        sp.wait_ge(a_ok, i * AB + (r + 1))
                        sp.dma_start(out[bass.ds(i, 1), r].rearrange("i p t -> (i p) t"), a[:, r % 2])\
                            .then_inc(a_kept[r % 2], 16)
                for c in range(2):
                    sp.wait_ge(a_kept[c], 16 * (AHEAD // 2) + 16)

            @block.tensor
            def _(pe):
                def scores(i):
                    for m in range(4):
                        pe.wait_ge(qt_ok, i * 4 + (m + 1))
                        if m >= 2:
                            pe.wait_ge(s_ok, i * 4 + (m - 1))
                        elif m == BANK_T and positive(i):
                            pe.wait_ge(pt_ok, i)
                        for j in range(4 * m, 4 * m + 4):
                            last = nc.tensor.matmul(ps[0:TT, m % 2, (j % 4) * NK:(j % 4 + 1) * NK], qt[:, j, :],
                                                    keys[:, j, :], start=True, stop=True)
                        last.then_inc(s_mm, 1)

                def ahead(i, first, past):
                    for q in range(first, past):
                        r, k = q // KD, q % KD
                        if k == 0:
                            pe.wait_ge(ul_ok, i * AB + (r + 1))
                            if positive(i) or r >= 2:
                                pe.wait_ge(a_ok, i * AB + (r - 1))
                        last = u_product(nc, pair(u_pairs(r)), uh[:, r % 2], ul[:, r % 2], hh, hl, k)
                        if k == KD - 1:
                            last.then_inc(u_mm, 1)

                def matrix_and_ahead(i):
                    ahead(i, 0, STEP[0])
                    for b in range(BT):
                        if positive(i):
                            pe.wait_ge(eq2_ok, i * BT + (b + 1 - BT))
                            pe.wait_ge(ga_ok, i * BT + (b + 1 - BT))
                            pe.wait_ge(g_ok, i * BT + (b + 1 - BT))
                            for t in range(OH):
                                last = nc.tensor.matmul(ps[:, BANK_G + b % 2, t * P:(t + 1) * P],
                                                        ga[:, b % 2, t, :], eq2[:, b % 2, t, :],
                                                        start=True, stop=True)
                            last.then_inc(g_mm, 1)
                        ahead(i, STEP[b], STEP[b + 1])
                    ahead(i, STEP[BT], AB * KD)

                def turn(i):
                    pe.wait_ge(pick_ok, i + 1)
                    for j in range(3):
                        last = nc.tensor.transpose(ps[:, BANK_T, j * TT:(j + 1) * TT], pick[:, j, :],
                                                   ident[0:TT, 0:TT])
                    last.then_inc(pt_mm, 1)

                pe.sem_inc(g_mm, CREDIT)
                pe.wait_ge(in_keys, 16)
                scores(0)
                pe.wait_ge(hl_ok, 1)
                matrix_and_ahead(0)
                turn(0)
                with pe.Fori(1, TILES) as i:
                    scores(i)
                    matrix_and_ahead(i)
                    turn(i)
                matrix_and_ahead(TILES)

            @block.scalar
            def _(act):
                tiles_of_qp = qp[:].rearrange("p j (i t) -> p i j t", t=TT)
                chunks = io["gates"].rearrange("g p (i c) a t -> i c p g (a t)", c=TT // CH)

                def inputs(i):
                    for m in range(4):
                        if isinstance(i, int):
                            src = tiles_of_qp[:, i]
                        else:
                            act.wait_ge(s_mm, i * 4 + (m - 3))
                            src = tiles_of_qp[:, bass.ds(i, 1)].rearrange("p i j t -> p (i j) t")
                        nc.scalar.activation(qt[:, 4 * m:4 * m + 4, :], src[:, 4 * m:4 * m + 4, :], ACT.Copy)\
                            .then_inc(qt_ok, 1)
                    if isinstance(i, int):
                        act.wait_ge(hl_ok, 1)
                    for m in range(4):
                        act.wait_ge(s_mm, i * 4 + (m + 1))
                        nc.scalar.activation(s[:, 4 * m:4 * m + 4, :], ps[0:TT, m % 2, :]
                                             .rearrange("p (j n) -> p j n", n=NK), ACT.Copy).then_inc(s_ok, 1)

                def high(m, r):
                    act.wait_ge(u_in[r % NU], m * (16 // NU) + (16 - 16 * (r % NU) // NU))
                    nc.scalar.activation(uh[:, r % 2], us[:, r % NU], ACT.Copy).then_inc(uh_ok, 1)

                def ahead(i, r):
                    act.wait_ge(u_mm, i * AB + (r + 1))
                    act.wait_ge(a_kept[r % 2], i * (8 * AB) + 16 * (r // 2) + 16)
                    nc.scalar.activation(halves(a[:, r % 2]), pair(u_pairs(r)), ACT.Gelu_apprx_tanh).then_inc(a_ok, 1)
                    high(i * AB + (r + 2), r)

                def store(i, c):
                    act.wait_ge(g_ok, i * BT + (-(-(c + 1) * CH // OH) - BT + CREDIT))
                    to = chunks[bass.ds(i - 1, 1), c] if not isinstance(i, int) else chunks[i - 1:i, c]
                    act.dma_start(to.rearrange("i p g a -> (i p) g a"),
                                  stage[:, c % 2].rearrange("p (g a) t -> p g (a t)", a=GB)).then_inc(kept[c % 2], 16)

                def copied(i, b):
                    act.wait_ge(g_mm, i * BT + (b + 1 - BT + CREDIT))
                    at, gates = b * OH, ps[:, BANK_G + b % 2, :].rearrange("p (t n) -> p t n", t=OH)
                    while at < (b + 1) * OH:
                        c = at // CH
                        upto = min((b + 1) * OH, (c + 1) * CH)
                        if at == c * CH:
                            act.wait_ge(kept[c % 2], i * 32 + (16 * (c // 2) - 16))
                        last = nc.scalar.activation(
                            stage[:, c % 2, :, at - c * CH:upto - c * CH].rearrange("p n t -> p t n"),
                            gates[:, at - b * OH:upto - b * OH, :], ACT.Copy)
                        at = upto
                    last.then_inc(g_ok, 1)

                def gated_and_ahead(i):
                    for b in range(BT):
                        if positive(i):
                            act.wait_ge(eq1_ok, i * BT + (b + 1 - BT))
                            for t in range(OH):
                                last = nc.scalar.activation(ga[:, b % 2, t, :], eq1[:, b % 2, t, :], ACT.Copy,
                                                            scale=pt[:, 2, b * OH + t:b * OH + t + 1])
                            last.then_inc(ga_ok, 1)
                            if b:
                                copied(i, b - 1)
                            for c in range(TT // CH):
                                if b - 2 == -(-(c + 1) * CH // OH) - 1:
                                    store(i, c)
                        for r in range(AB):
                            if BEHIND[r] + 1 == b:
                                ahead(i, r)
                    if positive(i):
                        copied(i, BT - 1)
                        store(i, TT // CH - 1)
                    for r in range(AB):
                        if BEHIND[r] + 1 == BT:
                            ahead(i, r)

                def softmax(i):
                    act.wait_ge(best_ok, i + 1)
                    nc.scalar.activation(ex[:], ex[:], ACT.Exp).then_inc(ex_ok, 1)
                    for r in range(AB - TAIL, AB):
                        ahead(i, r)
                    act.wait_ge(pt_mm, i + 1)
                    nc.scalar.activation(pt[:], ps[:, BANK_T, 0:3 * TT].rearrange("p (j t) -> p j t", j=3), ACT.Copy)\
                        .then_inc(pt_ok, 1)

                act.sem_inc(g_ok, CREDIT)
                for c in range(2):
                    act.sem_inc(kept[c], 16)
                nc.scalar.activation(hh[:], h[:], ACT.Copy).then_inc(hh_ok, 1)
                for r in range(2):
                    high(r, r)
                inputs(0)
                gated_and_ahead(0)
                softmax(0)
                with act.Fori(1, TILES) as i:
                    inputs(i)
                    gated_and_ahead(i)
                    softmax(i)
                gated_and_ahead(TILES)
                for r in range(AB - TAIL, AB):
                    ahead(TILES, r)
                for c in range(2):
                    act.wait_ge(kept[c], 32 * TILES + 16)

            @block.gpsimd
            def _(pool):
                with pool.Fori(1, TILES + 1) as i:
                    pool.wait_ge(pt_ok, i)
                    for b in range(BT):
                        pool.wait_ge(g_mm, i * BT + (b + 1 - BT))
                        nc.gpsimd.tensor_tensor(eq2[:, b % 2], iota.unsqueeze(1).to_broadcast([P, OH, P]),
                                                pt[:, 1, b * OH:(b + 1) * OH].unsqueeze(2).to_broadcast([P, OH, P]),
                                                ALU.subtract).then_inc(df2_ok, 1)
                        pool.wait_ge(df2_ok, i * BT + (b + 1 - BT))
                        pool.sem_inc(p_settled, 1)
                        nc.gpsimd.tensor_scalar(eq2[:, b % 2], eq2[:, b % 2], 0.0, None, ALU.is_equal).then_inc(eq2_ok, 1)

            @block.vector
            def _(dve):
                def low(m, r):
                    dve.wait_ge(uh_ok, m + 1)
                    nc.vector.tensor_tensor(ul[:, r % 2], us[:, r % NU], uh[:, r % 2].bitcast(F32), ALU.subtract)\
                        .then_inc(ul_ok, 1)

                def one_hot(i, b):
                    if b == 0:
                        dve.wait_ge(pt_ok, i)
                    dve.wait_ge(g_mm, i * BT + (b + 1 - BT))
                    nc.vector.tensor_tensor(eq1[:, b % 2], iota.unsqueeze(1).to_broadcast([P, OH, P]),
                                            pt[:, 0, b * OH:(b + 1) * OH].unsqueeze(2).to_broadcast([P, OH, P]),
                                            ALU.is_equal).then_inc(eq1_ok, 1)

                def batch(i, b):
                    if b < BT and positive(i):
                        one_hot(i, b)
                    for r in range(AB):
                        if BEHIND[r] + 2 == b:
                            low(i * AB + (r + 2), r)

                def choose(i):
                    done = [0]
                    calls = [0]
                    batches = [0]

                    def step(ins):
                        done[0] += 1
                        ins.then_inc(steps, 1)

                    def settle():
                        dve.wait_ge(steps, i * STEPS + done[0])
                        dve.sem_inc(settled, 1)

                    def between():
                        calls[0] += 1
                        if calls[0] % 4 == 0 and batches[0] < BT:
                            batch(i, batches[0])
                            batches[0] += 1

                    sets = range(2 * PH)
                    for j in sets:
                        if j % 4 == 0:
                            dve.wait_ge(s_ok, i * 4 + (j // 4 + 1))
                            dve.sem_inc(settled, 1)
                        last = nc.vector.max(top[:, j, 0:8], s[:, j, :])
                        if j == 2 * PH - 1:
                            step(last)
                        between()
                    settle()
                    for j in sets:
                        last = nc.vector.match_replace(s2[:, j, :], top[:, j, 0:8], s[:, j, :], LOWEST)
                        if j == 2 * PH - 1:
                            step(last)
                        between()
                    for j in sets:
                        nc.vector.max_index(topi[:, j, 0:8], top[:, j, 0:8], s[:, j, :])
                        between()
                    settle()
                    for j in sets:
                        last = nc.vector.max(top[:, j, 8:16], s2[:, j, :])
                        if j == 2 * PH - 1:
                            step(last)
                        between()
                    settle()
                    both = top[:].rearrange("p (h c) k -> p c h k", c=2)
                    r = 0
                    while r < TOPK:
                        n = ROW.count(ROW[r])
                        w = ROW[r]
                        last = nc.vector.tensor_tensor(
                            cand[:, :, AT[r]:AT[r] + n * w].rearrange("p h (a b) -> p h a b", b=w),
                            both[:, 0, :, r:r + n].unsqueeze(3).to_broadcast([TT, PH, n, w]),
                            both[:, 1, :, 0:w].unsqueeze(2).to_broadcast([TT, PH, n, w]), ALU.add)
                        r += n
                    step(last)
                    for j in sets:
                        last = nc.vector.max_index(topi[:, j, 8:16], top[:, j, 8:16], s2[:, j, :])
                        between()
                    step(last)
                    settle()
                    for j in range(PH):
                        last = nc.vector.max(best[:, j, 0:8], cand[:, j, :])
                        between()
                    step(last)
                    step(nc.vector.tensor_copy(topf[:], topi[:]))
                    settle()
                    for j in range(PH):
                        last = nc.vector.match_replace(cand2[:, j, :], best[:, j, 0:8], cand[:, j, :], LOWEST)
                        between()
                    step(last)
                    for j in range(PH):
                        nc.vector.max_index(pos[:, j, 0:8], best[:, j, 0:8], cand[:, j, :])
                        between()
                    settle()
                    for j in range(PH):
                        last = nc.vector.max(best[:, j, 8:16], cand2[:, j, :])
                        between()
                    step(last)
                    keys_at = topf[:].rearrange("p (h c) a -> p c h a", c=2)
                    nc.vector.tensor_copy(diff[:, :, 0:1], keys_at[:, 0, :, 0:1])
                    nc.vector.tensor_tensor(diff[:, :, 1:TOPK], keys_at[:, 0, :, 1:TOPK],
                                            keys_at[:, 0, :, 0:TOPK - 1], ALU.subtract)
                    settle()
                    for j in range(PH):
                        last = nc.vector.max_index(pos[:, j, 8:16], best[:, j, 8:16], cand2[:, j, :])
                        between()
                    step(last)
                    nc.vector.tensor_tensor(ex[:], best[:], best[:, :, 0:1].to_broadcast([TT, PH, TOPK]),
                                            ALU.subtract).then_inc(best_ok, 1)
                    settle()
                    step(nc.vector.tensor_copy(posf[:], pos[:].rearrange("p h k -> p (h k)")))
                    while batches[0] < BT + 2:
                        batch(i, batches[0])
                        batches[0] += 1
                    settle()
                    work = s2[:].rearrange("p j n -> p (j n)").rearrange("p (k a) -> p k a", a=TOPK)
                    work2 = s[:].rearrange("p j n -> p (j n)").rearrange("p (k a) -> p k a", a=TOPK)
                    by_head = lambda w: w.rearrange("p (h k) a -> p h k a", h=PH)
                    shape = [TT, PH, TOPK, TOPK]
                    nc.vector.tensor_scalar(over[:], posf[:], -float(AT[8]), 0.0, ALU.add, ALU.max)
                    step(nc.vector.tensor_tensor(work, posf[:].unsqueeze(2).to_broadcast([TT, HK, TOPK]),
                                                 starts.unsqueeze(1).to_broadcast([TT, HK, TOPK]), ALU.is_ge))
                    settle()
                    wide = work2[:, :, 0:8]
                    step(nc.vector.tensor_tensor(wide, work[:, :, 1:9],
                                                 widths.unsqueeze(1).to_broadcast([TT, HK, 8]), ALU.mult))
                    dve.wait_ge(steps, i * STEPS + done[0])
                    step(nc.vector.tensor_tensor(by_head(work), by_head(work),
                                                 diff[:].unsqueeze(2).to_broadcast(shape), ALU.mult))
                    step(nc.vector.tensor_reduce(start[:], wide, AX.X, ALU.add))
                    dve.wait_ge(steps, i * STEPS + (done[0] - 1))
                    step(nc.vector.tensor_reduce(pick[:, 0, :], work, AX.X, ALU.add))
                    dve.wait_ge(steps, i * STEPS + (done[0] - 1))
                    step(nc.vector.tensor_tensor(start[:], start[:], over[:], ALU.add))
                    settle()
                    step(nc.vector.tensor_tensor(posf[:], posf[:], start[:], ALU.subtract))
                    settle()
                    low(i * AB + (AB - TAIL + 2), AB - TAIL)
                    step(nc.vector.tensor_tensor(work, posf[:].unsqueeze(2).to_broadcast([TT, HK, TOPK]),
                                                 iota[0:TT, 0:TOPK].unsqueeze(1).to_broadcast([TT, HK, TOPK]),
                                                 ALU.is_equal))
                    dve.wait_ge(ex_ok, i + 1)
                    step(nc.vector.tensor_reduce(den[:], ex[:], AX.X, ALU.add))
                    settle()
                    step(nc.vector.tensor_tensor(by_head(work), by_head(work),
                                                 keys_at[:, 1].unsqueeze(2).to_broadcast(shape), ALU.mult))
                    step(nc.vector.reciprocal(den[:], den[:]))
                    settle()
                    nc.vector.tensor_tensor(pick[:, 2, :].rearrange("p (h k) -> p h k", h=PH), ex[:],
                                            den[:].unsqueeze(2).to_broadcast([TT, PH, TOPK]), ALU.mult)
                    nc.vector.tensor_reduce(pick[:, 1, :], work, AX.X, ALU.add).then_inc(pick_ok, 1)
                    for r in range(AB - TAIL + 1, AB):
                        low(i * AB + (r + 2), r)
                    assert done[0] == STEPS, done[0]

                dve.wait_ge(hh_ok, 1)
                nc.vector.tensor_tensor(hl[:], h[:], hh[:].bitcast(F32), ALU.subtract).then_inc(hl_ok, 1)
                for r in range(2):
                    low(r, r)
                choose(0)
                with dve.Fori(1, TILES) as i:
                    choose(i)
                for b in range(BT + 2):
                    batch(TILES, b)
                for r in range(AB - TAIL, AB):
                    low(TILES * AB + (r + 2), r)
                dve.wait_ge(ul_ok, AHEAD + 2)


def expert_stage(nc, sem, sb, pair, halves, residual, on_chip, u_side, io):
    x, h, mod, cst, gain, co, tsm, rs, ps = on_chip
    hh, hl, us, uh, ul, a, u_in, uh_ok, ul_ok, u_mm, a_ok = (
        u_side[n] for n in ("hh", "hl", "us", "uh", "ul", "a", "u_in", "uh_ok", "ul_ok", "u_mm", "a_ok"))
    ones = cst[:, 0, :]
    DH = D // 2
    KH = KD // 2
    stack = ExitStack()
    with stack:
        vs = sb(stack, "vblk", [P, 2, GB, DH])
        vh = sb(stack, "vh", [P, GB, D], F32R)
        vl = sb(stack, "vl", [P, GB, D], F32R)
        gt = sb(stack, "gt", [P, 2, NCH, GB, CH])
        aa = sb(stack, "aa", [P, GB, T])
        ch = sb(stack, "ch", [P, 2, GB, T], F32R)
        cl = sb(stack, "cl", [P, 2, GB, T], F32R)
        acc = h
        squares = gt[:].rearrange("p a c g t -> p (a c g t)").rearrange("p (k t) -> p k t", k=KD)

        v_in = [sem(f"v_in{n}") for n in range(2)]
        g_in = [sem(f"g_in{n}") for n in range(2)]
        aa_in = [sem(f"aa_in{n}") for n in range(GB)]
        c_ok = sem("c_ok")
        ch_ok = sem("ch_ok")
        cl_ok = sem("cl_ok")
        vh_ok = sem("vh_ok")
        vl_ok = sem("vl_ok")
        f_mm = sem("f_mm")
        f_ok = sem("f_ok")
        acc_ok = sem("acc_ok")
        fsq_ok, fss_mm, fms_ok, frt_ok = (sem(n) for n in ("fsq_ok", "fss_mm", "fms_ok", "frt_ok"))
        y_ok = sem("y_ok")
        y_out = sem("y_out")
        steps = sem("expert_dve")

        def groups(eng, step):
            step(0, 0)
            with eng.Fori(0, AGRP // 2 - 1) as i:
                step(i * 2 + 1, 1, ahead=True)
                step(i * 2 + 2, 0, ahead=True)
            step(AGRP - 1, 1)
            with eng.Fori(AGRP // 2, NGRP // 2 - 1) as i:
                step(i * 2, 0, ahead=False)
                step(i * 2 + 1, 1, ahead=False)
            step(NGRP - 2, 0)
            step(NGRP - 1, 1)
            step(NGRP, 0)

        def kind(g, ahead):
            if ahead is not None:
                return "ahead" if ahead else "make"
            return "ahead" if g < AGRP else "make" if g < NGRP else None

        with nc.Block() as block:

            @block.sync
            def _(sp):
                u_pairs_of = io["utab"].rearrange("(i j) p k e -> i j p k e", j=2 * GB)
                a_pairs_of = io["ahead"].rearrange("(i j) p t -> i j p t", j=2 * GB)
                v_pairs_of = io["vtab"].rearrange("p (i s j) (f d) -> i s f p j d", s=2, j=GB, f=2)
                g_pairs_of = io["gates"].rearrange("(i s) p c a t -> i s p c a t", s=2)

                def load_u(i, j, wait):
                    sp.wait_ge(ul_ok, wait)
                    sp.dma_start(us[:, j % NU], u_pairs_of[bass.ds(i, 1), j].rearrange("i p k e -> (i p) k e"))\
                        .then_inc(u_in[j % NU], 16)

                def load_a(i, j, wait):
                    if wait is not None:
                        sp.wait_ge(cl_ok, wait)
                    sp.dma_start(aa[:, j % GB], a_pairs_of[bass.ds(i, 1), j].rearrange("i p t -> (i p) t"))\
                        .then_inc(aa_in[j % GB], 16)

                def load_v(i, s, f, wait):
                    if wait is not None:
                        sp.wait_ge(vl_ok, wait)
                    sp.dma_start(vs[:, f], v_pairs_of[bass.ds(i, 1), s, f].rearrange("i p j d -> (i p) j d"))\
                        .then_inc(v_in[f], 16)

                def load_g(i, s, wait):
                    if wait is not None:
                        sp.wait_ge(c_ok, wait)
                    sp.dma_start(gt[:, s], g_pairs_of[bass.ds(i, 1), s].rearrange("i p c a t -> (i p) c a t"))\
                        .then_inc(g_in[s], 16)

                for s in range(2):
                    load_g(0, s, None)
                for j in range(GB):
                    load_a(0, j, None)
                for f in range(2):
                    load_v(0, 0, f, None)
                for j in range(GB):
                    load_a(0, GB + j, j + 1)
                for f in range(2):
                    load_v(0, 1, f, f + 1)
                with sp.Fori(1, AGRP // 2) as i:
                    for s in range(2):
                        load_g(i, s, i * (2 * GB) + (s - 1) * GB)
                        for j in range(GB):
                            load_a(i, GB * s + j, i * (2 * GB) + ((s - 1) * GB + j + 1))
                        for f in range(2):
                            load_v(i, s, f, i * 4 + (2 * (s - 1) + f + 1))
                first = AGRP // 2
                load_g(first, 0, (AGRP - 1) * GB)
                for f in range(2):
                    load_v(first, 0, f, 2 * (AGRP - 1) + f + 1)
                with sp.Fori(first, NGRP // 2 - 1) as i:
                    for s in range(2):
                        nxt, ns = (i, 1) if s == 0 else (i + 1, 0)
                        load_g(nxt, ns, i * (2 * GB) + s * GB)
                        for j in range(GB):
                            n = GB * s + j + NU
                            load_u(*((i, n) if n < 2 * GB else (i + 1, n - 2 * GB)),
                                   i * (2 * GB) + (GB * s + j + 1))
                        for f in range(2):
                            load_v(nxt, ns, f, i * 4 + (2 * s + f + 1))
                final = NGRP // 2 - 1
                load_g(final, 1, final * 2 * GB)
                for n in range(NU, 2 * GB):
                    load_u(final, n, final * 2 * GB + n - NU + 1)
                    if n == NU + GB - 1:
                        for f in range(2):
                            load_v(final, 1, f, final * 4 + f + 1)
                sp.wait_ge(y_ok, 1)
                sp.dma_start(io["yT"], x[:]).then_inc(y_out, 16)
                sp.wait_ge(y_out, 16)

            @block.tensor
            def _(pe):
                def step(g, parity, ahead=None):
                    if kind(g, ahead) == "make":
                        for j in range(GB):
                            n = g * GB + j
                            pe.wait_ge(ul_ok, n + 1)
                            pe.wait_ge(a_ok, n - 1)
                            for k in range(KD):
                                last = u_product(nc, pair(u_pairs(j)), uh[:, j % 2], ul[:, j % 2], hh, hl, k)
                            last.then_inc(u_mm, 1)
                    if positive(g):
                        pe.wait_ge(cl_ok, g * GB)
                        for k in range(KD):
                            if k % KH == 0:
                                pe.wait_ge(vl_ok, g * 2 + (k // KH - 1))
                            pe.wait_ge(f_ok, g * KD + (k + 1 - KD))
                            out = pair(3 * (k % 2))
                            for j in range(GB):
                                hi, lo = vh[:, j, k * P:(k + 1) * P], vl[:, j, k * P:(k + 1) * P]
                                c_hi, c_lo = ch[:, 1 - parity, j, :], cl[:, 1 - parity, j, :]
                                for n, (w, m) in enumerate(((hi, c_lo), (hi, c_hi), (lo, c_hi))):
                                    for half in range(2):
                                        last = nc.tensor.matmul(out[:, half, :], w, m[:, half * TH:(half + 1) * TH],
                                                                start=(j == 0 and n == 0),
                                                                stop=(j == GB - 1 and n == 2))
                            last.then_inc(f_mm, 1)

                pe.sem_inc(f_mm, KD)
                groups(pe, step)
                pe.wait_ge(fsq_ok, 1)
                for k in range(KD):
                    for half in range(2):
                        last = nc.tensor.matmul(ps[:, half, 0:TH], ones, squares[:, k, half * TH:(half + 1) * TH],
                                                start=(k == 0), stop=(k == KD - 1))
                last.then_inc(fss_mm, 1)

            @block.scalar
            def _(act):
                def high_v(g, f):
                    act.wait_ge(v_in[f], g * 16 + 16)
                    act.wait_ge(f_mm, g * KD + (f + 1) * KH)
                    nc.scalar.activation(vh[:, :, f * DH:(f + 1) * DH], vs[:, f], ACT.Copy).then_inc(vh_ok, 1)

                def step(g, parity, ahead=None):
                    what = kind(g, ahead)
                    for j in range(GB) if what else ():
                        n = g * GB + j
                        src = aa[:, j] if what == "ahead" else a[:, j % 2]
                        if what == "make":
                            act.wait_ge(u_mm, n + 1)
                            if not (isinstance(g, int) and g == AGRP and j < 2):
                                act.wait_ge(cl_ok, n - 1)
                            nc.scalar.activation(halves(a[:, j % 2]), pair(u_pairs(j)), ACT.Gelu_apprx_tanh)\
                                .then_inc(a_ok, 1)
                            if not (isinstance(g, int) and g == NGRP - 1 and j + 2 >= GB):
                                act.wait_ge(u_in[j % NU], n * (16 // NU) + (16 + 16 - 16 * (j % NU) // NU))
                                nc.scalar.activation(uh[:, j % 2], us[:, j % NU], ACT.Copy).then_inc(uh_ok, 1)
                        act.wait_ge(c_ok, n + 1)
                        if positive(g):
                            act.wait_ge(f_mm, g * KD)
                        nc.scalar.activation(ch[:, parity, j], src, ACT.Copy).then_inc(ch_ok, 1)
                    if what and positive(g):
                        for f in range(2):
                            high_v(g, f)

                for f in range(2):
                    high_v(0, f)
                groups(act, step)
                act.wait_ge(acc_ok, 2)
                nc.scalar.activation(squares, acc[:], ACT.Square).then_inc(fsq_ok, 1)
                act.wait_ge(fms_ok, 1)
                nc.scalar.activation(rs[:], rs[:], ACT.Sqrt).then_inc(frt_ok, 1)
                act.wait_ge(frt_ok, 1)

            @block.vector
            def _(dve):
                done = [0]

                def link(ins):
                    done[0] += 1
                    ins.then_inc(steps, 1)
                    dve.wait_ge(steps, done[0])

                def low(out, full, high):
                    return nc.vector.tensor_tensor(out, full, high.bitcast(F32), ALU.subtract)

                def low_v(g, f):
                    dve.wait_ge(vh_ok, g * 2 + (f + 1))
                    cols = slice(f * DH, (f + 1) * DH)
                    low(vl[:, :, cols], vs[:, f], vh[:, :, cols]).then_inc(vl_ok, 1)

                def by_chunk(ap):
                    return ap.rearrange("p (c t) -> p c t", t=CH)

                def step(g, parity, ahead=None):
                    what = kind(g, ahead)
                    for j in range(GB) if what else ():
                        n = g * GB + j
                        src = aa[:, j] if what == "ahead" else a[:, j % 2]
                        if what == "make":
                            dve.wait_ge(a_ok, n + 1)
                        else:
                            dve.wait_ge(aa_in[j], g * 16 + 16)
                        if j == 0:
                            dve.wait_ge(g_in[parity], g * 8 + (16 - 8 * parity))
                        nc.vector.tensor_tensor(by_chunk(src), by_chunk(src), gt[:, parity, :, j, :],
                                                ALU.mult).then_inc(c_ok, 1)
                        if what == "make" and not (isinstance(g, int) and g == NGRP - 1 and j + 2 >= GB):
                            dve.wait_ge(uh_ok, n + 3)
                            low(ul[:, j % 2], us[:, j % NU], uh[:, j % 2]).then_inc(ul_ok, 1)
                        dve.wait_ge(ch_ok, n + 1)
                        low(cl[:, parity, j], src, ch[:, parity, j]).then_inc(cl_ok, 1)
                    if positive(g):
                        for k in range(KD):
                            dve.wait_ge(f_mm, g * KD + (k + 1))
                            nc.vector.tensor_tensor(halves(acc[:, k]), pair(3 * (k % 2)), halves(acc[:, k]), ALU.add)\
                                .then_inc(f_ok, 1)
                            if what and k == KH:
                                low_v(g, 0)
                        if what:
                            low_v(g, 1)

                dve.sem_inc(f_ok, 2)
                nc.vector.memset(acc[:], 0.0).then_inc(acc_ok, 1)
                for f in range(2):
                    low_v(0, f)
                groups(dve, step)
                dve.wait_ge(f_ok, NGRP * KD + 2)
                dve.sem_inc(acc_ok, 1)
                dve.wait_ge(fss_mm, 1)
                nc.vector.tensor_scalar(halves(rs[:]), pair(0), 1.0 / D, EPS, ALU.mult, ALU.add).then_inc(fms_ok, 1)
                dve.wait_ge(frt_ok, 1)
                link(nc.vector.reciprocal(rs[:], rs[:]))
                residual(dve, link, acc, 3).then_inc(y_ok, 1)


def kernel(**inputs):
    from concourse import bacc
    from concourse.bass_utils import run_bass_kernel_spmd

    f32 = np.float32
    a = {k: np.asarray(v) for k, v in inputs.items()}
    laid = {}

    def rows_to_partitions(m):
        return np.ascontiguousarray(m.reshape(-1, P, m.shape[-1]).transpose(1, 0, 2))

    def columns(w):
        return np.ascontiguousarray(w.reshape(KD, P, -1, WC).transpose(2, 1, 0, 3))

    tokens = np.concatenate([a["x_prompt"][0], a["x_sample"][:, 0]])
    laid["xT"] = rows_to_partitions(tokens.T)
    laid["cT"] = rows_to_partitions(np.concatenate([a["c_prompt"], a["c_sample"]]).T)
    laid["w_ada"] = columns(a["w_ada"][0])
    laid["b_ada"] = np.ascontiguousarray(a["b_ada"][0].reshape(-1, P).T)
    laid["gains"] = np.ascontiguousarray(
        np.stack([a[n][0].reshape(KD, P) for n in ("g_pre1", "g_post1", "g_pre2", "g_post2")]).transpose(2, 0, 1))
    laid["w_in"] = columns(a["w_in"][0])
    laid["w_out"] = columns(a["w_out"][0])
    laid["w_q"] = columns(a["w_q"][0])
    laid["keysT"] = np.ascontiguousarray(a["sub_keys"][0].reshape(2 * PH, NK, P).transpose(2, 0, 1))
    laid["utab"] = np.ascontiguousarray(a["u_tab"][0].reshape(NK, NK, KD, P).transpose(1, 3, 2, 0))
    laid["vtab"] = np.ascontiguousarray(a["v_tab"][0].reshape(NK, NK, D))
    laid["s0"] = np.ascontiguousarray(a["state_ret"][0].transpose(2, 0, 1, 3))
    laid["conv_s"] = np.ascontiguousarray(a["cache_conv"][0].reshape(NS, CK - 1, RH, P).transpose(3, 2, 1, 0))
    laid["conv_w"] = np.ascontiguousarray(
        np.concatenate([a["conv_w"][0], a["conv_b"]]).reshape(CK + 1, RH, P).transpose(2, 1, 0))

    half = P // 2
    freqs = (f32(10000.0) ** (-np.arange(half, dtype=f32) / half)).astype(f32)
    where = np.concatenate([np.arange(SEQ), np.full(NS, PAST)]).astype(f32)
    angle = (freqs[:, None] * where[None, :]).astype(f32).astype(np.float64)
    cos = np.concatenate([np.cos(angle)] * 2)
    sin = np.concatenate([np.sin(angle), -np.sin(angle)])
    laid["trig"] = np.ascontiguousarray(
        np.stack([cos, sin, cos * P ** -0.5, sin * P ** -0.5]).transpose(1, 0, 2).astype(f32))
    gamma = 1.0 - 2.0 ** (-5.0 - np.arange(RH))
    rel = np.arange(SEQ)[None, :] - np.arange(P)[:, None]
    laid["decay"] = np.where(rel >= 0, gamma[:, None, None] ** np.maximum(rel, 0), 0.0).astype(f32)
    age = SEQ - 1 - np.arange(SEQ).reshape(CHUNKS, P)
    laid["kdecay"] = np.ascontiguousarray((gamma[:, None, None] ** age).transpose(2, 0, 1).astype(f32))
    width = [TOPK // (r + 1) for r in range(TOPK)]
    rows = np.zeros((P, P))
    rows[:, :TOPK] = np.cumsum([0] + width[:-1])
    rows[:, TOPK:TOPK + 8] = width[:8]
    laid["consts"] = np.ascontiguousarray(np.stack(
        [np.ones((P, P)), np.eye(P), np.tile(np.arange(P), (P, 1)), rows]).transpose(1, 0, 2).astype(f32))
    laid["starts"] = np.repeat(np.eye(NS, dtype=f32)[:, :, None], P, 2)

    nc = bacc.Bacc("TRN2", target_bir_lowering=False, num_devices=1)
    args = {k: nc.dram_tensor(k, v.shape, F32, kind="ExternalInput").ap() for k, v in laid.items()}
    outs = {"yT": (P, KD, T), "ret_p": (P, RH, P), "conv_p": (P, RH, CK - 1), "ret_s": (P, NS, RH, P),
            "conv_so": (P, RH, CK - 1, NS)}
    args |= {k: nc.dram_tensor(k, v, F32, kind="ExternalOutput").ap() for k, v in outs.items()}
    args["gates_dram"] = nc.dram_tensor("gates_dram", (NGRP, P, NCH, GB, CH), F32, kind="Internal").ap()
    args["ahead_dram"] = nc.dram_tensor("ahead_dram", (AHEAD, P, T), F32, kind="Internal").ap()
    build(nc, **args)
    r = run_bass_kernel_spmd(nc, [laid], core_ids=[0]).results[0]

    y = r["yT"].transpose(2, 1, 0).reshape(T, D)
    return (y[None, :SEQ], y[SEQ:, None, :],
            r["ret_p"].transpose(1, 0, 2)[None, None],
            r["conv_p"].transpose(2, 1, 0).reshape(1, 1, CK - 1, RH * P),
            r["ret_s"].transpose(1, 2, 0, 3)[None],
            r["conv_so"].transpose(3, 2, 1, 0).reshape(1, NS, CK - 1, RH * P))
```

```python
from contextlib import ExitStack

import numpy as np
import concourse.bass as bass
from concourse import mybir

F32 = mybir.dt.float32
F32R = mybir.dt.float32r
U32 = mybir.dt.uint32
ALU = mybir.AluOpType
ACT = mybir.ActivationFunctionType
AX = mybir.AxisListType

P = 128
D = 1024
KD = D // P
SEQ = 512
NS = 8
T = SEQ + NS
TH = T // 2
RH = 4
CHUNKS = SEQ // P
CK = 3
PAST = 4096
EPS = 1e-6
WC = 256
WB = WC // P
NSLOT = 3
PH = 8
NK = 128
TOPK = 16
HK = PH * TOPK
TT = 104
TILES = T // TT
CH = 26
TCH = TT // CH
NCH = T // CH
OH = 4
GB = 4
NGRP = NK // GB
AB = 12
AHEAD = AB * (TILES + 1)
AGRP = AHEAD // GB
NU = 2
NA = 3
LOWEST = -3.0e38

ADA, WIN, WOUT, WQ = "ada", "in", "out", "q"
ADA_AT = [part * KD // WB for part in (0, 2, 5, 6)]


def weight_loads():
    order = [(ADA, n) for n in range(ADA_AT[1])]
    for group in (0, 1, 2, 3, 5, 6, 4):
        order += [(WIN, group * 2 + n) for n in range(2)]
    order += [(ADA, n) for n in range(ADA_AT[1], ADA_AT[2])]
    order += [(WOUT, n) for n in range(D // WC)]
    order += [(ADA, n) for n in range(ADA_AT[2], ADA_AT[3])]
    order += [(WQ, n) for n in range(2 * PH * P // WC)]
    return order


def build(nc, xT, cT, w_ada, b_ada, gains, w_in, w_out, w_q, keysT, utab, vtab, s0, conv_s, conv_w,
          trig, decay, kdecay, consts, starts,
          yT, ret_p, conv_p, ret_s, conv_so, gates_dram, ahead_dram):
    outer = ExitStack()
    with outer:
        def sb(stack, name, shape, dt=F32, side="left"):
            return stack.enter_context(nc.sbuf_tensor(name, shape, dt, side=side))

        def sem(name):
            return outer.enter_context(nc.semaphore(name))

        x = sb(outer, "x", [P, KD, T])
        h = sb(outer, "h", [P, KD, T])
        mod = sb(outer, "mod", [P, 6 * KD, 1 + NS])
        cst = sb(outer, "cst", [P, 4, P])
        gain = sb(outer, "gain", [P, 4, KD])
        co = sb(outer, "co", [P, 4, KD, 1 + NS])
        tsm = sb(outer, "tsm", [P, KD, NS])
        rs = sb(outer, "rs", [P, T])
        ones, ident, iota = cst[:, 0, :], cst[:, 1, :], cst[:, 2, :]
        ps = outer.enter_context(nc.psum_tensor("ps", [P, 8, 512], F32))

        def pair(n):
            return ps[:, 2 * n:2 * n + 2, 0:TH]

        def halves(ap):
            return ap.rearrange("p (a b) -> p a b", a=2)

        def residual(note, await_step, m, slot, x_ok):
            rs_of_samples = rs[:, SEQ:T].unsqueeze(1).to_broadcast([P, KD, NS])
            await_step(note(nc.vector.tensor_tensor(tsm[:], m[:, :, SEQ:T], rs_of_samples, ALU.mult)))
            await_step(note(nc.vector.tensor_tensor(tsm[:], tsm[:], co[:, slot, :, 1:1 + NS], ALU.mult)))
            nc.vector.tensor_tensor(x[:, :, SEQ:T], x[:, :, SEQ:T], tsm[:], ALU.add)
            scaled = []
            for k in range(KD + 1):
                if k < KD:
                    scaled.append(note(nc.vector.tensor_tensor(m[:, k, 0:SEQ], m[:, k, 0:SEQ], rs[:, 0:SEQ],
                                                               ALU.mult)))
                if k:
                    await_step(scaled[k - 1])
                    nc.vector.scalar_tensor_tensor(
                        x[:, k - 1, 0:SEQ], m[:, k - 1, 0:SEQ], co[:, slot, k - 1, 0:1], x[:, k - 1, 0:SEQ],
                        ALU.mult, ALU.add).then_inc(x_ok, 1)

        hh = sb(outer, "hh", [P, KD, T], F32R, "right")
        hl = sb(outer, "hl", [P, KD, T], F32R, "right")
        upto_gates = ExitStack()
        qp = sb(upto_gates, "qp", [P, 2 * PH, T])
        io = dict(xT=xT, cT=cT, b_ada=b_ada, gains=gains, keysT=keysT, utab=utab, vtab=vtab, s0=s0,
                  conv_s=conv_s, conv_w=conv_w, trig=trig, decay=decay, kdecay=kdecay, consts=consts,
                  starts=starts, yT=yT, ret_p=ret_p, conv_p=conv_p, ret_s=ret_s, conv_so=conv_so,
                  gates=gates_dram)
        on_chip = (x, h, mod, cst, gain, co, tsm, rs, ps)
        mixer_stage(nc, sem, sb, pair, halves, residual, on_chip, hh, hl, qp, io,
                    {ADA: w_ada, WIN: w_in, WOUT: w_out, WQ: w_q})
        io["ahead"] = ahead_dram
        u_side = dict(
            hh=hh, hl=hl,
            us=sb(outer, "us", [P, NU, KD, P], F32, "right"),
            uh=sb(outer, "uh", [P, 2, KD, P], F32R, "right"), ul=sb(outer, "ul", [P, 2, KD, P], F32R, "right"),
            a=sb(outer, "a", [P, NA, T], F32, "right"),
            u_in=[sem(f"u_in{n}") for n in range(NU)],
            uh_ok=sem("uh_ok"),
            ul_ok=sem("ul_ok"),
            u_mm=sem("u_mm"),
            a_ok=sem("a_ok"))
        gate_stage(nc, sem, sb, pair, halves, on_chip, qp, u_side, io)
        upto_gates.close()
        expert_stage(nc, sem, sb, pair, halves, residual, on_chip, u_side, io)


def u_pairs(i):
    return 1 + i % 2


def u_product(nc, out, uh, ul, hh, hl, k):
    for n, (w, m) in enumerate(((uh, hl), (uh, hh), (ul, hh))):
        for half in range(2):
            last = nc.tensor.matmul(out[:, half, :], w[:, k, :], m[:, k, half * TH:(half + 1) * TH],
                                    start=(k == 0 and n == 0), stop=(k == KD - 1 and n == 2))
    return last


def positive(value):
    return not isinstance(value, int) or value > 0


def mixer_stage(nc, sem, sb, pair, halves, residual, on_chip, hh, hl, qp, io, w_dram):
    x, h, mod, cst, gain, co, tsm, rs, ps = on_chip
    ones, ident = cst[:, 0, :], cst[:, 1, :]
    stack = ExitStack()
    with stack:
        wr = sb(stack, "wr", [P, NSLOT, KD, WC])
        wh = sb(stack, "wh", [P, 2, KD, WC], F32R)
        wl = sb(stack, "wl", [P, 2, KD, WC], F32R)
        scr = qp[:, 0:KD, :]
        qk = qp[:, KD:2 * KD, :].rearrange("p (a h) t -> p a h t", a=2)
        mix = h
        vt = sb(stack, "vt", [P, CHUNKS, RH * P])
        vs = sb(stack, "vs", [P, RH * P])
        ext = sb(stack, "ext", [P, RH, CK - 1 + SEQ])
        exs = sb(stack, "exs", [P, RH, CK, NS])
        tg = sb(stack, "tg", [P, 4, T])
        dec = sb(stack, "dec", [P, 2, SEQ])
        kde = sb(stack, "kde", [P, RH, CHUNKS])
        pr = sb(stack, "pr", [P, CHUNKS, SEQ])
        kd = sb(stack, "kd", [P, CHUNKS, P])
        so = sb(stack, "so", [P, RH, P])
        t1, t2 = (pr[:].rearrange("p c t -> p (c t)")[:, n * T:(n + 1) * T] for n in range(2))
        cs = sb(stack, "cs", [P, KD, 1 + NS])
        rows = sb(stack, "rows", [1 + NS, 2, WC])
        bad = sb(stack, "bad", [P, 6 * KD])
        cw = sb(stack, "cw", [P, RH, CK + 1])
        sel = tg[:].rearrange("p a t -> p (a t)")[:, 0:NS * P].rearrange("p (b m) -> p b m", b=NS)
        state = scr.rearrange("p a b -> p (a b)")[:, 0:NS * RH * P]\
            .rearrange("p (b h e) -> p b h e", b=NS, h=RH)

        w_slot = [sem(f"w_slot{n}") for n in range(NSLOT)]
        in_x, in_c, in_cst, in_trig, in_state, in_misc, in_sel = (
            sem(n) for n in ("in_x", "in_c", "in_cst", "in_trig", "in_state", "in_misc", "in_sel"))
        in_dec = [sem(f"in_dec{hd}") for hd in range(RH)]
        stored = sem("mixer_stored")
        silu_c = sem("silu_c")
        mod_mm = sem("mod_mm")
        row_ok = sem("row_ok")
        turn_mm = sem("turn_mm")
        mod_ok = sem("mod_ok")
        wh_ok = sem("wh_ok")
        wl_ok = sem("wl_ok")
        sq_ok = sem("sq_ok")
        ss_mm = sem("ss_mm")
        ms_ok = sem("ms_ok")
        rt_ok = sem("rt_ok")
        hk_ok = sem("hk_ok")
        hh_ok = sem("hh_ok")
        hl_ok = sem("hl_ok")
        hc_ok = sem("hc_ok")
        hd_ok = sem("hd_ok")
        proj_mm = sem("proj_mm")
        rot_mul = sem("rot_mul")
        rot_ok = sem("rot_ok")
        v_mm = sem("v_mm")
        v_ok = sem("v_ok")
        g_ok = sem("g_ok")
        cg_ok = sem("cg_ok")
        zero_ok = sem("zero_ok")
        u_ok = sem("u_ok")
        conv_ok = sem("conv_ok")
        sc_mm = sem("sc_mm")
        pr_ok = sem("pr_ok")
        kt_mm = sem("kt_mm")
        kd_ok = sem("kd_ok")
        st_mm = sem("st_mm")
        st_ok = sem("st_ok")
        s0_ok = sem("s0_ok")
        vb_mm = sem("vb_mm")
        sn_ok = sem("sn_ok")
        o_mm = sem("o_mm")
        o_ok = sem("o_ok")
        mu_mm = sem("mu_mm")
        oc_ok = sem("oc_ok")
        oq_ok = sem("oq_ok")
        va_mm = sem("va_mm")
        ve_ok = sem("ve_ok")
        sd_ok = sem("sd_ok")
        ret_ok = sem("ret_ok")
        m_ok = sem("m_ok")
        x1_ok = sem("x1_ok")
        qp_ok = sem("qp_ok")
        steps = sem("mixer_dve")

        Q0, K0, G0, C0, X0, B0, M0 = (RH * n for n in range(7))
        Q2 = M0 + KD
        RING = 3
        SUMS = 3

        def read_of(m):
            for start, s in ((Q2, qp_ok), (M0, m_ok), (B0, conv_ok), (X0, u_ok), (C0, cg_ok), (G0, g_ok),
                             (Q0, rot_mul)):
                if m >= start:
                    return s, m - start + 1

        order = weight_loads()
        split, used, n_v, n_blocks = [], [], 0, 0
        for n, (kind, at) in enumerate(order):
            if kind == ADA:
                continue
            split.append(n)
            if kind == WIN and at // 2 == 2:
                n_v += 1
                used.append((v_mm, n_v))
            else:
                n_blocks += WB
                used.append((proj_mm, n_blocks))
        V_AT, OUT_AT, Q_AT = 4, 14, 14 + D // WC
        MIXED = 1 + KD
        SECOND = MIXED + RH
        ROWS_1, ROWS_2, ROWS_3 = ADA_AT[1:]
        ADA_BANKS = (((0, 1), 2, 0), ((7,), 7, WC), ((0,), 2, 0))

        def ada_part(n):
            return 0 if n < ROWS_1 else 1 if n < ROWS_2 else 2

        with nc.Block() as block:

            @block.sync
            def _(sp):
                sp.dma_start(cs[:], io["cT"]).then_inc(in_c, 16)

                def load(n):
                    kind, at = order[n]
                    if n >= NSLOT:
                        last = n - NSLOT
                        if last in split:
                            sp.wait_ge(wl_ok, split.index(last) + 1)
                        else:
                            sp.wait_ge(mod_mm, [m for m in range(last + 1) if m not in split].index(last) + 1)
                    sp.dma_start(wr[:, n % NSLOT], w_dram[kind][at]).then_inc(w_slot[n % NSLOT], 16)

                load(0)
                sp.dma_start(x[:], io["xT"]).then_inc(in_x, 16)
                sp.dma_start(cst[:], io["consts"]).then_inc(in_cst, 16)
                for n in range(1, NSLOT):
                    load(n)
                for dst, name in ((bad[:], "b_ada"), (gain[:], "gains"), (cw[:], "conv_w"),
                                  (exs[:, :, 0:CK - 1, :], "conv_s"), (kde[:], "kdecay")):
                    sp.dma_start(dst, io[name]).then_inc(in_misc, 16)
                for n in range(NSLOT, len(order)):
                    load(n)
                    if n == ROWS_1 + 2:
                        sp.dma_start(tg[:], io["trig"]).then_inc(in_trig, 16)
                    if n == ROWS_1 + 6:
                        for hd in range(2):
                            sp.dma_start(dec[:, hd, :], io["decay"][hd]).then_inc(in_dec[hd], 16)
                        sp.dma_start(state, io["s0"]).then_inc(in_state, 16)
                    if n == ROWS_1 + 14:
                        sp.wait_ge(rot_mul, 2 * RH)
                        sp.dma_start(sel, io["starts"]).then_inc(in_sel, 16)

            @block.tensor
            def _(pe):
                done = [0]
                halved = [0]
                made = [0]
                ada = [0, 0]

                def weights():
                    n = done[0]
                    done[0] += 1
                    pe.wait_ge(w_slot[n % NSLOT], 16 * (n // NSLOT + 1))
                    return n % NSLOT

                def parts():
                    done[0] += 1
                    i = halved[0]
                    halved[0] += 1
                    pe.wait_ge(wl_ok, i + 1)
                    return i % 2

                def ada_product():
                    n = ada[0]
                    ada[0] += 1
                    banks = ADA_BANKS[ada_part(n)][0]
                    s = weights()
                    for k in range(KD):
                        last = nc.tensor.matmul(ps[0:1 + NS, banks[n % len(banks)], 0:WC], cs[:, k, :], wr[:, s, k, :],
                                                start=(k == 0), stop=(k == KD - 1))
                    last.then_inc(mod_mm, 1)

                def ada_turn():
                    n = ada[1]
                    ada[1] += 1
                    part = ada_part(n)
                    bank, col = ADA_BANKS[part][1:]
                    pe.wait_ge(row_ok, n + 1)
                    for b in range(WB):
                        at = col + ((n - ADA_AT[part]) * WB + b) * (1 + NS)
                        last = nc.tensor.transpose(ps[:, bank, at:at + 1 + NS], rows[:, n % 2, b * P:(b + 1) * P],
                                                   ident[0:1 + NS, 0:1 + NS])
                    if n + 1 in ADA_AT:
                        last.then_inc(turn_mm, 1)

                def ada_step(first=False):
                    if not first:
                        ada_turn()
                    ada_product()

                def norm_sums(k, ready, count):
                    pe.wait_ge(ready, count)
                    for a in range(2):
                        last = nc.tensor.matmul(pair(SUMS)[:, a, :], ones, mix[:, k, a * TH:(a + 1) * TH],
                                                start=(k == 0), stop=(k == KD - 1))
                    if k == KD - 1:
                        last.then_inc(ss_mm, 1)

                def blocks(n_loads, each_k=None, turns=range(KD), behind=None):
                    for n in range(n_loads):
                        s = parts()
                        for b in range(WB):
                            m = made[0]
                            if m >= RING:
                                pe.wait_ge(*read_of(m - RING))
                            out = pair(m % RING)
                            for at, k in enumerate(turns):
                                if each_k and n == b == 0:
                                    pe.wait_ge(*each_k(k))
                                hi, lo = (w[:, s, k, b * P:(b + 1) * P] for w in (wh, wl))
                                for q, (w, r) in enumerate(((hi, hl), (hi, hh), (lo, hh))):
                                    for a in range(2):
                                        last = nc.tensor.matmul(out[:, a, :], w, r[:, k, a * TH:(a + 1) * TH],
                                                                start=(at == 0 and q == 0),
                                                                stop=(at == KD - 1 and q == 2))
                            last.then_inc(proj_mm, 1)
                            made[0] += 1
                            if behind:
                                behind(n * WB + b)

                def all_read():
                    for m in range(max(0, made[0] - RING), made[0]):
                        pe.wait_ge(*read_of(m))

                pe.wait_ge(silu_c, 1)
                for n in range(ROWS_1):
                    ada_product()
                    if n == 0:
                        pe.wait_ge(in_cst, 16)
                    else:
                        ada_turn()
                    if n == 3:
                        for k in range(KD):
                            norm_sums(k, sq_ok, 1)
                ada_turn()
                pe.wait_ge(mod_ok, 1)
                blocks(4, lambda k: (hl_ok, k + 2))
                all_read()
                for half in range(2):
                    s = parts()
                    for c in range(CHUNKS + 1):
                        first = min(c * P, T - P)
                        for k in range(KD):
                            hi, lo = (r[:, k, first:first + P] for r in (hh, hl))
                            for q, (w, r) in enumerate(((hi, wl), (hi, wh), (lo, wh))):
                                last = nc.tensor.matmul(ps[:, c, half * WC:(half + 1) * WC], w, r[:, s, k, :],
                                                        start=(k == 0 and q == 0), stop=(k == KD - 1 and q == 2))
                    last.then_inc(v_mm, 1)
                pe.wait_ge(v_ok, 2)
                blocks(8)

                pe.wait_ge(rot_ok, 2 * RH)
                all_read()
                for hd in range(RH):
                    q, k = qk[:, 0, hd, :], qk[:, 1, hd, :]
                    for c in range(CHUNKS):
                        if hd:
                            pe.wait_ge(pr_ok, CHUNKS * (hd - 1) + c + 1)
                        nc.tensor.matmul(ps[:, c, 0:SEQ - c * P], k[:, c * P:(c + 1) * P], q[:, c * P:SEQ],
                                         start=True, stop=True).then_inc(sc_mm, 1)
                    if hd:
                        pe.wait_ge(kd_ok, CHUNKS * hd)
                    for c in range(CHUNKS):
                        last = nc.tensor.transpose(ps[:, 4, c * P:(c + 1) * P], k[:, c * P:(c + 1) * P], ident)
                    last.then_inc(kt_mm, 1)
                    ada_step(first=(hd == 0))
                    if hd:
                        pe.wait_ge(o_ok, hd)
                    for c in range(CHUNKS):
                        pe.wait_ge(pr_ok, CHUNKS * hd + c + 1)
                        last = nc.tensor.matmul(ps[:, 5, c * P:SEQ], vt[:, c, hd * P:(hd + 1) * P],
                                                pr[:, c, 0:SEQ - c * P], start=(c == 0), stop=(c == CHUNKS - 1))
                    last.then_inc(o_mm, 1)
                    pe.wait_ge(kd_ok, CHUNKS * (hd + 1))
                    if hd:
                        pe.wait_ge(st_ok, hd)
                    for c in range(CHUNKS):
                        last = nc.tensor.matmul(ps[:, 6, 0:P], kd[:, c, :], vt[:, c, hd * P:(hd + 1) * P],
                                                start=(c == 0), stop=(c == CHUNKS - 1))
                    last.then_inc(st_mm, 1)
                    ada_step()
                pe.wait_ge(in_sel, 16)
                for b in range(NS):
                    if b >= 2:
                        pe.wait_ge(sn_ok, b - 1)
                    nc.tensor.matmul(ps[:, b % 2, :], sel[:, b, :], vs[:], start=True, stop=True)\
                        .then_inc(vb_mm, 1)
                    if b == 3:
                        ada_step()
                pe.wait_ge(sn_ok, NS)
                for hd in range(RH):
                    for b in range(NS):
                        last = nc.tensor.matmul(ps[:, 2, hd * NS + b:hd * NS + b + 1], state[:, b, hd, :],
                                                qk[:, 0, hd, SEQ + b:SEQ + b + 1], start=True, stop=True)
                last.then_inc(o_mm, 1)
                pe.wait_ge(o_ok, RH + 1)
                for hd in range(RH):
                    o = qk[:, 1, hd, :]
                    if hd:
                        pe.wait_ge(oc_ok, hd)
                    for a in range(2):
                        last = nc.tensor.matmul(ps[:, a, 0:TH], ones, o[:, a * TH:(a + 1) * TH],
                                                start=True, stop=True)
                    last.then_inc(mu_mm, 1)
                    pe.wait_ge(oq_ok, hd + 1)
                    if hd:
                        pe.wait_ge(ve_ok, hd)
                    for a in range(2):
                        last = nc.tensor.matmul(ps[:, 2 + a, 0:TH], ones, t1[:, a * TH:(a + 1) * TH],
                                                start=True, stop=True)
                    last.then_inc(va_mm, 1)
                    if hd < RH - 1:
                        ada_step()
                ada_turn()
                pe.wait_ge(st_ok, RH)
                pe.wait_ge(ve_ok, RH)
                pe.wait_ge(hd_ok, 1)
                pe.wait_ge(mod_ok, 2)

                def behind(b):
                    if b:
                        norm_sums(b - 1, m_ok, b)

                blocks(D // WC, lambda k: (hd_ok, 1) if k >= RH else (hl_ok, MIXED + k + 1),
                       [*range(RH, KD), *range(RH)], behind)
                norm_sums(KD - 1, m_ok, KD)
                all_read()
                ada_step(first=True)
                ada_step()
                pe.wait_ge(ms_ok, 2)
                for k in range(KD):
                    norm_sums(k, sq_ok, k + 2)
                    if k == 3:
                        ada_step()
                ada_step()
                ada_turn()
                pe.wait_ge(mod_ok, 3)
                blocks(2 * PH * P // WC, lambda k: (hl_ok, SECOND + k + 2))

            @block.scalar
            def _(act):
                row = [0]

                def copy_rows(count):
                    for _ in range(count):
                        n = row[0]
                        row[0] += 1
                        banks = ADA_BANKS[ada_part(n)][0]
                        act.wait_ge(mod_mm, n + 1)
                        nc.scalar.activation(rows[:, n % 2, :], ps[0:1 + NS, banks[n % len(banks)], 0:WC], ACT.Copy)\
                            .then_inc(row_ok, 1)

                def high(i):
                    n = split[i]
                    act.wait_ge(w_slot[n % NSLOT], 16 * (n // NSLOT + 1))
                    if i >= 2:
                        act.wait_ge(*used[i - 2])
                    nc.scalar.activation(wh[:, i % 2], wr[:, n % NSLOT], ACT.Copy).then_inc(wh_ok, 1)

                def root(n):
                    act.wait_ge(ms_ok, n)
                    nc.scalar.activation(rs[:], rs[:], ACT.Sqrt).then_inc(rt_ok, 1)

                def high_h(n, shift):
                    base = (n - 1) * (1 + KD)
                    act.wait_ge(hk_ok, base + 1)
                    nc.scalar.activation(hh[:, :, SEQ:T], tsm[:], ACT.Copy).then_inc(hh_ok, 1)
                    for k in range(KD):
                        act.wait_ge(hk_ok, base + k + 2)
                        nc.scalar.activation(hh[:, k, 0:SEQ], h[:, k, 0:SEQ], ACT.Identity,
                                             bias=mod[:, shift * KD + k, 0:1]).then_inc(hh_ok, 1)

                act.wait_ge(in_c, 16)
                nc.scalar.activation(cs[:], cs[:], ACT.Silu).then_inc(silu_c, 1)
                act.wait_ge(in_x, 16)
                nc.scalar.activation(mix[:], x[:], ACT.Square).then_inc(sq_ok, 1)
                copy_rows(5)
                root(1)
                copy_rows(ROWS_1 - 6)
                high(0)
                copy_rows(1)
                high_h(1, 0)
                for i in range(OUT_AT):
                    if i + 1 < OUT_AT:
                        high(i + 1)
                    if i == V_AT + 1:
                        act.wait_ge(v_mm, 2)
                        nc.scalar.activation(vt[:], ps[:, 0:CHUNKS, :], ACT.Copy).then_inc(v_ok, 1)
                        nc.scalar.activation(vs[:], ps[:, CHUNKS, :], ACT.Copy).then_inc(v_ok, 1)
                    if V_AT + 2 <= i < V_AT + 4:
                        if i == V_AT + 2:
                            act.wait_ge(rot_ok, 2 * RH)
                        for b in range(WB * (i - V_AT - 2), WB * (i - V_AT - 1)):
                            act.wait_ge(proj_mm, G0 + b + 1)
                            nc.scalar.activation(halves(mix[:, b, :]), pair((G0 + b) % RING), ACT.Silu)\
                                .then_inc(g_ok, 1)
                    if V_AT + 4 <= i < V_AT + 6:
                        for b in range(WB * (i - V_AT - 4), WB * (i - V_AT - 3)):
                            act.wait_ge(proj_mm, C0 + b + 1)
                            nc.scalar.activation(halves(mix[:, RH + b, :]), pair((C0 + b) % RING), ACT.Copy)\
                                .then_inc(cg_ok, 1)
                act.wait_ge(conv_ok, RH)
                nc.scalar.activation(hh[:, RH:KD], mix[:, RH:KD], ACT.Copy).then_inc(hc_ok, 1)
                act.wait_ge(in_misc, 16 * 5)
                for hd in range(RH):
                    act.wait_ge(kt_mm, hd + 1)
                    if hd:
                        act.wait_ge(st_mm, hd)
                    for c in range(CHUNKS):
                        nc.scalar.activation(kd[:, c, :], ps[:, 4, c * P:(c + 1) * P], ACT.Copy,
                                             scale=kde[:, hd, c:c + 1]).then_inc(kd_ok, 1)
                    copy_rows(1)
                    act.wait_ge(o_mm, hd + 1)
                    nc.scalar.activation(qk[:, 1, hd, 0:SEQ], ps[:, 5, :], ACT.Copy).then_inc(o_ok, 1)
                    act.wait_ge(st_mm, hd + 1)
                    nc.scalar.activation(so[:, hd, :], ps[:, 6, 0:P], ACT.Copy).then_inc(st_ok, 1)
                    copy_rows(1)
                copy_rows(1)
                act.wait_ge(o_mm, RH + 1)
                nc.scalar.activation(qk[:, 1, :, SEQ:T], ps[:, 2, 0:RH * NS].rearrange("p (h b) -> p h b", h=RH),
                                     ACT.Copy).then_inc(o_ok, 1)

                def high_rows(hd):
                    act.wait_ge(ret_ok, hd + 1)
                    nc.scalar.activation(hh[:, hd], mix[:, hd], ACT.Copy).then_inc(hh_ok, 1)

                for hd in range(RH):
                    if hd:
                        high_rows(hd - 1)
                    act.wait_ge(oc_ok, hd + 1)
                    if hd:
                        act.wait_ge(va_mm, hd)
                    nc.scalar.activation(t1, qk[:, 1, hd, :], ACT.Square).then_inc(oq_ok, 1)
                    act.wait_ge(ve_ok, hd + 1)
                    nc.scalar.activation(t2, t2, ACT.Sqrt).then_inc(sd_ok, 1)
                    if hd < RH - 1:
                        copy_rows(1)
                    else:
                        high(OUT_AT)
                high_rows(RH - 1)
                act.wait_ge(stored, 16 * 4)
                for b in range(KD):
                    if b % WB == 0 and b // WB + 1 < D // WC:
                        high(OUT_AT + b // WB + 1)
                    act.wait_ge(proj_mm, M0 + b + 1)
                    nc.scalar.activation(halves(scr[:, b, :]), pair((M0 + b) % RING), ACT.Copy)
                    nc.scalar.activation(halves(mix[:, b, :]), pair((M0 + b) % RING), ACT.Square).then_inc(m_ok, 1)
                root(2)
                copy_rows(2)
                for k in range(KD):
                    act.wait_ge(x1_ok, k + 1)
                    nc.scalar.activation(mix[:, k], x[:, k], ACT.Square).then_inc(sq_ok, 1)
                    if k == 3:
                        copy_rows(1)
                        high(Q_AT)
                root(3)
                copy_rows(1)
                high_h(2, 3)
                for b in range(2 * PH):
                    if b % WB == 0 and Q_AT + b // WB + 1 < len(split):
                        high(Q_AT + b // WB + 1)
                    act.wait_ge(proj_mm, Q2 + b + 1)
                    nc.scalar.activation(halves(qp[:, b, :]), pair((Q2 + b) % RING), ACT.Copy).then_inc(qp_ok, 1)
                act.wait_ge(qp_ok, 2 * PH)

            @block.gpsimd
            def _(pool):
                nc.gpsimd.memset(ext[:, :, 0:CK - 1], 0.0).then_inc(zero_ok, 1)
                for n in range(2 * RH):
                    pool.wait_ge(rot_mul, n + 1)
                    nc.gpsimd.tensor_tensor(qk[:, n // RH, n % RH, :], mix[:, n % 2, :], mix[:, 2 + n % 2, :],
                                            ALU.add).then_inc(rot_ok, 1)
                pool.wait_ge(in_state, 16)
                for hd in range(RH):
                    nc.gpsimd.tensor_scalar(state[:, :, hd, :], state[:, :, hd, :], 1.0 - 2.0 ** (-5 - hd),
                                            None, ALU.mult).then_inc(s0_ok, 1)
                pool.wait_ge(u_ok, RH)
                pool.wait_ge(in_misc, 16 * 5)
                pool.dma_start(io["conv_p"], ext[:, :, SEQ:SEQ + CK - 1]).then_inc(stored, 16)
                pool.dma_start(io["conv_so"], exs[:, :, 1:CK, :]).then_inc(stored, 16)
                pool.wait_ge(hc_ok, 1)
                nc.gpsimd.tensor_tensor(hl[:, RH:KD], mix[:, RH:KD], hh[:, RH:KD].bitcast(F32), ALU.subtract)\
                    .then_inc(hd_ok, 1)
                for hd in range(2, RH):
                    pool.wait_ge(pr_ok, CHUNKS * (hd - 1))
                    pool.dma_start(dec[:, hd % 2, :], io["decay"][hd]).then_inc(in_dec[hd], 16)
                pool.wait_ge(st_ok, RH)
                pool.dma_start(io["ret_p"], so[:]).then_inc(stored, 16)
                pool.wait_ge(sn_ok, NS)
                pool.dma_start(io["ret_s"], state).then_inc(stored, 16)
                pool.wait_ge(stored, 16 * 4)

            @block.vector
            def _(dve):
                done = [0]

                def note(ins):
                    done[0] += 1
                    ins.then_inc(steps, 1)
                    return done[0]

                def await_step(n):
                    dve.wait_ge(steps, n)

                def link(ins):
                    await_step(note(ins))

                def low(i):
                    dve.wait_ge(wh_ok, i + 1)
                    nc.vector.tensor_tensor(wl[:, i % 2], wr[:, split[i] % NSLOT], wh[:, i % 2].bitcast(F32),
                                            ALU.subtract).then_inc(wl_ok, 1)

                def coefficients(slot, part, g):
                    m = mod[:, part * KD:(part + 1) * KD, :]
                    gb = gain[:, g, :].unsqueeze(2).to_broadcast([P, KD, 1 + NS])
                    if part % 3 == 1:
                        link(nc.vector.scalar_tensor_tensor(co[:, slot], m, 1.0, gb, ALU.add, ALU.mult))
                    else:
                        link(nc.vector.tensor_tensor(co[:, slot], m, gb, ALU.mult))

                def mod_part(part):
                    lo, hi = ADA_AT[part] * WB, ADA_AT[part + 1] * WB
                    bank, col = ADA_BANKS[part][1:]
                    dve.wait_ge(turn_mm, part + 1)
                    sums = ps[:, bank, col:col + (hi - lo) * (1 + NS)].rearrange("p (b s) -> p b s", s=1 + NS)
                    nc.vector.tensor_tensor(mod[:, lo:hi, :], sums,
                                            bad[:, lo:hi].unsqueeze(2).to_broadcast([P, hi - lo, 1 + NS]), ALU.add)\
                        .then_inc(mod_ok, 1)
                    dve.wait_ge(mod_ok, part + 1)

                def inverse_rms(n):
                    dve.wait_ge(ss_mm, n)
                    nc.vector.tensor_scalar(halves(rs[:]), pair(SUMS), 1.0 / D, EPS, ALU.mult, ALU.add)\
                        .then_inc(ms_ok, 1)
                    dve.wait_ge(rt_ok, n)
                    link(nc.vector.reciprocal(rs[:], rs[:]))

                def modulated(n, slot, shift, first_high):
                    rs_of_samples = rs[:, SEQ:T].unsqueeze(1).to_broadcast([P, KD, NS])
                    link(nc.vector.tensor_tensor(tsm[:], x[:, :, SEQ:T], rs_of_samples, ALU.mult))
                    link(nc.vector.tensor_tensor(tsm[:], tsm[:], co[:, slot, :, 1:1 + NS], ALU.mult))
                    nc.vector.tensor_tensor(tsm[:], tsm[:], mod[:, shift * KD:(shift + 1) * KD, 1:1 + NS],
                                            ALU.add).then_inc(hk_ok, 1)
                    for k in range(KD + 2):
                        if k < KD:
                            nc.vector.scalar_tensor_tensor(h[:, k, 0:SEQ], x[:, k, 0:SEQ], co[:, slot, k, 0:1],
                                                           rs[:, 0:SEQ], ALU.mult, ALU.mult).then_inc(hk_ok, 1)
                        if k == 1:
                            dve.wait_ge(hh_ok, first_high + 1)
                            nc.vector.tensor_tensor(hl[:, :, SEQ:T], tsm[:], hh[:, :, SEQ:T].bitcast(F32),
                                                    ALU.subtract).then_inc(hl_ok, 1)
                        if k >= 2:
                            dve.wait_ge(hh_ok, first_high + k)
                            nc.vector.scalar_tensor_tensor(
                                hl[:, k - 2, 0:SEQ], h[:, k - 2, 0:SEQ], mod[:, shift * KD + k - 2, 0:1],
                                hh[:, k - 2, 0:SEQ].bitcast(F32), ALU.add, ALU.subtract).then_inc(hl_ok, 1)

                inverse_rms(1)
                low(0)
                dve.wait_ge(in_misc, 16 * 5)
                mod_part(0)
                coefficients(0, 1, 0)
                modulated(1, 0, 0, 0)

                dve.wait_ge(in_trig, 16)
                dve.wait_ge(hl_ok, 1 + KD)
                for i in range(OUT_AT):
                    if i + 1 < OUT_AT:
                        low(i + 1)
                    if i < V_AT:
                        for n in range(WB * i, WB * (i + 1)):
                            pq = pair(n % RING)
                            which = 2 * (n // RH)
                            dve.wait_ge(proj_mm, n + 1)
                            if n >= 2:
                                dve.wait_ge(rot_ok, n - 1)
                            nc.vector.tensor_tensor(halves(mix[:, n % 2, :]), pq, halves(tg[:, which, :]), ALU.mult)
                            for lo in (0, P // 2):
                                hi = P // 2 - lo
                                last = nc.vector.tensor_tensor(halves(mix[lo:lo + P // 2, 2 + n % 2, :]),
                                                               pq[hi:hi + P // 2],
                                                               halves(tg[hi:hi + P // 2, which + 1, :]), ALU.mult)
                            last.then_inc(rot_mul, 1)
                    if V_AT + 6 <= i < V_AT + 8:
                        dve.wait_ge(zero_ok, 1)
                        for b in range(WB * (i - V_AT - 6), WB * (i - V_AT - 5)):
                            n = X0 + b
                            dve.wait_ge(proj_mm, n + 1)
                            dve.wait_ge(cg_ok, b + 1)
                            c, xv = mix[:, RH + b, :], pair(n % RING)
                            nc.vector.tensor_tensor(ext[:, b, CK - 1:CK - 1 + TH], xv[:, 0, :], c[:, 0:TH], ALU.mult)
                            nc.vector.tensor_tensor(ext[:, b, CK - 1 + TH:CK - 1 + SEQ], xv[:, 1, 0:SEQ - TH],
                                                    c[:, TH:SEQ], ALU.mult)
                            nc.vector.tensor_tensor(exs[:, b, CK - 1, :], xv[:, 1, SEQ - TH:TH],
                                                    c[:, SEQ:T], ALU.mult).then_inc(u_ok, 1)
                    if i == V_AT + 8:
                        dve.wait_ge(u_ok, RH)
                        for j in range(CK):
                            for b in range(RH):
                                y = mix[:, RH + b, :]
                                for tap, out in ((ext[:, b, j:j + SEQ], y[:, 0:SEQ]), (exs[:, b, j, :], y[:, SEQ:T])):
                                    if j == 0:
                                        last = nc.vector.tensor_scalar(out, tap, cw[:, b, 0:1], cw[:, b, CK:CK + 1],
                                                                       ALU.mult, ALU.add)
                                    else:
                                        last = nc.vector.scalar_tensor_tensor(out, tap, cw[:, b, j:j + 1], out,
                                                                              ALU.mult, ALU.add)
                            link(last)
                    if i >= V_AT + 8:
                        for b in range(WB * (i - V_AT - 8), WB * (i - V_AT - 7)):
                            y = halves(mix[:, RH + b, :])
                            dve.wait_ge(proj_mm, B0 + b + 1)
                            nc.vector.tensor_tensor(y, pair((B0 + b) % RING), y, ALU.mult).then_inc(conv_ok, 1)
                for hd in range(RH):
                    dve.wait_ge(in_dec[hd], 16)
                    if hd:
                        dve.wait_ge(o_mm, hd)
                    for c in range(CHUNKS):
                        dve.wait_ge(sc_mm, CHUNKS * hd + c + 1)
                        nc.vector.tensor_tensor(pr[:, c, 0:SEQ - c * P], ps[:, c, 0:SEQ - c * P],
                                                dec[:, hd % 2, 0:SEQ - c * P], ALU.mult).then_inc(pr_ok, 1)
                dve.wait_ge(s0_ok, RH)
                for b in range(NS):
                    dve.wait_ge(vb_mm, b + 1)
                    for hd in range(RH):
                        last = nc.vector.scalar_tensor_tensor(
                            state[:, b, hd, :], ps[:, b % 2, hd * P:(hd + 1) * P],
                            qk[:, 1, hd, SEQ + b:SEQ + b + 1], state[:, b, hd, :], ALU.mult, ALU.add)
                    last.then_inc(sn_ok, 1)

                def low_rows(hd):
                    dve.wait_ge(hh_ok, MIXED + hd + 1)
                    nc.vector.tensor_tensor(hl[:, hd], mix[:, hd], hh[:, hd].bitcast(F32), ALU.subtract)\
                        .then_inc(hl_ok, 1)

                for hd in range(RH):
                    o = qk[:, 1, hd, :]
                    dve.wait_ge(mu_mm, hd + 1)
                    nc.vector.scalar_tensor_tensor(halves(o), pair(0), -1.0 / P, halves(o), ALU.mult, ALU.add)\
                        .then_inc(oc_ok, 1)
                    if hd:
                        low_rows(hd - 1)
                    dve.wait_ge(va_mm, hd + 1)
                    nc.vector.tensor_scalar(halves(t2), pair(1), 1.0 / P, EPS, ALU.mult, ALU.add)\
                        .then_inc(ve_ok, 1)
                    dve.wait_ge(sd_ok, hd + 1)
                    link(nc.vector.reciprocal(t2, t2))
                    link(nc.vector.tensor_tensor(t2, t2, o, ALU.mult))
                    nc.vector.tensor_tensor(mix[:, hd, :], t2, mix[:, hd, :], ALU.mult).then_inc(ret_ok, 1)
                mod_part(1)
                low(OUT_AT)
                low_rows(RH - 1)
                for slot, part in ((1, 2), (2, 4)):
                    coefficients(slot, part, slot)
                for i in range(1, D // WC):
                    low(OUT_AT + i)
                inverse_rms(2)
                residual(note, await_step, scr, 1, x1_ok)
                low(Q_AT)
                inverse_rms(3)
                modulated(2, 2, 3, SECOND)
                mod_part(2)
                for i in range(1, 2 * PH * P // WC):
                    low(Q_AT + i)
                coefficients(3, 5, 3)


def gate_stage(nc, sem, sb, pair, halves, on_chip, qp, u_side, io):
    x, h, mod, cst, gain, co, tsm, rs, ps = on_chip
    hh, hl, us, uh, ul, a, u_in, uh_ok, ul_ok, u_mm, a_ok = (
        u_side[n] for n in ("hh", "hl", "us", "uh", "ul", "a", "u_in", "uh_ok", "ul_ok", "u_mm", "a_ok"))
    ident, iota = cst[:, 1, :], cst[:, 2, :]
    starts, widths = cst[0:TT, 3, 0:TOPK], cst[0:TT, 3, TOPK:TOPK + 8]
    BT = TT // OH
    BUFS = 3
    STORES = 3
    CREDIT = 2
    EVERY = 4
    POOLS = [b for b in range(BT) if b % EVERY != EVERY - 1]
    STEPS = 22
    BANK_T, BANK_G = 1, 6
    ROW = [TOPK // (r + 1) for r in range(TOPK)]
    AT = [sum(ROW[:r]) for r in range(TOPK)]
    NC = sum(ROW)
    HEAD, TAIL = 1, 4
    STEP = [HEAD * KD + b * (AB - HEAD - TAIL) * KD // BT for b in range(BT + 1)]
    BEHIND = [-1 if r < HEAD else BT if r >= AB - TAIL else
              min(b for b in range(BT) if STEP[b + 1] >= (r + 1) * KD) for r in range(AB)]
    stack = ExitStack()
    with stack:
        keys = sb(stack, "keys", [P, 2 * PH, NK])
        qt = sb(stack, "qt", [P, 2 * PH, TT])
        on_h = h[:].rearrange("p k t -> p (k t)")
        s = on_h[0:TT, 0:2 * PH * NK].rearrange("p (j n) -> p j n", n=NK)
        s2 = on_h[0:TT, 2 * PH * NK:4 * PH * NK].rearrange("p (j n) -> p j n", n=NK)
        cand = sb(stack, "cand", [TT, PH, NC])
        cand2 = sb(stack, "cand2", [TT, PH, NC])
        top = sb(stack, "top", [TT, 2 * PH, TOPK])
        topi = sb(stack, "topi", [TT, 2 * PH, TOPK], U32)
        topf = sb(stack, "topf", [TT, 2 * PH, TOPK])
        diff = sb(stack, "diff", [TT, PH, TOPK])
        best = sb(stack, "best", [TT, PH, TOPK])
        pos = sb(stack, "pos", [TT, PH, TOPK], U32)
        posf = sb(stack, "posf", [TT, HK])
        start = sb(stack, "start", [TT, HK])
        over = sb(stack, "over", [TT, HK])
        ex = sb(stack, "ex", [TT, PH, TOPK])
        den = sb(stack, "den", [TT, PH])
        pick = sb(stack, "pick", [TT, 3, HK])
        pt = sb(stack, "pt", [P, 3, TT])
        eq1 = sb(stack, "eq1", [P, BUFS, OH, P])
        ga = sb(stack, "ga", [P, BUFS, OH, P])
        eq2 = sb(stack, "eq2", [P, BUFS, OH, P])
        stage = sb(stack, "stage", [P, 2, NK, CH])

        in_keys = sem("in_keys")
        qt_ok = sem("qt_ok")
        s_mm = sem("s_mm")
        s_ok = sem("s_ok")
        steps = sem("gate_dve")
        best_ok = sem("best_ok")
        ex_ok = sem("ex_ok")
        pick_ok = sem("pick_ok")
        pt_mm = sem("pt_mm")
        pt_ok = sem("pt_ok")
        eq1_ok = sem("eq1_ok")
        df2_ok = sem("df2_ok")
        eq2_ok = sem("eq2_ok")
        eqv_ok = sem("eqv_ok")
        ga_ok = sem("ga_ok")
        g_mm = sem("gate_mm")
        g_ok = sem("gate_ok")
        kept = [sem(f"kept{c}") for c in range(2)]
        a_kept = [sem(f"a_kept{c}") for c in range(NA)]
        settled = sem("settled")
        p_settled = sem("p_settled")

        with nc.Block() as block:

            @block.sync
            def _(sp):
                for c in range(NA):
                    sp.sem_inc(a_kept[c], 16)
                sp.dma_start(keys[:], io["keysT"]).then_inc(in_keys, 16)
                u_of = io["utab"][0:AB * (TILES + 2)].rearrange("(i r) p k e -> i r p k e", r=AB)
                out = io["ahead"].rearrange("(i r) p t -> i r p t", r=AB)
                for r in range(NU):
                    sp.dma_start(us[:, r], io["utab"][r]).then_inc(u_in[r], 16)

                with sp.Fori(0, TILES + 1) as i:
                    for r in range(AB):
                        sp.wait_ge(ul_ok, i * AB + (r + 1))
                        nxt = u_of[bass.ds(i, 1), r + NU] if r + NU < AB else u_of[bass.ds(i + 1, 1), r + NU - AB]
                        sp.dma_start(us[:, r % NU], nxt.rearrange("i p k e -> (i p) k e")).then_inc(u_in[r % NU], 16)
                        sp.wait_ge(a_ok, i * AB + (r + 1))
                        sp.dma_start(out[bass.ds(i, 1), r].rearrange("i p t -> (i p) t"), a[:, r % NA])\
                            .then_inc(a_kept[r % NA], 16)
                for c in range(NA):
                    sp.wait_ge(a_kept[c], 16 * (AHEAD // NA) + 16)

            @block.tensor
            def _(pe):
                def scores(i):
                    for m in range(4):
                        pe.wait_ge(qt_ok, i * 4 + (m + 1))
                        if m >= 2:
                            pe.wait_ge(s_ok, i * 4 + (m - 1))
                        elif m == BANK_T and positive(i):
                            pe.wait_ge(pt_ok, i)
                        for j in range(4 * m, 4 * m + 4):
                            last = nc.tensor.matmul(ps[0:TT, m % 2, (j % 4) * NK:(j % 4 + 1) * NK], qt[:, j, :],
                                                    keys[:, j, :], start=True, stop=True)
                        last.then_inc(s_mm, 1)

                def ahead(i, first, past):
                    for q in range(first, past):
                        r, k = q // KD, q % KD
                        if k == 0:
                            pe.wait_ge(ul_ok, i * AB + (r + 1))
                            if positive(i) or r >= 2:
                                pe.wait_ge(a_ok, i * AB + (r - 1))
                        last = u_product(nc, pair(u_pairs(r)), uh[:, r % 2], ul[:, r % 2], hh, hl, k)
                        if k == KD - 1:
                            last.then_inc(u_mm, 1)

                def matrix_and_ahead(i):
                    ahead(i, 0, STEP[0])
                    for b in range(BT):
                        if positive(i):
                            if b in POOLS:
                                n = len(POOLS)
                                pe.wait_ge(eq2_ok, i * n + (POOLS.index(b) + 1 - n))
                            else:
                                n = BT - len(POOLS)
                                pe.wait_ge(eqv_ok, i * n + (b // EVERY + 1 - n))
                            pe.wait_ge(ga_ok, i * BT + (b + 1 - BT))
                            pe.wait_ge(g_ok, i * BT + (b + 1 - BT))
                            for t in range(OH):
                                last = nc.tensor.matmul(ps[:, BANK_G + b % 2, t * P:(t + 1) * P],
                                                        ga[:, b % BUFS, t, :], eq2[:, b % BUFS, t, :],
                                                        start=True, stop=True)
                            last.then_inc(g_mm, 1)
                        ahead(i, STEP[b], STEP[b + 1])
                    ahead(i, STEP[BT], AB * KD)

                def turn(i):
                    pe.wait_ge(pick_ok, i + 1)
                    for j in range(3):
                        last = nc.tensor.transpose(ps[:, BANK_T, j * TT:(j + 1) * TT], pick[:, j, :],
                                                   ident[0:TT, 0:TT])
                    last.then_inc(pt_mm, 1)

                pe.sem_inc(g_mm, BUFS)
                pe.wait_ge(in_keys, 16)
                scores(0)
                matrix_and_ahead(0)
                turn(0)
                with pe.Fori(1, TILES) as i:
                    scores(i)
                    matrix_and_ahead(i)
                    turn(i)
                matrix_and_ahead(TILES)

            @block.scalar
            def _(act):
                tiles_of_qp = qp[:].rearrange("p j (i t) -> p i j t", t=TT)
                chunks = io["gates"].rearrange("g p (i c) a t -> i c p g (a t)", c=TT // CH)

                def inputs(i):
                    for m in range(4):
                        if isinstance(i, int):
                            src = tiles_of_qp[:, i]
                        else:
                            act.wait_ge(s_mm, i * 4 + (m - 3))
                            src = tiles_of_qp[:, bass.ds(i, 1)].rearrange("p i j t -> p (i j) t")
                        nc.scalar.activation(qt[:, 4 * m:4 * m + 4, :], src[:, 4 * m:4 * m + 4, :], ACT.Copy)\
                            .then_inc(qt_ok, 1)
                    for m in range(4):
                        act.wait_ge(s_mm, i * 4 + (m + 1))
                        nc.scalar.activation(s[:, 4 * m:4 * m + 4, :], ps[0:TT, m % 2, :]
                                             .rearrange("p (j n) -> p j n", n=NK), ACT.Copy).then_inc(s_ok, 1)

                def high(m, r):
                    act.wait_ge(u_in[r % NU], m * (16 // NU) + (16 - 16 * (r % NU) // NU))
                    nc.scalar.activation(uh[:, r % 2], us[:, r % NU], ACT.Copy).then_inc(uh_ok, 1)

                def ahead(i, r):
                    act.wait_ge(u_mm, i * AB + (r + 1))
                    act.wait_ge(a_kept[r % NA], i * (16 * AB // NA) + 16 * (r // NA) + 16)
                    nc.scalar.activation(halves(a[:, r % NA]), pair(u_pairs(r)), ACT.Gelu_apprx_tanh).then_inc(a_ok, 1)
                    high(i * AB + (r + 2), r)

                def store(i, c, n):
                    act.wait_ge(g_ok, i * BT + (-(-(c + 1) * CH // OH) - BT + CREDIT))
                    to = chunks[bass.ds(i - 1, 1), c] if not isinstance(i, int) else chunks[i - 1:i, c]
                    to = to.rearrange("i p g a -> (i p) g a")
                    held = stage[:, c % 2].rearrange("p (g a) t -> p g (a t)", a=GB)
                    part = slice(n * NGRP // STORES, (n + 1) * NGRP // STORES)
                    act.dma_start(to[:, part], held[:, part]).then_inc(kept[c % 2], 16)

                def copied(i, b):
                    act.wait_ge(g_mm, i * BT + (b + 1 - BT + BUFS))
                    at, gates = b * OH, ps[:, BANK_G + b % 2, :].rearrange("p (t n) -> p t n", t=OH)
                    while at < (b + 1) * OH:
                        c = at // CH
                        upto = min((b + 1) * OH, (c + 1) * CH)
                        if at == c * CH:
                            act.wait_ge(kept[c % 2], i * (32 * STORES) + 16 * STORES * (c // 2 - 1))
                        last = nc.scalar.activation(
                            stage[:, c % 2, :, at - c * CH:upto - c * CH].rearrange("p n t -> p t n"),
                            gates[:, at - b * OH:upto - b * OH, :], ACT.Copy)
                        at = upto
                    last.then_inc(g_ok, 1)

                def gated_and_ahead(i):
                    for b in range(BT):
                        if positive(i):
                            act.wait_ge(eq1_ok, i * BT + (b + 1 - BT))
                            for t in range(OH):
                                last = nc.scalar.activation(ga[:, b % BUFS, t, :], eq1[:, b % BUFS, t, :], ACT.Copy,
                                                            scale=pt[:, 2, b * OH + t:b * OH + t + 1])
                            last.then_inc(ga_ok, 1)
                            if b:
                                copied(i, b - 1)
                            for c in range(TT // CH):
                                n = b - 1 + (-(c + 1) * CH // OH)
                                if 0 <= n < STORES:
                                    store(i, c, n)
                        for r in range(AB):
                            if BEHIND[r] + 1 == b:
                                ahead(i, r)
                    if positive(i):
                        copied(i, BT - 1)
                        store(i, TT // CH - 1, 0)
                    for r in range(AB):
                        if BEHIND[r] + 1 == BT:
                            ahead(i, r)

                def tail(i):
                    for n in range(max(TAIL, STORES - 1)):
                        if n < TAIL:
                            ahead(i, AB - TAIL + n)
                        if positive(i) and n + 1 < STORES:
                            store(i, TT // CH - 1, n + 1)

                def softmax(i):
                    act.wait_ge(best_ok, i + 1)
                    nc.scalar.activation(ex[:], ex[:], ACT.Exp).then_inc(ex_ok, 1)
                    tail(i)
                    act.wait_ge(pt_mm, i + 1)
                    nc.scalar.activation(pt[:], ps[:, BANK_T, 0:3 * TT].rearrange("p (j t) -> p j t", j=3), ACT.Copy)\
                        .then_inc(pt_ok, 1)

                act.sem_inc(g_ok, CREDIT)
                for c in range(2):
                    act.sem_inc(kept[c], 16 * STORES)
                for r in range(2):
                    high(r, r)
                inputs(0)
                gated_and_ahead(0)
                softmax(0)
                with act.Fori(1, TILES) as i:
                    inputs(i)
                    gated_and_ahead(i)
                    softmax(i)
                gated_and_ahead(TILES)
                tail(TILES)
                for c in range(2):
                    act.wait_ge(kept[c], (32 * TILES + 16) * STORES)

            @block.gpsimd
            def _(pool):
                with pool.Fori(1, TILES + 1) as i:
                    pool.wait_ge(pt_ok, i)
                    for n, b in enumerate(POOLS):
                        pool.wait_ge(g_mm, i * BT + (b + 1 - BT))
                        nc.gpsimd.tensor_tensor(eq2[:, b % BUFS], iota.unsqueeze(1).to_broadcast([P, OH, P]),
                                                pt[:, 1, b * OH:(b + 1) * OH].unsqueeze(2).to_broadcast([P, OH, P]),
                                                ALU.subtract).then_inc(df2_ok, 1)
                        pool.wait_ge(df2_ok, i * len(POOLS) + (n + 1 - len(POOLS)))
                        pool.sem_inc(p_settled, 1)
                        nc.gpsimd.tensor_scalar(eq2[:, b % BUFS], eq2[:, b % BUFS], 0.0, None, ALU.is_equal).then_inc(eq2_ok, 1)

            @block.vector
            def _(dve):
                def low(m, r):
                    dve.wait_ge(uh_ok, m + 1)
                    nc.vector.tensor_tensor(ul[:, r % 2], us[:, r % NU], uh[:, r % 2].bitcast(F32), ALU.subtract)\
                        .then_inc(ul_ok, 1)

                def one_hot(i, b):
                    if b == 0:
                        dve.wait_ge(pt_ok, i)
                    dve.wait_ge(g_mm, i * BT + (b + 1 - BT))
                    nc.vector.tensor_tensor(eq1[:, b % BUFS], iota.unsqueeze(1).to_broadcast([P, OH, P]),
                                            pt[:, 0, b * OH:(b + 1) * OH].unsqueeze(2).to_broadcast([P, OH, P]),
                                            ALU.is_equal).then_inc(eq1_ok, 1)
                    if b not in POOLS:
                        nc.vector.tensor_tensor(eq2[:, b % BUFS], iota.unsqueeze(1).to_broadcast([P, OH, P]),
                                                pt[:, 1, b * OH:(b + 1) * OH].unsqueeze(2).to_broadcast([P, OH, P]),
                                                ALU.is_equal).then_inc(eqv_ok, 1)

                def batch(i, b):
                    if b < BT and positive(i):
                        one_hot(i, b)
                    for r in range(AB):
                        if BEHIND[r] + 2 == b:
                            low(i * AB + (r + 2), r)

                def choose(i):
                    done = [0]
                    calls = [0]
                    batches = [0]

                    def step(ins):
                        done[0] += 1
                        ins.then_inc(steps, 1)

                    def settle():
                        dve.wait_ge(steps, i * STEPS + done[0])
                        dve.sem_inc(settled, 1)

                    def between():
                        calls[0] += 1
                        if calls[0] % 4 == 0 and batches[0] < BT:
                            batch(i, batches[0])
                            batches[0] += 1

                    sets = range(2 * PH)
                    for j in sets:
                        if j % 4 == 0:
                            dve.wait_ge(s_ok, i * 4 + (j // 4 + 1))
                            dve.sem_inc(settled, 1)
                        last = nc.vector.max(top[:, j, 0:8], s[:, j, :])
                        if j == 2 * PH - 1:
                            step(last)
                        between()
                    settle()
                    for j in sets:
                        last = nc.vector.match_replace(s2[:, j, :], top[:, j, 0:8], s[:, j, :], LOWEST)
                        if j == 2 * PH - 1:
                            step(last)
                        between()
                    for j in sets:
                        nc.vector.max_index(topi[:, j, 0:8], top[:, j, 0:8], s[:, j, :])
                        between()
                    settle()
                    for j in sets:
                        last = nc.vector.max(top[:, j, 8:16], s2[:, j, :])
                        if j == 2 * PH - 1:
                            step(last)
                        between()
                    settle()
                    both = top[:].rearrange("p (h c) k -> p c h k", c=2)
                    r = 0
                    while r < TOPK:
                        n = ROW.count(ROW[r])
                        w = ROW[r]
                        last = nc.vector.tensor_tensor(
                            cand[:, :, AT[r]:AT[r] + n * w].rearrange("p h (a b) -> p h a b", b=w),
                            both[:, 0, :, r:r + n].unsqueeze(3).to_broadcast([TT, PH, n, w]),
                            both[:, 1, :, 0:w].unsqueeze(2).to_broadcast([TT, PH, n, w]), ALU.add)
                        r += n
                    step(last)
                    for j in sets:
                        last = nc.vector.max_index(topi[:, j, 8:16], top[:, j, 8:16], s2[:, j, :])
                        between()
                    step(last)
                    settle()
                    for j in range(PH):
                        last = nc.vector.max(best[:, j, 0:8], cand[:, j, :])
                        between()
                    step(last)
                    step(nc.vector.tensor_copy(topf[:], topi[:]))
                    settle()
                    for j in range(PH):
                        last = nc.vector.match_replace(cand2[:, j, :], best[:, j, 0:8], cand[:, j, :], LOWEST)
                        between()
                    step(last)
                    for j in range(PH):
                        nc.vector.max_index(pos[:, j, 0:8], best[:, j, 0:8], cand[:, j, :])
                        between()
                    settle()
                    for j in range(PH):
                        last = nc.vector.max(best[:, j, 8:16], cand2[:, j, :])
                        between()
                    step(last)
                    keys_at = topf[:].rearrange("p (h c) a -> p c h a", c=2)
                    nc.vector.tensor_copy(diff[:, :, 0:1], keys_at[:, 0, :, 0:1])
                    nc.vector.tensor_tensor(diff[:, :, 1:TOPK], keys_at[:, 0, :, 1:TOPK],
                                            keys_at[:, 0, :, 0:TOPK - 1], ALU.subtract)
                    settle()
                    for j in range(PH):
                        last = nc.vector.max_index(pos[:, j, 8:16], best[:, j, 8:16], cand2[:, j, :])
                        between()
                    step(last)
                    nc.vector.tensor_tensor(ex[:], best[:], best[:, :, 0:1].to_broadcast([TT, PH, TOPK]),
                                            ALU.subtract).then_inc(best_ok, 1)
                    settle()
                    step(nc.vector.tensor_copy(posf[:], pos[:].rearrange("p h k -> p (h k)")))
                    while batches[0] < BT + 2:
                        batch(i, batches[0])
                        batches[0] += 1
                    settle()
                    work = s2[:].rearrange("p j n -> p (j n)").rearrange("p (k a) -> p k a", a=TOPK)
                    work2 = s[:].rearrange("p j n -> p (j n)").rearrange("p (k a) -> p k a", a=TOPK)
                    by_head = lambda w: w.rearrange("p (h k) a -> p h k a", h=PH)
                    shape = [TT, PH, TOPK, TOPK]
                    nc.vector.tensor_scalar(over[:], posf[:], -float(AT[8]), 0.0, ALU.add, ALU.max)
                    step(nc.vector.tensor_tensor(work, posf[:].unsqueeze(2).to_broadcast([TT, HK, TOPK]),
                                                 starts.unsqueeze(1).to_broadcast([TT, HK, TOPK]), ALU.is_ge))
                    settle()
                    wide = work2[:, :, 0:8]
                    step(nc.vector.tensor_tensor(wide, work[:, :, 1:9],
                                                 widths.unsqueeze(1).to_broadcast([TT, HK, 8]), ALU.mult))
                    dve.wait_ge(steps, i * STEPS + done[0])
                    step(nc.vector.tensor_tensor(by_head(work), by_head(work),
                                                 diff[:].unsqueeze(2).to_broadcast(shape), ALU.mult))
                    step(nc.vector.tensor_reduce(start[:], wide, AX.X, ALU.add))
                    dve.wait_ge(steps, i * STEPS + (done[0] - 1))
                    step(nc.vector.tensor_reduce(pick[:, 0, :], work, AX.X, ALU.add))
                    dve.wait_ge(steps, i * STEPS + (done[0] - 1))
                    step(nc.vector.tensor_tensor(start[:], start[:], over[:], ALU.add))
                    settle()
                    step(nc.vector.tensor_tensor(posf[:], posf[:], start[:], ALU.subtract))
                    settle()
                    low(i * AB + (AB - TAIL + 2), AB - TAIL)
                    step(nc.vector.tensor_tensor(work, posf[:].unsqueeze(2).to_broadcast([TT, HK, TOPK]),
                                                 iota[0:TT, 0:TOPK].unsqueeze(1).to_broadcast([TT, HK, TOPK]),
                                                 ALU.is_equal))
                    dve.wait_ge(ex_ok, i + 1)
                    step(nc.vector.tensor_reduce(den[:], ex[:], AX.X, ALU.add))
                    settle()
                    step(nc.vector.tensor_tensor(by_head(work), by_head(work),
                                                 keys_at[:, 1].unsqueeze(2).to_broadcast(shape), ALU.mult))
                    step(nc.vector.reciprocal(den[:], den[:]))
                    low(i * AB + (AB - TAIL + 3), AB - TAIL + 1)
                    settle()
                    nc.vector.tensor_tensor(pick[:, 2, :].rearrange("p (h k) -> p h k", h=PH), ex[:],
                                            den[:].unsqueeze(2).to_broadcast([TT, PH, TOPK]), ALU.mult)
                    nc.vector.tensor_reduce(pick[:, 1, :], work, AX.X, ALU.add).then_inc(pick_ok, 1)
                    for r in range(AB - TAIL + 2, AB):
                        low(i * AB + (r + 2), r)
                    assert done[0] == STEPS, done[0]

                for r in range(2):
                    low(r, r)
                choose(0)
                with dve.Fori(1, TILES) as i:
                    choose(i)
                for b in range(BT + 2):
                    batch(TILES, b)
                for r in range(AB - TAIL, AB):
                    low(TILES * AB + (r + 2), r)
                dve.wait_ge(ul_ok, AHEAD + 2)


def expert_stage(nc, sem, sb, pair, halves, residual, on_chip, u_side, io):
    x, h, mod, cst, gain, co, tsm, rs, ps = on_chip
    hh, hl, us, uh, ul, a, u_in, uh_ok, ul_ok, u_mm, a_ok = (
        u_side[n] for n in ("hh", "hl", "us", "uh", "ul", "a", "u_in", "uh_ok", "ul_ok", "u_mm", "a_ok"))
    ones = cst[:, 0, :]
    DH = D // 2
    KH = KD // 2
    stack = ExitStack()
    with stack:
        vs = sb(stack, "vblk", [P, 2, GB, DH])
        vh = sb(stack, "vh", [P, GB, D], F32R)
        vl = sb(stack, "vl", [P, GB, D], F32R)
        gt = sb(stack, "gt", [P, 2, NCH, GB, CH])
        aa = sb(stack, "aa", [P, GB, T])
        ch = sb(stack, "ch", [P, 2, GB, T], F32R)
        cl = sb(stack, "cl", [P, 2, GB, T], F32R)
        acc = h
        squares = gt[:].rearrange("p a c g t -> p (a c g t)").rearrange("p (k t) -> p k t", k=KD)

        v_in = [sem(f"v_in{n}") for n in range(2)]
        g_in = [sem(f"g_in{n}") for n in range(2)]
        aa_in = [sem(f"aa_in{n}") for n in range(GB)]
        c_ok = sem("c_ok")
        ch_ok = sem("ch_ok")
        cl_ok = sem("cl_ok")
        vh_ok = sem("vh_ok")
        vl_ok = sem("vl_ok")
        f_mm = sem("f_mm")
        f_ok = sem("f_ok")
        fsq_ok, fss_mm, fms_ok, frt_ok = (sem(n) for n in ("fsq_ok", "fss_mm", "fms_ok", "frt_ok"))
        y_ok = sem("y_ok")
        y_out = sem("y_out")
        steps = sem("expert_dve")

        def groups(eng, step):
            step(0, 0)
            with eng.Fori(0, AGRP // 2) as i:
                step(i * 2 + 1, 1, ahead=True)
                step(i * 2 + 2, 0, ahead=True)
            with eng.Fori(AGRP // 2, NGRP // 2 - 1) as i:
                step(i * 2 + 1, 1, ahead=False)
                step(i * 2 + 2, 0, ahead=False)
            step(NGRP - 1, 1)
            step(NGRP, 0)

        def kind(g, ahead):
            if ahead is not None:
                return "ahead" if ahead else "make"
            return "make" if g < NGRP else None

        def block_of(g, j):
            return (AGRP * GB if isinstance(g, int) and g == 0 else g * GB) + j

        with nc.Block() as block:

            @block.sync
            def _(sp):
                u_pairs_of = io["utab"].rearrange("(i j) p k e -> i j p k e", j=2 * GB)
                a_pairs_of = io["ahead"].rearrange("(i j) p t -> i j p t", j=2 * GB)
                v_pairs_of = io["vtab"].rearrange("p (i s j) (f d) -> i s f p j d", s=2, j=GB, f=2)
                g_pairs_of = io["gates"].rearrange("(i s) p c a t -> i s p c a t", s=2)

                def load_u(i, j, wait):
                    sp.wait_ge(ul_ok, wait)
                    src = u_pairs_of[i, j] if isinstance(i, int) else \
                        u_pairs_of[bass.ds(i, 1), j].rearrange("i p k e -> (i p) k e")
                    sp.dma_start(us[:, j % NU], src).then_inc(u_in[j % NU], 16)

                def load_a(i, s, j, wait=None):
                    if wait is not None:
                        sp.wait_ge(cl_ok, wait)
                    sp.dma_start(aa[:, j], a_pairs_of[bass.ds(i, 1), GB * s + j].rearrange("i p t -> (i p) t"))\
                        .then_inc(aa_in[j], 16)

                def load_v(i, s, f, wait=None):
                    if wait is not None:
                        sp.wait_ge(vl_ok, wait)
                    sp.dma_start(vs[:, f], v_pairs_of[bass.ds(i, 1), s, f].rearrange("i p j d -> (i p) j d"))\
                        .then_inc(v_in[f], 16)

                def load_g(i, s, parity, wait=None):
                    if wait is not None:
                        sp.wait_ge(c_ok, wait)
                    sp.dma_start(gt[:, parity], g_pairs_of[bass.ds(i, 1), s].rearrange("i p c a t -> (i p) c a t"))\
                        .then_inc(g_in[parity], 16)

                first = AGRP // 2
                for j in range(NU, GB):
                    load_u(first, j, AHEAD + j - NU + 1)
                load_g(first, 0, 0)
                for f in range(2):
                    load_v(first, 0, f)
                for j in range(GB):
                    load_a(0, 0, j)
                load_g(0, 0, 1)
                for j in range(GB, 2 * GB):
                    load_u(first, j, AHEAD + j - NU + 1)
                for f in range(2):
                    load_v(0, 0, f, f + 1)

                def beside_ahead(i, s):
                    load_g(i, s, 1 - s, i * (2 * GB) + s * GB)
                    for j in range(GB):
                        load_a(i, s, j, i * (2 * GB) + (s * GB + j + 1))
                    for f in range(2):
                        load_v(i, s, f, i * 4 + (2 * s + f + 1))

                beside_ahead(0, 1)
                with sp.Fori(1, AGRP // 2) as i:
                    for s in range(2):
                        beside_ahead(i, s)
                load_g(first, 1, 1, AGRP * GB)
                for f in range(2):
                    load_v(first, 1, f, 2 * AGRP + f + 1)
                with sp.Fori(AGRP // 2, NGRP // 2 - 1) as i:
                    for s in range(2):
                        load_g(i + 1, s, s, i * (2 * GB) + (1 + s) * GB)
                        for j in range(GB):
                            load_u(i + 1, GB * s + j, i * (2 * GB) + ((1 + s) * GB + j + NU + 1))
                        for f in range(2):
                            load_v(i + 1, s, f, i * 4 + (2 * (1 + s) + f + 1))
                for k in range(0, KD, 2):
                    sp.wait_ge(y_ok, k + 2)
                    sp.dma_start(io["yT"][:, k:k + 2], x[:, k:k + 2]).then_inc(y_out, 16)
                sp.wait_ge(y_out, 16 * KD // 2)

            @block.tensor
            def _(pe):
                def step(g, parity, ahead=None):
                    if kind(g, ahead) == "make":
                        for j in range(GB):
                            n = block_of(g, j)
                            pe.wait_ge(ul_ok, n + 1)
                            pe.wait_ge(a_ok, n - 1)
                            for k in range(KD):
                                last = u_product(nc, pair(u_pairs(j)), uh[:, j % 2], ul[:, j % 2], hh, hl, k)
                            last.then_inc(u_mm, 1)
                    if positive(g):
                        pe.wait_ge(cl_ok, g * GB)
                        for k in range(KD):
                            if k % KH == 0:
                                pe.wait_ge(vl_ok, g * 2 + (k // KH - 1))
                            pe.wait_ge(f_ok, g * KD + (k + 1 - KD))
                            out = pair(3 * (k % 2))
                            for j in range(GB):
                                hi, lo = vh[:, j, k * P:(k + 1) * P], vl[:, j, k * P:(k + 1) * P]
                                c_hi, c_lo = ch[:, 1 - parity, j, :], cl[:, 1 - parity, j, :]
                                for n, (w, m) in enumerate(((hi, c_lo), (hi, c_hi), (lo, c_hi))):
                                    for half in range(2):
                                        last = nc.tensor.matmul(out[:, half, :], w, m[:, half * TH:(half + 1) * TH],
                                                                start=(j == 0 and n == 0),
                                                                stop=(j == GB - 1 and n == 2))
                            last.then_inc(f_mm, 1)

                pe.sem_inc(f_mm, KD)
                groups(pe, step)
                for k in range(KD):
                    pe.wait_ge(fsq_ok, k + 1)
                    for half in range(2):
                        last = nc.tensor.matmul(ps[:, 2 + half, 0:TH], ones, squares[:, k, half * TH:(half + 1) * TH],
                                                start=(k == 0), stop=(k == KD - 1))
                last.then_inc(fss_mm, 1)

            @block.scalar
            def _(act):
                def high_v(g, f):
                    act.wait_ge(v_in[f], g * 16 + 16)
                    act.wait_ge(f_mm, g * KD + (f + 1) * KH)
                    nc.scalar.activation(vh[:, :, f * DH:(f + 1) * DH], vs[:, f], ACT.Copy).then_inc(vh_ok, 1)

                def step(g, parity, ahead=None):
                    what = kind(g, ahead)
                    for j in range(GB) if what else ():
                        n = g * GB + j
                        src = aa[:, j] if what == "ahead" else a[:, j % 2]
                        if what == "make":
                            u = block_of(g, j)
                            act.wait_ge(u_mm, u + 1)
                            if positive(g) or j >= 2:
                                act.wait_ge(cl_ok, n - 1)
                            nc.scalar.activation(halves(a[:, j % 2]), pair(u_pairs(j)), ACT.Gelu_apprx_tanh)\
                                .then_inc(a_ok, 1)
                            if not (isinstance(g, int) and g == NGRP - 1 and j + 2 >= GB):
                                act.wait_ge(u_in[j % NU], u * (16 // NU) + (16 + 16 - 16 * (j % NU) // NU))
                                nc.scalar.activation(uh[:, j % 2], us[:, j % NU], ACT.Copy).then_inc(uh_ok, 1)
                        act.wait_ge(c_ok, n + 1)
                        if positive(g):
                            act.wait_ge(f_mm, g * KD)
                        nc.scalar.activation(ch[:, parity, j], src, ACT.Copy).then_inc(ch_ok, 1)
                    if what:
                        for f in range(2):
                            high_v(g, f)

                groups(act, step)
                for k in range(KD):
                    act.wait_ge(f_ok, NGRP * KD + (k + 3 - KD))
                    nc.scalar.activation(squares[:, k], acc[:, k], ACT.Square).then_inc(fsq_ok, 1)
                act.wait_ge(fms_ok, 1)
                nc.scalar.activation(rs[:], rs[:], ACT.Sqrt).then_inc(frt_ok, 1)
                act.wait_ge(frt_ok, 1)

            @block.vector
            def _(dve):
                done = [0]

                def note(ins):
                    done[0] += 1
                    ins.then_inc(steps, 1)
                    return done[0]

                def await_step(n):
                    dve.wait_ge(steps, n)

                def low(out, full, high):
                    return nc.vector.tensor_tensor(out, full, high.bitcast(F32), ALU.subtract)

                def low_v(g, f):
                    dve.wait_ge(vh_ok, g * 2 + (f + 1))
                    cols = slice(f * DH, (f + 1) * DH)
                    low(vl[:, :, cols], vs[:, f], vh[:, :, cols]).then_inc(vl_ok, 1)

                def by_chunk(ap):
                    return ap.rearrange("p (c t) -> p c t", t=CH)

                def coefficients(g, parity, what, j):
                    src = aa[:, j] if what == "ahead" else a[:, j % 2]
                    u = block_of(g, j)
                    if what == "make":
                        dve.wait_ge(a_ok, u + 1)
                    else:
                        dve.wait_ge(aa_in[j], g * 16)
                    if j == 0:
                        dve.wait_ge(g_in[parity], g * 8 + (16 - 8 * parity))
                    nc.vector.tensor_tensor(by_chunk(src), by_chunk(src), gt[:, parity, :, j, :],
                                            ALU.mult).then_inc(c_ok, 1)
                    if what == "make" and not (isinstance(g, int) and g == NGRP - 1 and j + 2 >= GB):
                        dve.wait_ge(uh_ok, u + 3)
                        low(ul[:, j % 2], us[:, j % NU], uh[:, j % 2]).then_inc(ul_ok, 1)

                def low_coefficients(g, parity, what, j):
                    src = aa[:, j] if what == "ahead" else a[:, j % 2]
                    dve.wait_ge(ch_ok, g * GB + j + 1)
                    low(cl[:, parity, j], src, ch[:, parity, j]).then_inc(cl_ok, 1)

                def step(g, parity, ahead=None):
                    what = kind(g, ahead)
                    between = what == "ahead" and positive(g)
                    for j in range(GB) if what and not between else ():
                        coefficients(g, parity, what, j)
                        low_coefficients(g, parity, what, j)
                    if positive(g):
                        for k in range(KD):
                            if between and k < GB:
                                coefficients(g, parity, what, k)
                            dve.wait_ge(f_mm, g * KD + (k + 1))
                            nc.vector.tensor_tensor(halves(acc[:, k]), pair(3 * (k % 2)), halves(acc[:, k]), ALU.add)\
                                .then_inc(f_ok, 1)
                            if between and k < GB:
                                low_coefficients(g, parity, what, k)
                            if what and k == KH:
                                low_v(g, 0)
                    else:
                        low_v(g, 0)
                    if what:
                        low_v(g, 1)

                dve.sem_inc(f_ok, 2)
                nc.vector.memset(acc[:], 0.0)
                groups(dve, step)
                dve.wait_ge(fss_mm, 1)
                nc.vector.tensor_scalar(halves(rs[:]), pair(1), 1.0 / D, EPS, ALU.mult, ALU.add).then_inc(fms_ok, 1)
                dve.wait_ge(frt_ok, 1)
                await_step(note(nc.vector.reciprocal(rs[:], rs[:])))
                residual(note, await_step, acc, 3, y_ok)


def kernel(**inputs):
    from concourse import bacc
    from concourse.bass_utils import run_bass_kernel_spmd

    f32 = np.float32
    a = {k: np.asarray(v) for k, v in inputs.items()}
    laid = {}

    def rows_to_partitions(m):
        return np.ascontiguousarray(m.reshape(-1, P, m.shape[-1]).transpose(1, 0, 2))

    def columns(w):
        return np.ascontiguousarray(w.reshape(KD, P, -1, WC).transpose(2, 1, 0, 3))

    tokens = np.concatenate([a["x_prompt"][0], a["x_sample"][:, 0]])
    laid["xT"] = rows_to_partitions(tokens.T)
    laid["cT"] = rows_to_partitions(np.concatenate([a["c_prompt"], a["c_sample"]]).T)
    laid["w_ada"] = columns(a["w_ada"][0])
    laid["b_ada"] = np.ascontiguousarray(a["b_ada"][0].reshape(-1, P).T)
    laid["gains"] = np.ascontiguousarray(
        np.stack([a[n][0].reshape(KD, P) for n in ("g_pre1", "g_post1", "g_pre2", "g_post2")]).transpose(2, 0, 1))
    laid["w_in"] = columns(a["w_in"][0])
    laid["w_out"] = columns(a["w_out"][0])
    laid["w_q"] = columns(a["w_q"][0])
    laid["keysT"] = np.ascontiguousarray(a["sub_keys"][0].reshape(2 * PH, NK, P).transpose(2, 0, 1))
    laid["utab"] = np.ascontiguousarray(a["u_tab"][0].reshape(NK, NK, KD, P).transpose(1, 3, 2, 0))
    laid["vtab"] = np.ascontiguousarray(a["v_tab"][0].reshape(NK, NK, D))
    laid["s0"] = np.ascontiguousarray(a["state_ret"][0].transpose(2, 0, 1, 3))
    laid["conv_s"] = np.ascontiguousarray(a["cache_conv"][0].reshape(NS, CK - 1, RH, P).transpose(3, 2, 1, 0))
    laid["conv_w"] = np.ascontiguousarray(
        np.concatenate([a["conv_w"][0], a["conv_b"]]).reshape(CK + 1, RH, P).transpose(2, 1, 0))

    half = P // 2
    freqs = (f32(10000.0) ** (-np.arange(half, dtype=f32) / half)).astype(f32)
    where = np.concatenate([np.arange(SEQ), np.full(NS, PAST)]).astype(f32)
    angle = (freqs[:, None] * where[None, :]).astype(f32).astype(np.float64)
    cos = np.concatenate([np.cos(angle)] * 2)
    sin = np.concatenate([np.sin(angle), -np.sin(angle)])
    laid["trig"] = np.ascontiguousarray(
        np.stack([cos, sin, cos * P ** -0.5, sin * P ** -0.5]).transpose(1, 0, 2).astype(f32))
    gamma = 1.0 - 2.0 ** (-5.0 - np.arange(RH))
    rel = np.arange(SEQ)[None, :] - np.arange(P)[:, None]
    laid["decay"] = np.where(rel >= 0, gamma[:, None, None] ** np.maximum(rel, 0), 0.0).astype(f32)
    age = SEQ - 1 - np.arange(SEQ).reshape(CHUNKS, P)
    laid["kdecay"] = np.ascontiguousarray((gamma[:, None, None] ** age).transpose(2, 0, 1).astype(f32))
    width = [TOPK // (r + 1) for r in range(TOPK)]
    rows = np.zeros((P, P))
    rows[:, :TOPK] = np.cumsum([0] + width[:-1])
    rows[:, TOPK:TOPK + 8] = width[:8]
    laid["consts"] = np.ascontiguousarray(np.stack(
        [np.ones((P, P)), np.eye(P), np.tile(np.arange(P), (P, 1)), rows]).transpose(1, 0, 2).astype(f32))
    laid["starts"] = np.repeat(np.eye(P, dtype=f32)[:, P - NS:, None], P, 2)

    nc = bacc.Bacc("TRN2", target_bir_lowering=False, num_devices=1)
    args = {k: nc.dram_tensor(k, v.shape, F32, kind="ExternalInput").ap() for k, v in laid.items()}
    outs = {"yT": (P, KD, T), "ret_p": (P, RH, P), "conv_p": (P, RH, CK - 1), "ret_s": (P, NS, RH, P),
            "conv_so": (P, RH, CK - 1, NS)}
    args |= {k: nc.dram_tensor(k, v, F32, kind="ExternalOutput").ap() for k, v in outs.items()}
    args["gates_dram"] = nc.dram_tensor("gates_dram", (NGRP, P, NCH, GB, CH), F32, kind="Internal").ap()
    args["ahead_dram"] = nc.dram_tensor("ahead_dram", (AHEAD, P, T), F32, kind="Internal").ap()
    build(nc, **args)
    r = run_bass_kernel_spmd(nc, [laid], core_ids=[0]).results[0]

    y = r["yT"].transpose(2, 1, 0).reshape(T, D)
    return (y[None, :SEQ], y[SEQ:, None, :],
            r["ret_p"].transpose(1, 0, 2)[None, None],
            r["conv_p"].transpose(2, 1, 0).reshape(1, 1, CK - 1, RH * P),
            r["ret_s"].transpose(1, 2, 0, 3)[None],
            r["conv_so"].transpose(3, 2, 1, 0).reshape(1, NS, CK - 1, RH * P))
```
